# Optimizing a Trainium2 kernel written in Bass

```python
import jax
import jax.numpy as jnp
from jax import lax
import numpy as np
import math
import jax, jax.numpy as jnp

D_MODEL = 1024
BATCH = 1
SEQ = 256
DEPTH = 2

HEAD_DIM = 64
MIX_WIDTH = D_MODEL
GROUP_WIDTH = MIX_WIDTH // 2
N_HEADS = GROUP_WIDTH // HEAD_DIM
CONV_WIDTH = 31
MOBA_BLOCK = 256
MOBA_TOPK = 3
MOBA_Q_CHUNK = 32
NSA_KV_HEADS = 2
NSA_KV_WIDTH = NSA_KV_HEADS * HEAD_DIM
NSA_CMP_LEN = 32
NSA_CMP_STRIDE = 16
NSA_CMP_HIDDEN = 256
NSA_SEL_BLOCK = 64
NSA_TOPN = 16
NSA_WINDOW = 512
NSA_Q_CHUNK = 64
NSA_FORCE = 1e4
SWA_KV_HEADS = 2
SWA_KV_WIDTH = SWA_KV_HEADS * HEAD_DIM
SWA_WINDOW = 128
BAND_Q_BLOCK = 128
EPS = 1e-6
NEG = -1e30
TINY = 1e-30

EVEN_SIZES = (GROUP_WIDTH, GROUP_WIDTH, GROUP_WIDTH, GROUP_WIDTH, GROUP_WIDTH, GROUP_WIDTH, GROUP_WIDTH)
ODD_SIZES = (GROUP_WIDTH, NSA_KV_WIDTH, NSA_KV_WIDTH, NSA_KV_WIDTH, NSA_KV_WIDTH, NSA_KV_WIDTH,
             NSA_KV_WIDTH, 3 * N_HEADS, GROUP_WIDTH, GROUP_WIDTH, SWA_KV_WIDTH, SWA_KV_WIDTH, GROUP_WIDTH)
EVEN_IN = sum(EVEN_SIZES)
ODD_IN = sum(ODD_SIZES)


def _split(t, sizes):
    points = np.cumsum(sizes)[:-1].tolist()
    return jnp.split(t, points, axis=-1)

def _rmsnorm(x, g):
    xf = x.astype(jnp.float32)
    y = xf * lax.rsqrt(jnp.mean(xf * xf, axis=-1, keepdims=True) + EPS)
    return (y * g.astype(jnp.float32)).astype(x.dtype)

def _layernorm(x, g, b):
    xf = x.astype(jnp.float32)
    mu = jnp.mean(xf, axis=-1, keepdims=True)
    xc = xf - mu
    y = xc * lax.rsqrt(jnp.mean(xc * xc, axis=-1, keepdims=True) + EPS)
    return (y * g.astype(jnp.float32) + b.astype(jnp.float32)).astype(x.dtype)

def _split_heads(t, n):
    b, s, _ = t.shape
    return t.reshape(b, s, n, HEAD_DIM).transpose(0, 2, 1, 3)

def _merge_heads(t):
    b, n, s, d = t.shape
    return t.transpose(0, 2, 1, 3).reshape(b, s, n * d)

def _alibi_slopes(n):
    return jnp.asarray(np.power(2.0, -8.0 * np.arange(1, n + 1) / n).astype(np.float32))

def _masked_softmax(s, mask, sink=None):
    s = jnp.where(mask, s, NEG)
    m = jnp.max(s, axis=-1, keepdims=True)
    if sink is not None:
        m = jnp.maximum(m, sink)
    e = jnp.where(mask, jnp.exp(s - m), 0.0)
    den = jnp.sum(e, axis=-1, keepdims=True)
    if sink is not None:
        den = den + jnp.exp(sink - m)
    return e / jnp.maximum(den, TINY)

def _conformer_conv(u_val, u_gate, w_dw, b_dw, ln_g, ln_b):
    c = u_val.shape[-1]
    h = u_val * jax.nn.sigmoid(u_gate)
    h = jnp.pad(h, ((0, 0), (CONV_WIDTH - 1, 0), (0, 0)))
    y = lax.conv_general_dilated(h, w_dw[:, None, :].astype(h.dtype), (1,), 'VALID',
                                 dimension_numbers=('NWC', 'WIO', 'NWC'), feature_group_count=c)
    y = _layernorm(y + b_dw.astype(y.dtype), ln_g, ln_b)
    return jax.nn.silu(y)

def _moba_attention(q, k, v, slopes):
    b, h, s, d = q.shape
    nblk = -(-s // MOBA_BLOCK)
    sp = nblk * MOBA_BLOCK
    padw = ((0, 0), (0, 0), (0, sp - s), (0, 0))
    q, k, v = jnp.pad(q, padw), jnp.pad(k, padw), jnp.pad(v, padw)
    kb = k.reshape(b, h, nblk, MOBA_BLOCK, d)
    vb = v.reshape(b, h, nblk, MOBA_BLOCK, d)
    kmean = jnp.mean(kb.astype(jnp.float32), axis=3)
    n_sel = min(MOBA_TOPK, nblk)
    n_g = n_sel * MOBA_BLOCK
    scale = d ** -0.5
    bi = jnp.arange(b)[:, None, None, None]
    hi = jnp.arange(h)[None, :, None, None]
    offs = jnp.arange(MOBA_BLOCK)
    blk_ids = jnp.arange(nblk)
    sl = slopes[:, None, None]

    def chunk(c):
        t0 = c * MOBA_Q_CHUNK
        own = t0 // MOBA_BLOCK
        qc = lax.dynamic_slice_in_dim(q, t0, MOBA_Q_CHUNK, axis=2)
        tp = t0 + jnp.arange(MOBA_Q_CHUNK)
        gate = jnp.einsum('bhtd,bhnd->bhtn', qc.astype(jnp.float32), kmean)
        gate = jnp.where(blk_ids < own, gate, NEG)
        _, idx = lax.top_k(gate, n_sel)
        ks = kb[bi, hi, idx]
        vs = vb[bi, hi, idx]
        kpos = idx[..., None] * MOBA_BLOCK + offs
        dist = (tp[:, None, None] - kpos).astype(jnp.float32)
        s_sel = jnp.einsum('bhtd,bhtnld->bhtnl', qc, ks).astype(jnp.float32) * scale - sl[..., None] * dist
        m_sel = jnp.broadcast_to((idx < own)[..., None], s_sel.shape)
        k_own = lax.dynamic_index_in_dim(kb, own, axis=2, keepdims=False)
        v_own = lax.dynamic_index_in_dim(vb, own, axis=2, keepdims=False)
        kpos_own = own * MOBA_BLOCK + offs
        dist_own = (tp[:, None] - kpos_own[None, :]).astype(jnp.float32)
        s_own = jnp.einsum('bhtd,bhld->bhtl', qc, k_own).astype(jnp.float32) * scale - sl * dist_own
        m_own = jnp.broadcast_to(dist_own >= 0, s_own.shape)
        scores = jnp.concatenate([s_sel.reshape(b, h, MOBA_Q_CHUNK, n_g), s_own], axis=-1)
        mask = jnp.concatenate([m_sel.reshape(b, h, MOBA_Q_CHUNK, n_g), m_own], axis=-1)
        p = _masked_softmax(scores, mask).astype(v.dtype)
        out = jnp.einsum('bhtm,bhtmd->bhtd', p[..., :n_g], vs.reshape(b, h, MOBA_Q_CHUNK, n_g, d))
        return out + jnp.einsum('bhtl,bhld->bhtd', p[..., n_g:], v_own)

    outs = lax.map(chunk, jnp.arange(sp // MOBA_Q_CHUNK))
    outs = jnp.moveaxis(outs, 0, 2).reshape(b, h, sp, d)
    return outs[:, :, :s]

def _banded_attention(q, k, v, sl, window, sink=None):
    b, g, r, s, d = q.shape
    nq = s // BAND_Q_BLOCK
    span = window + BAND_Q_BLOCK
    padw = ((0, 0), (0, 0), (window, 0), (0, 0))
    kp, vp = jnp.pad(k, padw), jnp.pad(v, padw)
    kidx = jnp.arange(nq)[:, None] * BAND_Q_BLOCK + jnp.arange(span)[None, :]
    kband = kp[:, :, kidx]
    vband = vp[:, :, kidx]
    qb = q.reshape(b, g, r, nq, BAND_Q_BLOCK, d)
    tpos = jnp.arange(s).reshape(nq, BAND_Q_BLOCK)
    kpos = kidx - window
    dist = tpos[:, :, None] - kpos[:, None, :]
    mask = (dist >= 0) & (dist < window) & (kpos[:, None, :] >= 0)
    scores = (jnp.einsum('bgrnqd,bgnkd->bgrnqk', qb, kband).astype(jnp.float32) * d ** -0.5
              - sl[:, :, None, None, None] * dist.astype(jnp.float32))
    sk = None if sink is None else sink.astype(jnp.float32)[:, :, None, None, None]
    p = _masked_softmax(scores, mask, sk)
    out = jnp.einsum('bgrnqk,bgnkd->bgrnqd', p.astype(v.dtype), vband)
    return out.reshape(b, g, r, s, d)

def _compress(x, pos, w1, b1, w2, b2):
    s = x.shape[2]
    n_cmp = (s - NSA_CMP_LEN) // NSA_CMP_STRIDE + 1
    idx = jnp.arange(n_cmp)[:, None] * NSA_CMP_STRIDE + jnp.arange(NSA_CMP_LEN)[None, :]
    blocks = x[:, :, idx] + pos.astype(x.dtype)
    flat = blocks.reshape(blocks.shape[0], blocks.shape[1], n_cmp, NSA_CMP_LEN * x.shape[-1])
    hid = jax.nn.silu(flat @ w1 + b1)
    return hid @ w2 + b2

def _overlap_matrix(n_cmp, nsb):
    start = np.arange(n_cmp)[:, None] * NSA_CMP_STRIDE
    bs = np.arange(nsb)[None, :] * NSA_SEL_BLOCK
    return jnp.asarray(((start < bs + NSA_SEL_BLOCK) & (start + NSA_CMP_LEN > bs)).astype(np.float32))

def _nsa_attention(q, k_cmp, v_cmp, k_slc, v_slc, k_win, v_win, gates, kn_cmp,
                   pos_k, pos_v, kw1, kb1, kw2, kb2, vw1, vb1, vw2, vb2, slopes):
    b, h, s, d = q.shape
    g = k_slc.shape[1]
    r = h // g
    scale = d ** -0.5
    qg = q.reshape(b, g, r, s, d)
    sl = slopes.reshape(g, r)
    tpos = jnp.arange(s)
    kc = _rmsnorm(_compress(k_cmp, pos_k, kw1, kb1, kw2, kb2), kn_cmp)
    vc = _compress(v_cmp, pos_v, vw1, vb1, vw2, vb2)
    n_cmp = kc.shape[2]
    cend = jnp.arange(n_cmp) * NSA_CMP_STRIDE + NSA_CMP_LEN - 1
    dist_c = tpos[:, None] - cend[None, :]
    s_c = (jnp.einsum('bgrtd,bgcd->bgrtc', qg, kc).astype(jnp.float32) * scale
           - sl[:, :, None, None] * dist_c.astype(jnp.float32))
    p_c = _masked_softmax(s_c, dist_c >= 0)
    o_cmp = jnp.einsum('bgrtc,bgcd->bgrtd', p_c.astype(vc.dtype), vc)
    nsb = s // NSA_SEL_BLOCK
    imp = jnp.einsum('bgrtc,cn->bgtn', p_c, _overlap_matrix(n_cmp, nsb))
    blk = jnp.arange(nsb)[None, :]
    cur = (tpos // NSA_SEL_BLOCK)[:, None]
    forced = (blk == 0) | (blk == cur) | (blk == cur - 1)
    imp = jnp.where(forced, NSA_FORCE, imp)
    imp = jnp.where(blk <= cur, imp, NEG)
    n_top = min(NSA_TOPN, nsb)
    _, sel = lax.top_k(imp, n_top)
    kbk = k_slc.reshape(b, g, nsb, NSA_SEL_BLOCK, d)
    vbk = v_slc.reshape(b, g, nsb, NSA_SEL_BLOCK, d)
    bi = jnp.arange(b)[:, None, None, None]
    gi = jnp.arange(g)[None, :, None, None]
    offs = jnp.arange(NSA_SEL_BLOCK)
    n_g = n_top * NSA_SEL_BLOCK

    def chunk(c):
        t0 = c * NSA_Q_CHUNK
        qc = lax.dynamic_slice_in_dim(qg, t0, NSA_Q_CHUNK, axis=3)
        idx = lax.dynamic_slice_in_dim(sel, t0, NSA_Q_CHUNK, axis=2)
        tp = t0 + jnp.arange(NSA_Q_CHUNK)
        ks = kbk[bi, gi, idx]
        vs = vbk[bi, gi, idx]
        kpos = idx[..., None] * NSA_SEL_BLOCK + offs
        dist = (tp[:, None, None] - kpos).astype(jnp.float32)
        sc = (jnp.einsum('bgrtd,bgtnld->bgrtnl', qc, ks).astype(jnp.float32) * scale
              - sl[:, :, None, None, None] * dist[:, :, None])
        mask = jnp.broadcast_to((dist >= 0)[:, :, None], sc.shape)
        p = _masked_softmax(sc.reshape(b, g, r, NSA_Q_CHUNK, n_g), mask.reshape(b, g, r, NSA_Q_CHUNK, n_g))
        return jnp.einsum('bgrtm,bgtmd->bgrtd', p.astype(vs.dtype), vs.reshape(b, g, NSA_Q_CHUNK, n_g, d))

    o_slc = lax.map(chunk, jnp.arange(s // NSA_Q_CHUNK))
    o_slc = jnp.moveaxis(o_slc, 0, 3).reshape(b, g, r, s, d)
    o_win = _banded_attention(qg, k_win, v_win, sl, NSA_WINDOW)
    gt = [jnp.transpose(gates[:, :, i], (0, 2, 1)).reshape(b, g, r, s, 1) for i in range(3)]
    o = gt[0] * o_cmp + gt[1] * o_slc + gt[2] * o_win
    return o.astype(q.dtype).reshape(b, h, s, d)

def first_inputs(seed: int = 0) -> dict:
    key = jax.random.key(seed)
    keys = iter(jax.random.split(key, 40))
    ne = (DEPTH + 1) // 2
    no = DEPTH // 2

    def nrm(shape, scale):
        return jax.random.normal(next(keys), shape, jnp.float32) * scale

    def gain(shape):
        return 1.0 + nrm(shape, 0.02)

    hd = HEAD_DIM
    flat = NSA_CMP_LEN * hd
    return {
        'x': nrm((BATCH, SEQ, D_MODEL), 1.0),
        'norm_g': gain((DEPTH, D_MODEL)),
        'w_out': nrm((DEPTH, MIX_WIDTH, D_MODEL), MIX_WIDTH ** -0.5),
        'e_w_in': nrm((ne, D_MODEL, EVEN_IN), D_MODEL ** -0.5),
        'a_conv_w': nrm((ne, CONV_WIDTH, GROUP_WIDTH), CONV_WIDTH ** -0.5),
        'a_conv_b': nrm((ne, GROUP_WIDTH), 0.02),
        'a_ln_g': gain((ne, GROUP_WIDTH)),
        'a_ln_b': nrm((ne, GROUP_WIDTH), 0.02),
        'b_qnorm_g': gain((ne, hd)),
        'b_knorm_g': gain((ne, hd)),
        'o_w_in': nrm((no, D_MODEL, ODD_IN), D_MODEL ** -0.5),
        'c_qnorm_g': gain((no, hd)),
        'c_knorm_cmp_g': gain((no, hd)),
        'c_knorm_slc_g': gain((no, hd)),
        'c_knorm_win_g': gain((no, hd)),
        'c_pos_k': nrm((no, NSA_CMP_LEN, hd), 0.02),
        'c_pos_v': nrm((no, NSA_CMP_LEN, hd), 0.02),
        'c_k_w1': nrm((no, flat, NSA_CMP_HIDDEN), flat ** -0.5),
        'c_k_b1': nrm((no, NSA_CMP_HIDDEN), 0.02),
        'c_k_w2': nrm((no, NSA_CMP_HIDDEN, hd), NSA_CMP_HIDDEN ** -0.5),
        'c_k_b2': nrm((no, hd), 0.02),
        'c_v_w1': nrm((no, flat, NSA_CMP_HIDDEN), flat ** -0.5),
        'c_v_b1': nrm((no, NSA_CMP_HIDDEN), 0.02),
        'c_v_w2': nrm((no, NSA_CMP_HIDDEN, hd), NSA_CMP_HIDDEN ** -0.5),
        'c_v_b2': nrm((no, hd), 0.02),
        'd_qnorm_g': gain((no, hd)),
        'd_knorm_g': gain((no, hd)),
        'd_sinks': nrm((no, N_HEADS), 0.5),
    }

def first_block(x, norm_g, w_out, e_w_in, a_conv_w, a_conv_b, a_ln_g, a_ln_b, b_qnorm_g, b_knorm_g,
              o_w_in, c_qnorm_g, c_knorm_cmp_g, c_knorm_slc_g, c_knorm_win_g, c_pos_k, c_pos_v,
              c_k_w1, c_k_b1, c_k_w2, c_k_b2, c_v_w1, c_v_b1, c_v_w2, c_v_b2,
              d_qnorm_g, d_knorm_g, d_sinks):
    slopes = _alibi_slopes(N_HEADS)
    bsz, slen, _ = x.shape
    for layer in range(DEPTH):
        h = _rmsnorm(x, norm_g[layer])
        if layer % 2 == 0:
            i = layer // 2
            proj = jnp.einsum('bsd,de->bse', h, e_w_in[i])
            u_val, u_gate, z_a, q_b, k_b, v_b, z_b = _split(proj, EVEN_SIZES)
            y_a = _conformer_conv(u_val, u_gate, a_conv_w[i], a_conv_b[i], a_ln_g[i], a_ln_b[i]) * jax.nn.silu(z_a)
            q = _rmsnorm(_split_heads(q_b, N_HEADS), b_qnorm_g[i])
            k = _rmsnorm(_split_heads(k_b, N_HEADS), b_knorm_g[i])
            v = _split_heads(v_b, N_HEADS)
            y_b = _merge_heads(_moba_attention(q, k, v, slopes)) * jax.nn.silu(z_b)
            y = jnp.concatenate([y_a, y_b], axis=-1)
        else:
            i = layer // 2
            proj = jnp.einsum('bsd,de->bse', h, o_w_in[i])
            (q_c, kc_, vc_, ks_, vs_, kw_, vw_, g_c, z_c, q_d, k_d, v_d, z_d) = _split(proj, ODD_SIZES)
            qc = _rmsnorm(_split_heads(q_c, N_HEADS), c_qnorm_g[i])
            gates = jax.nn.sigmoid(g_c.astype(jnp.float32)).reshape(bsz, slen, 3, N_HEADS)
            o_c = _nsa_attention(
                qc, _split_heads(kc_, NSA_KV_HEADS), _split_heads(vc_, NSA_KV_HEADS),
                _rmsnorm(_split_heads(ks_, NSA_KV_HEADS), c_knorm_slc_g[i]), _split_heads(vs_, NSA_KV_HEADS),
                _rmsnorm(_split_heads(kw_, NSA_KV_HEADS), c_knorm_win_g[i]), _split_heads(vw_, NSA_KV_HEADS),
                gates, c_knorm_cmp_g[i], c_pos_k[i], c_pos_v[i],
                c_k_w1[i], c_k_b1[i], c_k_w2[i], c_k_b2[i], c_v_w1[i], c_v_b1[i], c_v_w2[i], c_v_b2[i], slopes)
            y_c = _merge_heads(o_c) * jax.nn.silu(z_c)
            r = N_HEADS // SWA_KV_HEADS
            qd = _rmsnorm(_split_heads(q_d, N_HEADS), d_qnorm_g[i]).reshape(bsz, SWA_KV_HEADS, r, slen, HEAD_DIM)
            kd = _rmsnorm(_split_heads(k_d, SWA_KV_HEADS), d_knorm_g[i])
            vd = _split_heads(v_d, SWA_KV_HEADS)
            o_d = _banded_attention(qd, kd, vd, slopes.reshape(SWA_KV_HEADS, r), SWA_WINDOW,
                                    d_sinks[i].reshape(SWA_KV_HEADS, r))
            y_d = _merge_heads(o_d.reshape(bsz, N_HEADS, slen, HEAD_DIM)) * jax.nn.silu(z_d)
            y = jnp.concatenate([y_c, y_d], axis=-1)
        x = x + jnp.einsum('bse,ed->bsd', y, w_out[layer]).astype(x.dtype)
    return x


DEPTH_2 = 1

RET_HEADS = 4
RET_DK = 256
RET_DV = 512
RET_CHUNK = 128
RET_QK_W = RET_HEADS * RET_DK
RET_V_W = RET_HEADS * RET_DV
ATT_GROUPS = ((128, 1), (512, 4), (2048, 16))
N_ATT_GROUPS = len(ATT_GROUPS)
ATT_HEADS_PER_GROUP = 4
ATT_HEAD_DIM = 128
ATT_GROUP_W = ATT_HEADS_PER_GROUP * ATT_HEAD_DIM
N_ATT_HEADS = N_ATT_GROUPS * ATT_HEADS_PER_GROUP
REL_BUCKETS = 32
REL_MAX_DIST = 2048
D_FF = 4 * D_MODEL
N_BRANCHES = 2
RMS_EPS = 1e-6
GN_EPS = 1e-5
ROPE_BASE = 10000.0

IN_SIZES = ([RET_QK_W, RET_QK_W, RET_V_W, RET_V_W]
            + [ATT_GROUP_W] * (3 * N_ATT_GROUPS)
            + [D_MODEL] * N_BRANCHES)
IN_COLS = sum(IN_SIZES)
IN_OFFSETS = [sum(IN_SIZES[:i + 1]) for i in range(len(IN_SIZES) - 1)]


def rms_norm(x, g):
    xf = x.astype(jnp.float32)
    y = xf * lax.rsqrt(jnp.mean(xf * xf, axis=-1, keepdims=True) + RMS_EPS)
    return (y * g.astype(jnp.float32)).astype(x.dtype)

def modulate(h, shift, scale):
    return h * (1 + scale[:, None, :]) + shift[:, None, :]

def t5_bucket(dist):
    max_exact = REL_BUCKETS // 2
    d_f = jnp.maximum(dist, 1).astype(jnp.float32)
    large = max_exact + (jnp.log(d_f / max_exact) / math.log(REL_MAX_DIST / max_exact)
                         * (REL_BUCKETS - max_exact)).astype(jnp.int32)
    large = jnp.minimum(large, REL_BUCKETS - 1)
    return jnp.where(dist < max_exact, dist, large)

def rotary(x, pos):
    half = x.shape[-1] // 2
    inv = ROPE_BASE ** (-jnp.arange(half, dtype=jnp.float32) / half)
    ang = pos.astype(jnp.float32)[:, None] * inv[None, :]
    cos, sin = jnp.cos(ang).astype(x.dtype), jnp.sin(ang).astype(x.dtype)
    x1, x2 = x[..., :half], x[..., half:]
    return jnp.concatenate([x1 * cos - x2 * sin, x1 * sin + x2 * cos], axis=-1)

def retention(q, k, v):
    B, H, S, dk = q.shape
    dv = v.shape[-1]
    C = RET_CHUNK
    nc = S // C
    log_g = jnp.log1p(-(2.0 ** (-5.0 - jnp.arange(H, dtype=jnp.float32))))
    idx = jnp.arange(C, dtype=jnp.float32)
    rel = idx[:, None] - idx[None, :]
    inner_decay = jnp.where(rel >= 0, jnp.exp(log_g[:, None, None] * jnp.maximum(rel, 0.0)), 0.0)
    q_decay = jnp.exp(log_g[:, None] * (idx + 1.0))
    k_decay = jnp.exp(log_g[:, None] * (C - 1.0 - idx))
    chunk_decay = jnp.exp(log_g * C)

    def to_chunks(t):
        return jnp.moveaxis(t.astype(jnp.float32).reshape(B, H, nc, C, t.shape[-1]), 2, 0)

    qc, kc, vc = to_chunks(q), to_chunks(k), to_chunks(v)

    def step(state, inp):
        qi, ki, vi = inp
        s = jnp.einsum('bhid,bhjd->bhij', qi, ki) * inner_decay[None]
        o = (jnp.einsum('bhij,bhje->bhie', s, vi)
             + jnp.einsum('bhid,bhde->bhie', qi, state) * q_decay[None, :, :, None])
        state = (state * chunk_decay[None, :, None, None]
                 + jnp.einsum('bhjd,bhje->bhde', ki * k_decay[None, :, :, None], vi))
        return state, o

    state0 = jnp.zeros((B, H, dk, dv), jnp.float32)
    _, o = lax.scan(step, state0, (qc, kc, vc))
    return jnp.moveaxis(o, 0, 2).reshape(B, H, S, dv)

def dilated_group(q, k, v, bias_tab, window, dilation):
    B, H, S, dh = q.shape
    w = window // dilation
    blk = w
    span = dilation * blk
    Sp = -(-S // span) * span
    L = Sp // dilation
    nb = L // blk

    def split(t):
        t = jnp.pad(t, ((0, 0), (0, 0), (0, Sp - S), (0, 0)))
        t = t.reshape(B, H, L, dilation, dh).transpose(0, 1, 3, 2, 4)
        return t.reshape(B, H, dilation, nb, blk, dh)

    qs, ks, vs = split(q), split(k), split(v)

    def with_prev(t):
        prev = jnp.pad(t[:, :, :, :-1], ((0, 0), (0, 0), (0, 0), (1, 0), (0, 0), (0, 0)))
        return jnp.concatenate([prev, t], axis=4)

    kb, vb = with_prev(ks), with_prev(vs)
    qi = jnp.arange(blk)[:, None]
    kj = jnp.arange(2 * blk)[None, :]
    m = blk + qi - kj
    band = (m >= 0) & (m <= w)
    first_ok = kj >= blk
    valid = band[None] & ((jnp.arange(nb)[:, None, None] > 0) | first_ok[None])
    bias = bias_tab[t5_bucket(jnp.clip(m, 0, w) * dilation)]
    bias = jnp.moveaxis(bias, -1, 0).astype(jnp.float32)

    s = (jnp.einsum('bhrnid,bhrnjd->bhrnij', qs, kb).astype(jnp.float32) * (dh ** -0.5)
         + bias[None, :, None, None])
    s = jnp.where(valid[None, None, None], s, -1e30)
    mx = jnp.max(s, axis=-1, keepdims=True)
    e = jnp.exp(s - mx)
    den = jnp.sum(e, axis=-1, keepdims=True)
    p = (e / den).astype(v.dtype)
    lse = (mx + jnp.log(den))[..., 0]
    o = jnp.einsum('bhrnij,bhrnjd->bhrnid', p, vb)

    def merge(t):
        t = t.reshape(B, H, dilation, L, *t.shape[5:])
        t = jnp.swapaxes(t, 2, 3)
        t = t.reshape(B, H, Sp, *t.shape[4:])
        return t[:, :, :S]

    return merge(o), merge(lse)

def token_mixer(h, w_in, rel_bias, gn_g, gn_b, w_ret_out, w_att_out, w_o):
    B, S, _ = h.shape
    proj = h @ w_in
    parts = jnp.split(proj, IN_OFFSETS, axis=-1)

    def heads(t, n):
        return t.reshape(B, S, n, -1).transpose(0, 2, 1, 3)

    pos = jnp.arange(S)
    rq, rk, rv, rg = parts[0], parts[1], parts[2], parts[3]
    rq = rotary(heads(rq, RET_HEADS), pos)
    rk = rotary(heads(rk, RET_HEADS), pos) * (RET_DK ** -0.5)
    ro = retention(rq, rk, heads(rv, RET_HEADS))
    mu = jnp.mean(ro, axis=-1, keepdims=True)
    var = jnp.mean(jnp.square(ro - mu), axis=-1, keepdims=True)
    ro = ((ro - mu) * lax.rsqrt(var + GN_EPS)).transpose(0, 2, 1, 3).reshape(B, S, RET_V_W)
    ro = (ro * gn_g.astype(jnp.float32) + gn_b.astype(jnp.float32)).astype(h.dtype)
    ret_out = (jax.nn.silu(rg) * ro) @ w_ret_out

    outs, lses = [], []
    for gi, (win, dil) in enumerate(ATT_GROUPS):
        aq, ak, av = parts[4 + 3 * gi], parts[5 + 3 * gi], parts[6 + 3 * gi]
        tab = rel_bias[:, gi * ATT_HEADS_PER_GROUP:(gi + 1) * ATT_HEADS_PER_GROUP]
        o, lse = dilated_group(heads(aq, ATT_HEADS_PER_GROUP), heads(ak, ATT_HEADS_PER_GROUP),
                               heads(av, ATT_HEADS_PER_GROUP), tab, win, dil)
        outs.append(o)
        lses.append(lse)
    o_all = jnp.stack(outs, axis=0)
    wts = jax.nn.softmax(jnp.stack(lses, axis=0), axis=0)
    att = jnp.einsum('gbhs,gbhsd->bshd', wts.astype(o_all.dtype), o_all).reshape(B, S, ATT_GROUP_W)
    att_out = att @ w_att_out

    gate_a, gate_b = parts[-2], parts[-1]
    merged = jax.nn.sigmoid(gate_a) * ret_out + jax.nn.sigmoid(gate_b) * att_out
    return merged @ w_o

def squared_relu_mlp(h, w1, w2):
    return jnp.square(jax.nn.relu(h @ w1)) @ w2

def second_inputs(seed: int = 0) -> dict:
    key = jax.random.key(seed)
    ks = jax.random.split(key, 18)
    nrm = jax.random.normal
    f32 = jnp.float32
    return {
        "x": nrm(ks[0], (BATCH, SEQ, D_MODEL), f32),
        "c": nrm(ks[1], (BATCH, D_MODEL), f32),
        "w_ada": nrm(ks[2], (DEPTH_2, D_MODEL, 6 * D_MODEL), f32) * D_MODEL ** -0.5,
        "b_ada": nrm(ks[3], (DEPTH_2, 6 * D_MODEL), f32) * 0.02,
        "norm1_g": 1.0 + 0.02 * nrm(ks[4], (DEPTH_2, D_MODEL), f32),
        "w_in": nrm(ks[5], (DEPTH_2, D_MODEL, IN_COLS), f32) * D_MODEL ** -0.5,
        "rel_bias": nrm(ks[6], (REL_BUCKETS, N_ATT_HEADS), f32) * 0.5,
        "ret_gn_g": 1.0 + 0.02 * nrm(ks[7], (DEPTH_2, RET_V_W), f32),
        "ret_gn_b": 0.02 * nrm(ks[8], (DEPTH_2, RET_V_W), f32),
        "w_ret_out": nrm(ks[9], (DEPTH_2, RET_V_W, D_MODEL), f32) * RET_V_W ** -0.5,
        "w_att_out": nrm(ks[10], (DEPTH_2, ATT_GROUP_W, D_MODEL), f32) * ATT_GROUP_W ** -0.5,
        "w_o": nrm(ks[11], (DEPTH_2, D_MODEL, D_MODEL), f32) * D_MODEL ** -0.5,
        "norm2_g": 1.0 + 0.02 * nrm(ks[12], (DEPTH_2, D_MODEL), f32),
        "w_ff1": nrm(ks[13], (DEPTH_2, D_MODEL, D_FF), f32) * D_MODEL ** -0.5,
        "w_ff2": nrm(ks[14], (DEPTH_2, D_FF, D_MODEL), f32) * D_FF ** -0.5,
        "norm_f_g": 1.0 + 0.02 * nrm(ks[15], (D_MODEL,), f32),
    }

def second_block(x, c, w_ada, b_ada, norm1_g, w_in, rel_bias, ret_gn_g, ret_gn_b,
              w_ret_out, w_att_out, w_o, norm2_g, w_ff1, w_ff2, norm_f_g):
    for l in range(DEPTH_2):
        mod = jax.nn.silu(c) @ w_ada[l] + b_ada[l]
        sh1, sc1, g1, sh2, sc2, g2 = jnp.split(mod, 6, axis=-1)
        h = modulate(rms_norm(x, norm1_g[l]), sh1, sc1)
        x = x + g1[:, None, :] * token_mixer(h, w_in[l], rel_bias, ret_gn_g[l], ret_gn_b[l],
                                             w_ret_out[l], w_att_out[l], w_o[l])
        h = modulate(rms_norm(x, norm2_g[l]), sh2, sc2)
        x = x + g2[:, None, :] * squared_relu_mlp(h, w_ff1[l], w_ff2[l])
    return rms_norm(x, norm_f_g)


def setup_inputs(seed=0):
    out = dict(first_inputs(seed))
    for name, value in second_inputs(seed + 1).items():
        if name != "x":
            out[name + "_2"] = value
    return out


def reference(
    x, norm_g, w_out, e_w_in, a_conv_w, a_conv_b, a_ln_g, a_ln_b, b_qnorm_g, b_knorm_g, o_w_in,
    c_qnorm_g, c_knorm_cmp_g, c_knorm_slc_g, c_knorm_win_g, c_pos_k, c_pos_v, c_k_w1, c_k_b1,
    c_k_w2, c_k_b2, c_v_w1, c_v_b1, c_v_w2, c_v_b2, d_qnorm_g, d_knorm_g, d_sinks, c_2, w_ada_2,
    b_ada_2, norm1_g_2, w_in_2, rel_bias_2, ret_gn_g_2, ret_gn_b_2, w_ret_out_2, w_att_out_2,
    w_o_2, norm2_g_2, w_ff1_2, w_ff2_2, norm_f_g_2,
):
    x = first_block(
        x, norm_g, w_out, e_w_in, a_conv_w, a_conv_b, a_ln_g, a_ln_b, b_qnorm_g, b_knorm_g,
        o_w_in, c_qnorm_g, c_knorm_cmp_g, c_knorm_slc_g, c_knorm_win_g, c_pos_k, c_pos_v,
        c_k_w1, c_k_b1, c_k_w2, c_k_b2, c_v_w1, c_v_b1, c_v_w2, c_v_b2, d_qnorm_g, d_knorm_g,
        d_sinks,
    )
    return second_block(
        x, c_2, w_ada_2, b_ada_2, norm1_g_2, w_in_2, rel_bias_2, ret_gn_g_2, ret_gn_b_2,
        w_ret_out_2, w_att_out_2, w_o_2, norm2_g_2, w_ff1_2, w_ff2_2, norm_f_g_2,
    )


_drawn_inputs = setup_inputs


def setup_inputs(seed=0):
    import zlib

    import numpy as np

    out = dict(_drawn_inputs(seed))
    spreads = {}
    factors = {'norm_g': 4.363,
     'a_conv_b': 3.586,
     'a_ln_g': 8.0,
     'a_ln_b': 8.0,
     'b_qnorm_g': 8.0,
     'b_knorm_g': 8.0,
     'c_qnorm_g': 8.0,
     'c_knorm_cmp_g': 8.0,
     'c_knorm_slc_g': 8.0,
     'c_knorm_win_g': 8.0,
     'c_pos_k': 8.0,
     'c_pos_v': 35.793,
     'c_k_b1': 8.0,
     'c_k_b2': 37.169,
     'c_v_b1': 35.309,
     'c_v_b2': 22.521,
     'd_qnorm_g': 8.0,
     'd_knorm_g': 8.0,
     'd_sinks': 41.216,
     'norm1_g_2': 5.464,
     'ret_gn_g_2': 37.312,
     'ret_gn_b_2': 36.731,
     'norm2_g_2': 17.156,
     'norm_f_g_2': 24.008,
     'rel_bias_2': 27.355}
    for name, (base, spread) in spreads.items():
        noise = np.random.default_rng([zlib.crc32(name.encode()), seed]).standard_normal(out[name].shape)
        drawn = base * np.exp(spread * noise) if base else spread * noise
        out[name] = jnp.asarray(drawn.astype(out[name].dtype))
    for name, factor in factors.items():
        out[name] = (out[name] * factor).astype(out[name].dtype)
    return out
```

```python
import numpy as np
import concourse.bass as bass
from concourse import mybir
from contextlib import ExitStack

F32 = mybir.dt.float32
ALU = mybir.AluOpType
ACT = mybir.ActivationFunctionType
AX = mybir.AxisListType

P = 128
S = 256
TT = S // P
D = 1024
KD = D // P
GW = 512
HD = 64
NH = 8
TAPS = 31
NCMP = 15
RH, RDK, RDV = 4, 256, 512
AG, AH = 3, 4
DFF = 4 * D
EPS = 1e-6
GN_EPS = 1e-5
LINE = 384
NSLOT = 3
SLOT = 4096
NPP = 3
PADW = S + TAPS - 1

EV = dict(uv=0, ug=512, za=1024, bq=1536, bk=2048, bv=2560, zb=3072)
OD = dict(qc=0, kc=512, kw=1024, zc=1304, qd=1816, kd=2328, zd=2584)
IN2_Q, IN2_K, IN2_V, IN2_G, IN2_ATT, IN2_GATE = 0, 1024, 2048, 4096, 6144, 10752


def slab_plan():
    out = [(n, 8, 512) for n in ("uv", "ug", "bq", "bk", "bv", "zb", "za", "wo0a", "wo0b")]
    out += [("kc", 8, 512), ("qc", 8, 512), ("kw", 8, 280), ("ck", 16, 256), ("cv", 16, 256), ("qd", 8, 512),
            ("kd", 8, 256), ("zc", 8, 512), ("zd", 8, 512), ("wo1a", 8, 512), ("wo1b", 8, 512)]
    out += [(f"{n}{i}", 8, 512) for n, c in (("rq", 2), ("rk", 2), ("rv", 4)) for i in range(c)]
    out += [(f"a{n}{g}", 8, 512) for g in range(AG) for n in "qk"] + [(f"av{g}", 8, 512) for g in range(AG)]
    out += [(f"{n}{i}", 8, 512) for n, c in (("rg", 4), ("ga", 2), ("gb", 2)) for i in range(c)]
    out += [(f"wr{i}", 16, 256) for i in range(4)] + [("wa", 4, 1024), ("wo2a", 8, 512), ("wo2b", 8, 512)]
    out += [(f"f1_{i}", 8, 512) for i in range(8)] + [(f"f2_{i}", 32, 128) for i in range(8)]
    return out


SLABS = slab_plan()
SLAB_AT = {n: i for i, (n, _, _) in enumerate(SLABS)}


PAIRED = ("qc", "qd", "zc", "zd")


def slab_pieces(name):
    return 4 if name.startswith("wo1") else NH if name in PAIRED else 1


def slab_last_group(name):
    named = dict(uv="uv1", ug="ug1", bq="bq1", bk="bk1", bv="bv1", zb="zb1", za="za1", wo0a="wo0_1", wo0b="wo0_3",
                 kc="vs", qc="qc1", kw="vw", ck="hidk", cv="hidv", qd="qd1", kd="vd", zc="zc1", zd="zd1",
                 wo1a="wo1_1", wo1b="wo1_3", wa="wa3", wo2a="wo2_1", wo2b="wo2_3")
    if name in named:
        return GROUP_AT[named[name]]
    stem, i = name[:-1], int(name[-1])
    if stem == "rv":
        return GROUP_AT[f"rv{i}_1"]
    if stem in ("aq", "ak", "av"):
        return GROUP_AT[f"{name}_1"]
    if stem == "f1_":
        return GROUP_AT[f"f1_{2 * i + 1}"]
    return GROUP_AT[f"{stem}{i if stem in ('wr', 'f2_') else 2 * i + 1}"]


def slab_target(n):
    return 16 * sum(slab_pieces(SLABS[i][0]) for i in range(n % NSLOT, n + 1, NSLOT))


RET_FILL = [f"a{n}{g}_{i}" for g in range(AG) for n in "qk" for i in range(2)] + \
    [f"av{g}_{i}" for g in range(AG) for i in range(2)]


def group_plan():
    out = ["vec", "dl0", "dl1", "dl2", "x0", "x1", "x2", "x3"]
    out += ["uv0", "uv1", "ug0", "ug1", "bq0", "bq1", "bk0", "bk1", "bv0", "bv1", "zb0", "zb1", "za0", "za1"]
    out += [f"wo0_{i}" for i in range(4)]
    out += ["kcvc", "ks", "vs", "qc0", "qc1", "kw", "vw", "hidk", "hidv", "kc2", "vc2",
            "qd0", "qd1", "kd", "vd", "zc0", "zc1", "zd0", "zd1", "mod"]
    out += [f"wo1_{i}" for i in range(4)]
    out += [f"rq{i}" for i in range(4)] + [f"rk{i}" for i in range(4)]
    out += [f"rv{s}_{t}" for s in range(4) for t in range(2)]
    for h in range(RH):
        out += RET_FILL[4 * h:4 * h + 4] + [f"rt{h}_0", f"rt{h}_1"]
    out += RET_FILL[16:]
    out += [f"rg{i}" for i in range(8)] + [f"ga{i}" for i in range(4)] + [f"gb{i}" for i in range(4)]
    out += [f"wr{i}" for i in range(4)] + [f"wa{i}" for i in range(4)] + [f"wo2_{i}" for i in range(4)]
    out += [f"f1_{i}" for i in range(16)] + [f"f2_{i}" for i in range(8)] + [f"out{i}" for i in range(4)]
    return out


GROUPS = group_plan()
GROUP_AT = {n: i for i, n in enumerate(GROUPS)}

ROWS_A, ROWS_B = {}, {}
_n = 0
for _name, _c in (("norm_g", 16), ("a_conv_b", 4), ("a_ln_g", 4), ("a_ln_b", 4), ("norm1_g_2", 8), ("norm2_g_2", 8),
                  ("norm_f_g_2", 8), ("c_k_b1", 2), ("c_v_b1", 2), ("c_2", 8), ("c_pos_k", 16), ("c_pos_v", 16),
                  ("b_qnorm_g", 1), ("b_knorm_g", 1), ("c_qnorm_g", 1), ("c_knorm_cmp_g", 1), ("c_knorm_slc_g", 1),
                  ("c_knorm_win_g", 1), ("d_qnorm_g", 1), ("d_knorm_g", 1), ("c_k_b2", 1)):
    ROWS_A[_name] = (_n, _c)
    _n += _c
N_ROWS_A = _n
_n = 0
for _name, _c in (("ret_gn_g_2", 16), ("ret_gn_b_2", 16), ("b_ada_2", 48)):
    ROWS_B[_name] = (_n, _c)
    _n += _c
N_ROWS_B = _n
HALF_ROWS = ("b_qnorm_g", "b_knorm_g", "c_qnorm_g", "c_knorm_cmp_g", "c_knorm_slc_g", "c_knorm_win_g",
             "d_qnorm_g", "d_knorm_g", "c_k_b2")


def attention_units():
    out, step = [], 0
    for bp in range(2):
        for qt in range(2):
            out.append(("b", step, 0, True, bp, qt, P * (qt + 1)))
            step += 1
    for bp in range(2):
        for qt in range(2):
            for br in range(3):
                out.append(("c", step, br, br == 2, bp, qt, NCMP if br == 0 else P * (qt + 1)))
            step += 1
    for bp in range(2):
        for qt in range(2):
            out.append(("d", step, 0, True, bp, qt, P * (qt + 1)))
            step += 1
    for hh in range(AH):
        for qt in range(2):
            out.append(("a", step, 0, True, hh, qt, P * (qt + 1)))
            step += 1
    return out


UNITS = attention_units()


def key_tiles(u):
    return -(-UNITS[u][6] // P)


def rounds_before(u):
    return sum(key_tiles(i) for i in range(u))


PART = {p: [u for u in range(len(UNITS)) if UNITS[u][0] == p] for p in "bcda"}

NORMS = ["x0", "bq0", "bq1", "bk0", "bk1", "x1", "ks", "qc0", "qc1", "kw", "cmp", "qd0", "qd1", "kd", "x2", "x3", "xf"]
NORM_AT = {n: i for i, n in enumerate(NORMS)}


SILU = ["ug0", "ug1", "zb0", "zb1", "za0", "za1", "zc0", "zc1", "zd0", "zd1"] + [f"rg{i}" for i in range(8)] + \
    [f"ga{i}" for i in range(4)] + [f"gb{i}" for i in range(4)]
FILL_B = [["zb0"], ["zb1"], ["za0"], ["za1"]]
FILL_CD = [["zc0"], ["zc1"], ["zd0"], ["zd1"]] + [[] for _ in range(12)]
FILL_A = [SILU[10 + 2 * i:12 + 2 * i] for i in range(8)]


def mixer_kernel(nc, a, out):
    ctx = ExitStack()
    with ctx:
        sems = {}

        def sem(name):
            if name not in sems:
                sems[name] = ctx.enter_context(nc.semaphore(name))
            return sems[name]

        def sb(name, shape):
            return ctx.enter_context(nc.sbuf_tensor(name, shape, F32))

        def cut(ap, n):
            return ap.rearrange("p (k n) -> p k n", n=n)

        ring = sb("ring", [P, NSLOT, SLOT])
        xT = sb("xT", [P, KD, S])
        hT = sb("hT", [P, KD, S])
        wide = sb("wide", [P, KD * S])
        ident = sb("ident", [P, P])
        ones = sb("ones", [P, P])
        halves = sb("halves", [P, P])
        cols = sb("cols", [P, N_ROWS_A + N_ROWS_B + 4 * TAPS])
        silu_c = sb("silu_c", [P, KD])
        mod = sb("mod", [P, 48])
        gain1 = sb("gain1", [P, KD])
        gain2 = sb("gain2", [P, KD])
        sinks = sb("sinks", [P, NH])
        sinks8 = sb("sinks8", [P, NH])
        cmp_bias = sb("cmp_bias", [P, 2, NH, NCMP])
        decay = sb("decay", [P, RH, LINE])
        cos_t = sb("cos_t", [P, S])
        sin_t = sb("sin_t", [P, S])
        dil_bias = sb("dil_bias", [P, AG, AH, S])
        prob = sb("prob", [P, 2, 4, S])
        probT = sb("probT", [P, 3 * 2 * 4 * P])
        sq = sb("sq", [P, 512])
        rstd = sb("rstd", [P, 512])
        stat = sb("stat", [P, 2, 20])
        bn = sb("bn", [P, 2, 10])
        tmp = sb("tmp", [P, 2, 512])
        rel = sb("rel", [32, AG * AH])
        line = sb("line", [AH, AG, LINE])
        vb2 = sb("vb2", [NCMP, 2, HD])
        kw2 = sb("kw2", [P, 2, 2, HD])
        vw2 = sb("vw2", [P, 2, HD])
        arena = sb("arena", [P, 19456])

        def place(at, *shape):
            n = int(np.prod(shape))
            assert at + n <= 19456
            v = arena[:, at:at + n]
            if len(shape) == 2:
                return cut(v, shape[1])
            if len(shape) == 3:
                return v.rearrange("p (a b c) -> p a b c", b=shape[1], c=shape[2])
            return v

        alibi = place(0, NH, S)
        swa = place(2048, NH, S)
        ada_acc = place(4096, 6 * D)
        ada_slab = place(10240, 2, KD, P)
        L = 12288
        rows_a, rows_b, rows_c = place(L, P), place(L + P, P), place(L + 2 * P, GW)
        onehot = place(L + 768, AG, LINE)
        linemask = place(L + 1920, AG, LINE)
        bqT, bkT, bv = place(L, 4, S), place(L + 1024, 4, S), place(L + 2048, 2, GW)
        hpad = place(L + 3072, 4, PADW)
        yT0 = place(L + 4224, KD, S)
        u_val = cut(wide[:, 0:1024], S)
        qcT, qdT = place(L, 4, S), place(L + 1024, 4, S)
        ksT, kwT, kdT = place(L + 2048, S), place(L + 2304, S), place(L + 2560, S)
        vs, vw, vd = place(L + 2816, 2, P), place(L + 3072, 2, P), place(L + 3328, 2, P)
        gates = place(L + 3584, 2, 24)
        kcn = place(L + 3632, 2 * NCMP)
        vcn = place(L + 3664, P)
        yT1 = place(L + 4224, KD, S)
        kcv = cut(wide[:, 0:512], S)
        pairs = wide[:, 512:1536].rearrange("p (v g t) -> p v g t", v=2, g=2)
        blocks = probT[:, 0:960].rearrange("p (v j n) -> p v j n", v=2, j=16)
        hid_x = probT[:, 960:1080].rearrange("p (v k n) -> p v k n", v=2, k=2)
        hid_e = probT[:, 1080:1200].rearrange("p (v k n) -> p v k n", v=2, k=2)
        yretT = place(0, 16, S)
        rqT, rkT, rv = place(4096, 8, S), place(6144, 8, S), place(8192, 2, RH * RDV)
        av = place(4096, AG, 2, GW)
        gaT, gbT = place(8192, 8, S), place(10240, 8, S)
        aqT, akT = place(12288, AG, AH * S), place(15360, AG, AH * S)
        attT = place(18432, AH, S)
        mT = place(12288, 8, S)
        hidT = place(0, 32, S)
        ron = probT[:, 0:2048].rearrange("p (h t n) -> p h t n", h=2, t=2)
        pTv = probT[:, :].rearrange("p (b k i q) -> p b k i q", b=3, k=2, i=4)

        pp = [ctx.enter_context(nc.psum_tensor(f"proj{i}", [P, 512], F32)) for i in range(NPP)]
        st = ctx.enter_context(nc.psum_tensor("sums", [P, 512], F32))
        sc = [ctx.enter_context(nc.psum_tensor(f"scores{i}", [P, 512], F32)) for i in range(2)]
        pt = ctx.enter_context(nc.psum_tensor("transposed", [P, 512], F32))
        po = ctx.enter_context(nc.psum_tensor("mixed", [P, 512], F32))
        lines_d = nc.dram_tensor("dil_lines", (AG * AH, P, LINE), F32, kind="Internal").ap()

        slab_in = [sem(f"slab_in{i}") for i in range(NSLOT)]
        bank_free = [sem(f"bank_free{i}") for i in range(NPP)]
        proj_ready = sem("proj_ready")
        setup_in, x_in, const_in, bias_in = sem("setup_in"), sem("x_in"), sem("const_in"), sem("bias_in")
        h_pre, h_ready = sem("h_pre"), sem("h_ready")
        norm_sq, norm_sum = sem("norm_sq"), sem("norm_sum")
        norm_var, norm_sqrt, norm_done = sem("norm_var"), sem("norm_sqrt"), sem("norm_done")
        sc_ready, sc_free = sem("sc_ready"), sem("sc_free")
        mx_ready, exp_done, p_ready = sem("mx_ready"), sem("exp_done"), sem("p_ready")
        tr_ready, pt_ready = sem("tr_ready"), sem("pt_ready")
        pv_ready, po_free = sem("pv_ready"), sem("po_free")

        N_SETUP = 3 + len(ROWS_A) + len(ROWS_B) + len(HALF_ROWS) + 10

        def col(name, k=0, n=1):
            if name in ROWS_A:
                at = ROWS_A[name][0]
            else:
                at = N_ROWS_A + ROWS_B[name][0]
            return cols[:, at + k:at + k + n]

        def conv_col(c, tap):
            at = N_ROWS_A + N_ROWS_B + c * TAPS + tap
            return cols[:, at:at + 1]

        def bank(name):
            return pp[GROUP_AT[name] % NPP]

        def evacuated(name):
            m = GROUP_AT[name]
            return bank_free[m % NPP], m // NPP + 1

        def free_of(name):
            return bank_free[GROUP_AT[name] % NPP]

        class Steps:

            def __init__(self, eng, name):
                self.eng, self.sem, self.n = eng, sem(name), 0

            def did(self, ins):
                ins.then_inc(self.sem, 1)
                self.n += 1

            def settle(self):
                self.eng.wait_ge(self.sem, self.n)

        block = ctx.enter_context(nc.Block())

        @block.sync
        def _(sp):
            sp.dma_start(cut(wide[:, :], D), a["x"][0].rearrange("(t p) d -> p t d", p=P)).then_inc(x_in, 16)

            def source(name):
                two = lambda w, c, n: w[:, c:c + n].rearrange("(k p) n -> p k n", p=P)
                if name in EV:
                    return two(a["e_w_in"][0], EV[name], 512)
                if name in OD:
                    return two(a["o_w_in"][0], OD[name], dict(kw=280, kd=256).get(name, 512))
                if name.startswith("wo"):
                    c = 512 * (name[3] == "b")
                    return two(a["w_out"][0] if name[2] == "0" else a["w_o_2"][0], c, 512)
                if name in ("ck", "cv"):
                    return two(a["c_k_w1" if name == "ck" else "c_v_w1"][0], 0, 256)
                if name == "wa":
                    return two(a["w_att_out_2"][0], 0, 1024)
                i = int(name[-1])
                if name[:2] == "wr":
                    return two(a["w_ret_out_2"][0], 256 * i, 256)
                if name[:2] == "f1":
                    return two(a["w_ff1_2"][0], 512 * i, 512)
                if name[:2] == "f2":
                    return two(a["w_ff2_2"][0], 128 * i, 128)
                if name[0] == "a":
                    return two(a["w_in_2"][0], IN2_ATT + 1536 * i + 512 * "qkv".index(name[1]), 512)
                at = dict(rq=IN2_Q, rk=IN2_K, rv=IN2_V, rg=IN2_G, ga=IN2_GATE, gb=IN2_GATE + D)[name[:2]]
                return two(a["w_in_2"][0], at + 512 * i, 512)

            for n, (name, kt, w) in enumerate(SLABS):
                if n >= NSLOT:
                    sp.wait_ge(proj_ready, slab_last_group(SLABS[n - NSLOT][0]) + 1)
                dst = cut(ring[:, n % NSLOT, 0:kt * w], w)
                if name.startswith("wo1"):
                    c = 512 * (name[3] == "b")
                    rows = a["w_out"][1][:, c:c + 512].rearrange("(s g b d) n -> s g d b n", s=2, g=2, b=4)
                    for s in range(2):
                        for g in range(2):
                            sp.dma_start(dst[HD * g:HD * g + HD, 4 * s:4 * s + 4, :], rows[s, g]) \
                              .then_inc(slab_in[n % NSLOT], 16)
                elif name in PAIRED:
                    for h in range(NH):
                        to = HD * (2 * (h % 4) + h // 4)
                        sp.dma_start(dst[:, :, to:to + HD], source(name)[:, :, HD * h:HD * h + HD]).then_inc(slab_in[n % NSLOT], 16)
                else:
                    sp.dma_start(dst, source(name)).then_inc(slab_in[n % NSLOT], 16)

        @block.gpsimd
        def _(pool):
            for dst, src in ((alibi, a["alibi"]), (cmp_bias[:], a["cmp_bias"]), (swa, a["swa"])):
                pool.dma_start(dst, src).then_inc(const_in, 16)
            w_ada = a["w_ada_2"][0].rearrange("(k p) n -> p k n", p=P)
            ada_in = [sem("ada_in0"), sem("ada_in1")]
            own = Steps(pool, "pool_step")
            n_ada = 6 * D // P
            for j in range(2):
                pool.dma_start(ada_slab[:, j], w_ada[:, :, P * j:P * j + P]).then_inc(ada_in[j], 16)
            for dst, src in ((decay[:], a["decay"]), (cos_t[:], a["cos"]), (sin_t[:], a["sin"])):
                pool.dma_start(dst, src).then_inc(const_in, 16)
            pool.wait_ge(sem("line_ready"), AG)
            for g in range(AG):
                pool.dma_start(lines_d[AH * g:AH * g + AH], line[:, g, :].unsqueeze(1).broadcast_to([AH, P, LINE])) \
                    .then_inc(sem("lines_out"), 16)
            pool.wait_ge(sem("lines_out"), 16 * AG)
            flat = lines_d.rearrange("h r u -> (h r u)")
            skew = bass.AP(flat.tensor, P - 1, [[LINE - 1, P], [P * LINE, AG * AH], [1, S]])
            pool.dma_start(dil_bias[:].rearrange("p g h j -> p (g h) j"), skew).then_inc(sem("dil_in"), 16)
            pool.wait_ge(sem("silu_c_ready"), 1)
            for j in range(n_ada):
                w = ada_slab[:, j % 2]
                pool.wait_ge(ada_in[j % 2], 16 * (j // 2 + 1))
                own.did(nc.gpsimd.tensor_tensor(w, w, silu_c[:].unsqueeze(2).broadcast_to([P, KD, P]), ALU.mult))
                own.settle()
                for half in (4, 2):
                    own.did(nc.gpsimd.tensor_tensor(w[:, 0:half], w[:, 0:half], w[:, half:2 * half], ALU.add))
                    own.settle()
                ins = nc.gpsimd.tensor_tensor(ada_acc[:, P * j:P * j + P], w[:, 0], w[:, 1], ALU.add)
                ins.then_inc(sem("ada_sum"), 1)
                if j + 2 < n_ada:
                    pool.wait_ge(sem("ada_sum"), j + 1)
                    pool.dma_start(w, w_ada[:, :, P * (j + 2):P * (j + 2) + P]).then_inc(ada_in[j % 2], 16)

        @block.tensor
        def _(pe):
            state = dict(filled=0, norm=0)

            def begin(name):
                m = state["filled"]
                assert GROUPS[m] == name, (GROUPS[m], name)
                if m >= NPP:
                    pe.wait_ge(bank_free[m % NPP], m // NPP)
                return pp[m % NPP]

            def end(last):
                last.then_inc(proj_ready, 1)
                state["filled"] += 1

            def slab(name):
                n = SLAB_AT[name]
                pe.wait_ge(slab_in[n % NSLOT], slab_target(n))
                kt, w = SLABS[n][1:]
                return cut(ring[:, n % NSLOT, 0:kt * w], w)

            def features(name, w, lhs, rhs, nblk=2, fresh=None):
                b = begin(name)
                kt = w.shape[1]
                for j in range(nblk):
                    for k in range(kt):
                        if fresh is not None and j == 0:
                            pe.wait_ge(h_ready, KD * fresh + k + 1)
                        last = nc.tensor.matmul(b[:, S * j:S * j + S], lhs(w, k, j), rhs[:, k, :],
                                                start=k == 0, stop=k == kt - 1)
                end(last)

            def tokens(name, w, c, n, tiles, step):
                b = begin(name)
                for i, t in enumerate(tiles):
                    for k in range(KD):
                        last = nc.tensor.matmul(b[:, step * i:step * i + n], hT[:, k, P * t:P * t + P], w[:, k, c:c + n],
                                                start=k == 0, stop=k == KD - 1)
                end(last)

            def plain(c0):
                return lambda w, k, j: w[:, k, c0 + P * j:c0 + P * j + P]

            def slab_features(name, groups, rhs=None, fresh=None):
                w = slab(name)
                for i, g in enumerate(groups):
                    features(g, w, plain(256 * i), hT if rhs is None else rhs, fresh=fresh if i == 0 else None)

            def norm_sums(name, mat, src, chunks, w):
                n = NORM_AT[name]
                assert n == state["norm"]
                state["norm"] += 1
                pe.wait_ge(norm_sq, n + 1)
                if n:
                    pe.wait_ge(norm_var, n)
                for k in range(chunks):
                    last = nc.tensor.matmul(st[:, 0:w], mat[:], src[:, k], start=k == 0, stop=k == chunks - 1)
                last.then_inc(norm_sum, 1)

            def stream_sums(name):
                norm_sums(name, ones, cut(wide[:, :], S), KD, S)

            def head_sums(name, w=512):
                norm_sums(name, halves, sq[:, 0:w].unsqueeze(1), 1, w)

            def scores(u):
                part, step, br, last_br, at, qt, n = UNITS[u]
                if u:
                    pe.wait_ge(sc_free, u)
                if part == "a":
                    for g in range(AG):
                        q = aqT[:, g, S * at + P * qt:S * at + P * qt + P]
                        last = nc.tensor.matmul(sc[g // 2][:, S * (g % 2):S * (g % 2) + n], q,
                                                akT[:, g, S * at:S * at + n], start=True, stop=True)
                else:
                    q, k = dict(b=(bqT, None), c=(qcT, (kcn, ksT, kwT)[br]), d=(qdT, kdT))[part]
                    for bi in range(2):
                        for f in range(2):
                            lo, b = HD * f, 2 * at + bi
                            if part == "b":
                                keys = bkT[lo:lo + HD, b, 0:n]
                            elif br == 0 and part == "c":
                                keys = kcn[lo:lo + HD, NCMP * f:NCMP * f + n]
                            else:
                                keys = k[lo:lo + HD, 0:n]
                            last = nc.tensor.matmul(sc[f][:, S * bi:S * bi + n], q[lo:lo + HD, b, P * qt:P * qt + P],
                                                    keys, start=True, stop=True)
                last.then_inc(sc_ready, 1)

            def transposes(u):
                part, step, br, last_br, at, qt, n = UNITS[u]
                pe.wait_ge(p_ready, u + 1)
                for r in range(key_tiles(u)):
                    if rounds_before(u) + r:
                        pe.wait_ge(pt_ready, rounds_before(u) + r)
                    for i in range(3 if part == "a" else 4):
                        w = min(n - P * r, P)
                        last = nc.tensor.transpose(pt[0:w, P * i:P * i + P], prob[:, u % 2, i, P * r:P * r + w], ident[:])
                    last.then_inc(tr_ready, 1)

            def mix(u):
                part, step, br, last_br, at, qt, n = UNITS[u]
                pe.wait_ge(pt_ready, rounds_before(u + 1))
                if step:
                    pe.wait_ge(po_free, step)
                if part == "a":
                    todo = [(g, r) for g in range(AG) for r in range(qt + 1)]
                    for i, (g, r) in enumerate(todo):
                        last = nc.tensor.matmul(po[:, 0:P], av[:, g, r, P * at:P * at + P], pTv[:, 0, r, g, :],
                                                start=i == 0, stop=i == len(todo) - 1)
                else:
                    for bi in range(2):
                        for f in range(2):
                            b = 2 * at + bi
                            todo = []
                            for x in range(br + 1):
                                if part == "c" and x == 0:
                                    todo.append((vcn[0:NCMP, HD * f:HD * f + HD], pTv[0:NCMP, 0, 0, 2 * f + bi, :]))
                                    continue
                                for r in range(qt + 1):
                                    v = bv[:, r, HD * (2 * b + f):HD * (2 * b + f) + HD] if part == "b" else \
                                        (vd if part == "d" else (None, vs, vw)[x])[:, r, HD * f:HD * f + HD]
                                    todo.append((v, pTv[:, x, r, 2 * f + bi, :]))
                            for i, (v, p) in enumerate(todo):
                                last = nc.tensor.matmul(po[HD * f:HD * f + HD, P * bi:P * bi + P], v, p,
                                                        start=i == 0, stop=i == len(todo) - 1)
                last.then_inc(pv_ready, 1)

            def attention(units, fill):
                scores(units[0])
                for i, u in enumerate(units):
                    if i + 1 < len(units):
                        scores(units[i + 1])
                    for f in fill[i]:
                        f()
                    transposes(u)
                    if UNITS[u][3]:
                        mix(u)

            pe.wait_ge(setup_in, 16 * N_SETUP)
            b = begin("vec")
            nc.tensor.transpose(b[:, 0:N_ROWS_A], rows_a[0:N_ROWS_A, :], ident[0:N_ROWS_A, 0:N_ROWS_A])
            nc.tensor.transpose(b[:, 128:128 + N_ROWS_B], rows_b[0:N_ROWS_B, :], ident[0:N_ROWS_B, 0:N_ROWS_B])
            for c in range(4):
                last = nc.tensor.transpose(b[:, 256 + 32 * c:256 + 32 * c + TAPS], rows_c[0:TAPS, P * c:P * c + P],
                                           ident[0:TAPS, 0:TAPS])
            end(last)
            for g in range(AG):
                b = begin(f"dl{g}")
                end(nc.tensor.matmul(b[0:AH, 0:LINE], rel[:, AH * g:AH * g + AH], onehot[0:32, g, :], start=True, stop=True))
            pe.wait_ge(x_in, 16)
            for i in range(4):
                b = begin(f"x{i}")
                for j in range(2):
                    for t in range(TT):
                        c = D * t + P * (2 * i + j)
                        last = nc.tensor.transpose(b[:, S * j + P * t:S * j + P * t + P], wide[:, c:c + P], ident[:])
                end(last)

            stream_sums("x0")
            slab_features("uv", ["uv0", "uv1"], fresh=0)
            slab_features("ug", ["ug0", "ug1"])
            w = slab("bq")
            features("bq0", w, plain(0), hT)
            features("bq1", w, plain(256), hT)
            head_sums("bq0")
            w = slab("bk")
            features("bk0", w, plain(0), hT)
            head_sums("bq1")
            features("bk1", w, plain(256), hT)
            head_sums("bk0")
            w = slab("bv")
            tokens("bv0", w, 0, GW, [0], 512)
            head_sums("bk1")
            tokens("bv1", w, 0, GW, [1], 512)
            pe.wait_ge(norm_done, NORM_AT["bk1"] + 1)
            pe.wait_ge(*evacuated("bv1"))
            fill = [[lambda n=n: features(n, slab(n[:2]), plain(256 * int(n[2])), hT) for n in f] for f in FILL_B]
            attention(PART["b"], fill)
            pe.wait_ge(sem("conv_done"), 1)
            for c in range(4):
                last = nc.tensor.matmul(st[:, 0:S], ones[:], yT0[:, c, :], start=c == 0, stop=c == 3)
            last.then_inc(sem("ln_mean"), 1)
            pe.wait_ge(sem("ln_sq"), 1)
            for c in range(4):
                last = nc.tensor.matmul(st[:, 0:S], ones[:], wide[:, S * c:S * c + S], start=c == 0, stop=c == 3)
            last.then_inc(sem("ln_sum"), 1)
            pe.wait_ge(po_free, UNITS[PART["b"][-1]][1] + 1)
            pe.wait_ge(sem("y_a_ready"), 1)
            slab_features("wo0a", ["wo0_0", "wo0_1"], yT0)
            slab_features("wo0b", ["wo0_2", "wo0_3"], yT0)

            stream_sums("x1")
            w = slab("kc")
            features("kcvc", w, plain(0), hT, fresh=1)
            features("ks", w, plain(256), hT, nblk=1)
            tokens("vs", w, 384, P, [0, 1], 256)
            head_sums("ks", S)
            w = slab("qc")
            features("qc0", w, plain(0), hT)
            features("qc1", w, plain(256), hT)
            head_sums("qc0")
            w = slab("kw")
            features("kw", w, plain(0), hT, nblk=1)
            head_sums("qc1")
            tokens("vw", w, 128, P + 24, [0, 1], 256)
            head_sums("kw", S)
            pe.wait_ge(sem("blocks_ready"), 4)
            for v, (name, group) in enumerate((("ck", "hidk"), ("cv", "hidv"))):
                w = slab(name)
                b = begin(group)
                for nb in range(2):
                    for j in range(16):
                        last = nc.tensor.matmul(b[:, 32 * nb:32 * nb + 30], w[:, j, P * nb:P * nb + P], blocks[:, v, j, :],
                                                start=j == 0, stop=j == 15)
                end(last)
            pe.wait_ge(sem("hid_ready"), 1)
            b = begin("kc2")
            for k in range(2):
                last = nc.tensor.matmul(b[:, 0:30], kw2[:, k].rearrange("p g d -> p (g d)"), hid_x[:, 0, k, :],
                                        start=k == 0, stop=k == 1)
            end(last)
            pe.wait_ge(sem("hid_ready"), 2)
            b = begin("vc2")
            for g in range(2):
                for k in range(2):
                    last = nc.tensor.matmul(b[0:NCMP, HD * g:HD * g + HD], hid_x[:, 1, k, NCMP * g:NCMP * g + NCMP],
                                            vw2[:, k, :], start=k == 0, stop=k == 1)
            end(last)
            w = slab("qd")
            features("qd0", w, plain(0), hT)
            head_sums("cmp", 30)
            features("qd1", w, plain(256), hT)
            head_sums("qd0")
            w = slab("kd")
            features("kd", w, plain(0), hT, nblk=1)
            head_sums("qd1")
            tokens("vd", w, 128, P, [0, 1], 256)
            head_sums("kd", S)
            pe.wait_ge(norm_done, NORM_AT["kd"] + 1)
            pe.wait_ge(*evacuated("vs"))
            pe.wait_ge(*evacuated("vw"))
            pe.wait_ge(*evacuated("vc2"))
            pe.wait_ge(*evacuated("vd"))
            fill = [[lambda n=n: features(n, slab(n[:2]), plain(256 * int(n[2])), hT) for n in f] for f in FILL_CD]
            attention(PART["c"] + PART["d"], fill)
            pe.wait_ge(sem("ada_sum"), 6 * D // P)
            b = begin("mod")
            for j in range(6 * D // P):
                last = nc.tensor.matmul(b[:, j:j + 1], ada_acc[:, P * j:P * j + P], ones[:, 0:1], start=True, stop=True)
            end(last)
            pe.wait_ge(po_free, UNITS[PART["d"][-1]][1] + 1)
            slab_features("wo1a", ["wo1_0", "wo1_1"], yT1)
            slab_features("wo1b", ["wo1_2", "wo1_3"], yT1)

            stream_sums("x2")
            for i in range(2):
                slab_features(f"rq{i}", [f"rq{2 * i}", f"rq{2 * i + 1}"], fresh=2 if i == 0 else None)
            for i in range(2):
                slab_features(f"rk{i}", [f"rk{2 * i}", f"rk{2 * i + 1}"])
            for s in range(4):
                w = slab(f"rv{s}")
                for t in range(TT):
                    tokens(f"rv{s}_{t}", w, 0, 512, [t], 512)

            def dilated_fill(name):
                w, i = slab(name[:3]), int(name[-1])
                if name[1] == "v":
                    tokens(name, w, 0, 512, [i], 512)
                else:
                    features(name, w, plain(256 * i), hT)

            for h in range(RH):
                pe.wait_ge(*evacuated(f"rk{h}"))
                if h >= 2:
                    pe.wait_ge(sem("ret_decayed"), h - 1)
                for jt in range(2):
                    n, at = (S, 0) if jt == 0 else (P, S)
                    for k in range(2):
                        last = nc.tensor.matmul(sc[h % 2][:, at:at + n], rkT[:, 2 * h + k, P * jt:P * jt + P],
                                                rqT[:, 2 * h + k, S - n:S], start=k == 0, stop=k == 1)
                last.then_inc(sem("ret_scores"), 1)
                for i in range(2):
                    dilated_fill(RET_FILL[4 * h + i])
                pe.wait_ge(sem("ret_decayed"), h + 1)
                pe.wait_ge(*evacuated(f"rv{h}_1"))
                if h:
                    pe.wait_ge(sem("ret_normed"), 2 * h)
                e = prob[:, h % 2].rearrange("p i j -> p (i j)")
                for t, dst in enumerate((pt, po)):
                    for jt in range(t + 1):
                        at = P * t if jt == 0 else S
                        last = nc.tensor.matmul(dst[:], e[:, at:at + P], rv[:, jt, RDV * h:RDV * h + RDV],
                                                start=jt == 0, stop=jt == t)
                    last.then_inc(sem("ret_out"), 1)
                for i in range(2, 4):
                    dilated_fill(RET_FILL[4 * h + i])
                pe.wait_ge(sem("ret_normed"), 2 * h + 2)
                for half in range(2):
                    b = begin(f"rt{h}_{half}")
                    for j in range(2):
                        for t in range(TT):
                            c = P * (2 * half + j)
                            last = nc.tensor.transpose(b[:, S * j + P * t:S * j + P * t + P], ron[:, h % 2, t, c:c + P], ident[:])
                    end(last)
            for name in RET_FILL[16:]:
                dilated_fill(name)

            pe.wait_ge(*evacuated("av2_1"))
            fill = [[lambda n=n: features(n, slab(f"{n[:2]}{int(n[2]) // 2}"), plain(256 * (int(n[2]) % 2)), hT) for n in f]
                    for f in FILL_A]
            attention(PART["a"], fill)

            pe.wait_ge(*evacuated("rg7"))
            for i in range(4):
                features(f"wr{i}", slab(f"wr{i}"), plain(0), yretT)
            pe.wait_ge(po_free, UNITS[-1][1] + 1)
            for i in range(4):
                features(f"wa{i}", slab("wa"), plain(256 * i), attT)
            pe.wait_ge(sem("merged"), 1)
            slab_features("wo2a", ["wo2_0", "wo2_1"], mT)
            slab_features("wo2b", ["wo2_2", "wo2_3"], mT)

            stream_sums("x3")
            for i in range(8):
                slab_features(f"f1_{i}", [f"f1_{2 * i}", f"f1_{2 * i + 1}"], fresh=3 if i == 0 else None)
            pe.wait_ge(sem("hid_sq"), 16)
            for i in range(8):
                features(f"f2_{i}", slab(f"f2_{i}"), plain(0), hidT, nblk=1)
            stream_sums("xf")
            for i in range(4):
                t, half = divmod(i, 2)
                b = begin(f"out{i}")
                for j in range(4):
                    pe.wait_ge(h_ready, KD * 4 + 4 * half + j + 1)
                    last = nc.tensor.transpose(b[:, P * j:P * j + P], hT[:, 4 * half + j, P * t:P * t + P], ident[:])
                end(last)
            assert state["filled"] == len(GROUPS) and state["norm"] == len(NORMS)

        @block.scalar
        def _(act):
            own = Steps(act, "act_step")

            def vector_rows(name, n):
                src = a[name]
                flat = src if len(src.shape) == 1 else src.rearrange("l d -> (l d)") if len(src.shape) == 2 else \
                    src.rearrange("l d n -> (l d n)")
                return flat.rearrange("(k p) -> k p", p=P)

            n = 0
            act.dma_start(ident[:], a["ident"]).then_inc(setup_in, 16)
            act.dma_start(ones[:], a["ones"]).then_inc(setup_in, 16)
            act.dma_start(halves[:], a["halves"]).then_inc(setup_in, 16)
            n += 3
            for rows, plan in ((rows_a, ROWS_A), (rows_b, ROWS_B)):
                for name, (at, c) in plan.items():
                    if name in HALF_ROWS:
                        for f in range(2):
                            act.dma_start(rows[at:at + 1, HD * f:HD * f + HD], a[name]).then_inc(setup_in, 16)
                            n += 1
                    else:
                        act.dma_start(rows[at:at + c, :], vector_rows(name, c)).then_inc(setup_in, 16)
                        n += 1
            for dst, src in ((rows_c[0:TAPS, :], a["a_conv_w"][0]), (rel[:], a["rel_bias_2"]), (onehot[0:32], a["onehot"]),
                             (linemask[0:AH], a["linemask"]), (sinks[:], a["d_sinks"][0].partition_broadcast(P)),
                             (kw2[:, :, 0, :], a["c_k_w2"][0].rearrange("(k p) d -> p k d", p=P)),
                             (kw2[:, :, 1, :], a["c_k_w2"][0].rearrange("(k p) d -> p k d", p=P)),
                             (vw2[:], a["c_v_w2"][0].rearrange("(k p) d -> p k d", p=P)),
                             (vb2[:, 0, :], a["c_v_b2"][0].partition_broadcast(NCMP)),
                             (vb2[:, 1, :], a["c_v_b2"][0].partition_broadcast(NCMP))):
                act.dma_start(dst, src).then_inc(setup_in, 16)
                n += 1
            assert n == N_SETUP, n

            def ready(name):
                act.wait_ge(proj_ready, GROUP_AT[name] + 1)
                return bank(name)

            def copy_out(name, dst, w=512, lo=0, fn=ACT.Copy):
                b = ready(name)
                nc.scalar.activation(dst, b[:, lo:lo + w], fn).then_inc(free_of(name), 1)

            def head_squares(name, dst, w=512):
                n = NORM_AT[name]
                b = ready(name)
                act.wait_ge(norm_sum, n)
                nc.scalar.activation(sq[:, 0:w], b[:, 0:w], ACT.Square).then_inc(norm_sq, 1)
                nc.scalar.activation(dst, b[:, 0:w], ACT.Copy).then_inc(free_of(name), 1)

            def root(name, w=512):
                act.wait_ge(norm_var, NORM_AT[name] + 1)
                nc.scalar.activation(rstd[:, 0:w], rstd[:, 0:w], ACT.Sqrt).then_inc(norm_sqrt, 1)

            def stream_squares(name, after):
                act.wait_ge(*evacuated(after))
                n = NORM_AT[name]
                if n:
                    act.wait_ge(norm_sum, n)
                nc.scalar.activation(wide[:, :], xT[:].rearrange("p k t -> p (k t)"), ACT.Square).then_inc(norm_sq, 1)
                root(name, S)

            def exp_neg(name):
                z = SILU.index(name)
                b = ready(name)
                if z >= 2:
                    act.wait_ge(*evacuated(SILU[z - 2]))
                nc.scalar.activation(tmp[:, z % 2], b[:], ACT.Exp, scale=-1.0).then_inc(sem("silu_exp"), 1)

            def exps(u):
                part, step, br, last_br, at, qt, n = UNITS[u]
                act.wait_ge(mx_ready, u + 1)
                s = stat[:, u % 2]
                if part == "a":
                    nc.scalar.activation(prob[:, u % 2, 0:AG, 0:n], prob[:, u % 2, 0:AG, 0:n], ACT.Exp, bias=s[:, 4:5],
                                         accum_out=s[:, 8:9]).then_inc(exp_done, 1)
                    return
                for i in range(4):
                    last = nc.scalar.activation(prob[:, u % 2, i, 0:n], prob[:, u % 2, i, 0:n], ACT.Exp, bias=s[:, 4 + i:5 + i],
                                                scale=0.125, accum_out=s[:, 8 + i:9 + i])
                if part == "d":
                    last = nc.scalar.activation(s[:, 16:20], s[:, 16:20], ACT.Exp)
                last.then_inc(exp_done, 1)

            def transposed_out(u):
                part, step, br, last_br, at, qt, n = UNITS[u]
                m = 3 if part == "a" else 4
                for r in range(key_tiles(u)):
                    act.wait_ge(tr_ready, rounds_before(u) + r + 1)
                    if step:
                        act.wait_ge(pv_ready, step)
                    w = min(n - P * r, P)
                    nc.scalar.activation(pTv[0:w, br, r, 0:m, :], cut(pt[0:w, 0:P * m], P), ACT.Copy).then_inc(pt_ready, 1)

            def attention(units, fill):
                exps(units[0])
                for i, u in enumerate(units):
                    if i + 1 < len(units):
                        exps(units[i + 1])
                    for name in fill[i]:
                        exp_neg(name)
                    transposed_out(u)

            act.wait_ge(*evacuated("vec"))
            nc.scalar.activation(silu_c[:], col("c_2", 0, 8), ACT.Exp, scale=-1.0).then_inc(sem("c_exp"), 1)

            stream_squares("x0", "x3")
            copy_out("uv0", wide[:, 0:512])
            copy_out("uv1", wide[:, 512:1024])
            exp_neg("ug0")
            exp_neg("ug1")
            fl = lambda ap: ap.rearrange("p k t -> p (k t)")
            head_squares("bq0", fl(bqT[:, 0:2]))
            head_squares("bq1", fl(bqT[:, 2:4]))
            root("bq0")
            head_squares("bk0", fl(bkT[:, 0:2]))
            root("bq1")
            head_squares("bk1", fl(bkT[:, 2:4]))
            root("bk0")
            copy_out("bv0", bv[:, 0])
            root("bk1")
            copy_out("bv1", bv[:, 1])
            attention(PART["b"], FILL_B)
            act.wait_ge(sem("ln_centred"), 1)
            y_a = fl(yT0[:, 0:4])
            nc.scalar.activation(wide[:, 0:1024], y_a, ACT.Square).then_inc(sem("ln_sq"), 1)
            act.wait_ge(sem("ln_var"), 1)
            nc.scalar.activation(rstd[:, 0:S], rstd[:, 0:S], ACT.Sqrt).then_inc(sem("ln_sqrt"), 1)
            act.wait_ge(sem("ln_scaled"), 1)
            for c in range(4):
                own.did(nc.scalar.activation(yT0[:, c, :], yT0[:, c, :], ACT.Identity, bias=col("a_ln_b", c), scale=col("a_ln_g", c)))
            own.settle()
            nc.scalar.activation(wide[:, 0:1024], y_a, ACT.Exp, scale=-1.0).then_inc(sem("ln_exp"), 1)

            stream_squares("x1", "wo0_3")
            copy_out("kcvc", fl(kcv))
            act.wait_ge(*evacuated("kcvc"))
            for f in range(2):
                for g in range(2):
                    act.dma_start(pairs[HD * f:HD * f + HD, :, g, 0:S - f], kcv[HD * g:HD * g + HD, :, f:S]) \
                        .then_inc(sem("pairs_in"), 16)
            head_squares("ks", ksT, S)
            b = ready("vs")
            nc.scalar.activation(vs, cut(b[:], 256)[:, :, 0:P], ACT.Copy).then_inc(free_of("vs"), 1)
            root("ks", S)
            head_squares("qc0", fl(qcT[:, 0:2]))
            head_squares("qc1", fl(qcT[:, 2:4]))
            root("qc0")
            head_squares("kw", kwT, S)
            root("qc1")
            b = ready("vw")
            nc.scalar.activation(gates, cut(b[:], 256)[:, :, P:P + 24], ACT.Exp, scale=-1.0).then_inc(sem("gate_exp"), 1)
            nc.scalar.activation(vw, cut(b[:], 256)[:, :, 0:P], ACT.Copy).then_inc(free_of("vw"), 1)
            root("kw", S)
            for v, (group, bias) in enumerate((("hidk", "c_k_b1"), ("hidv", "c_v_b1"))):
                b = ready(group)
                for k in range(2):
                    last = nc.scalar.activation(hid_x[:, v, k, :], b[:, 32 * k:32 * k + 30], ACT.Identity, bias=col(bias, k))
                last.then_inc(free_of(group), 1)
                act.wait_ge(*evacuated(group))
                nc.scalar.activation(hid_e[:, v], hid_x[:, v], ACT.Exp, scale=-1.0).then_inc(sem("hid_exp"), 1)
            b = ready("kc2")
            nc.scalar.activation(kcn, b[:, 0:30], ACT.Identity, bias=col("c_k_b2")).then_inc(free_of("kc2"), 1)
            act.wait_ge(*evacuated("kc2"))
            act.wait_ge(norm_sum, NORM_AT["cmp"])
            nc.scalar.activation(sq[:, 0:30], kcn, ACT.Square).then_inc(norm_sq, 1)
            head_squares("qd0", fl(qdT[:, 0:2]))
            root("cmp", 30)
            head_squares("qd1", fl(qdT[:, 2:4]))
            root("qd0")
            head_squares("kd", kdT, S)
            root("qd1")
            b = ready("vd")
            nc.scalar.activation(vd, cut(b[:], 256)[:, :, 0:P], ACT.Copy).then_inc(free_of("vd"), 1)
            root("kd", S)
            attention(PART["c"] + PART["d"], FILL_CD)

            def shifted(fresh, shift):
                for k in range(KD):
                    act.wait_ge(h_pre, KD * fresh + k + 1)
                    nc.scalar.activation(hT[:, k, :], hT[:, k, :], ACT.Identity, bias=mod[:, shift + k:shift + k + 1]) \
                        .then_inc(h_ready, 1)

            stream_squares("x2", "wo1_3")
            shifted(0, 0)
            for s in range(4):
                for t in range(TT):
                    copy_out(f"rv{s}_{t}", rv[:, t, 512 * s:512 * s + 512])

            def dilated_out(name):
                g, i = int(name[2]), int(name[-1])
                if name[1] == "v":
                    copy_out(name, av[:, g, i])
                else:
                    copy_out(name, (aqT if name[1] == "q" else akT)[:, g, 512 * i:512 * i + 512])

            for h in range(RH):
                for i in range(2):
                    dilated_out(RET_FILL[4 * h + i])
                for t in range(TT):
                    act.wait_ge(sem("ret_var"), 2 * h + t + 1)
                    nc.scalar.activation(bn[:, t, 8:9], bn[:, t, 8:9], ACT.Sqrt).then_inc(sem("ret_sqrt"), 1)
                for i in range(2, 4):
                    dilated_out(RET_FILL[4 * h + i])
                for half in range(2):
                    b = ready(f"rt{h}_{half}")
                    for j in range(2):
                        c = 4 * h + 2 * half + j
                        last = nc.scalar.activation(yretT[:, c, :], b[:, S * j:S * j + S], ACT.Identity,
                                                    bias=col("ret_gn_b_2", c), scale=col("ret_gn_g_2", c))
                    last.then_inc(free_of(f"rt{h}_{half}"), 1)
            for name in RET_FILL[16:]:
                dilated_out(name)
            attention(PART["a"], FILL_A)
            stream_squares("x3", "wo2_3")
            shifted(1, 24)
            for i in range(16):
                copy_out(f"f1_{i}", fl(hidT[:, 2 * i:2 * i + 2]), fn=ACT.Relu)
            stream_squares("xf", "f2_7")
            for i in range(4):
                t, half = divmod(i, 2)
                at = 512 * i
                copy_out(f"out{i}", wide[:, at:at + 512])
                act.wait_ge(*evacuated(f"out{i}"))
                act.dma_start(out[0, P * t:P * t + P, 512 * half:512 * half + 512], wide[:, at:at + 512]) \
                    .then_inc(sem("stored"), 16)
            act.wait_ge(sem("stored"), 64)

        @block.vector
        def _(dve):
            own = Steps(dve, "dve_step")
            V = nc.vector

            def ready(name):
                dve.wait_ge(proj_ready, GROUP_AT[name] + 1)
                return bank(name)

            def variance(name, width, w=512):
                n = NORM_AT[name]
                dve.wait_ge(norm_sum, n + 1)
                if n:
                    dve.wait_ge(norm_done, n)
                V.tensor_scalar(rstd[:, 0:w], st[:, 0:w], 1.0 / width, EPS, ALU.mult, ALU.add).then_inc(norm_var, 1)

            def inverse(name, w=512):
                dve.wait_ge(norm_sqrt, NORM_AT[name] + 1)
                own.did(V.reciprocal(rstd[:, 0:w], rstd[:, 0:w]))
                own.settle()

            def stream_norm(name, gain, shifted=False):
                variance(name, D, S)
                inverse(name, S)
                for k in range(KD):
                    ins = V.scalar_tensor_tensor(hT[:, k, :], xT[:, k, :], gain[:, k:k + 1], rstd[:, 0:S], ALU.mult, ALU.mult)
                    ins.then_inc(h_pre if shifted else h_ready, 1)
                V.tensor_copy(bn[:, 0, 9:10], rstd[:, 0:1]).then_inc(norm_done, 1)

            def head_norm_end(name, src, dst, gain, w=512):
                inverse(name, w)
                dve.wait_ge(*evacuated(src))
                V.scalar_tensor_tensor(dst, dst, col(gain), rstd[:, 0:w], ALU.mult, ALU.mult).then_inc(norm_done, 1)

            def sigmoid(name):
                z = SILU.index(name)
                dve.wait_ge(sem("silu_exp"), z + 1)
                t = tmp[:, z % 2]
                own.did(V.tensor_scalar(t, t, 1.0, None, ALU.add))
                own.settle()
                return t

            def silu(name, dst, other=None):
                t = sigmoid(name)
                own.did(V.reciprocal(t, t))
                own.settle()
                if other is not None:
                    own.did(V.tensor_tensor(t, t, bank(name)[:], ALU.mult))
                    own.settle()
                    V.tensor_tensor(dst, t, other, ALU.mult).then_inc(free_of(name), 1)
                else:
                    V.tensor_tensor(dst, t, bank(name)[:], ALU.mult).then_inc(free_of(name), 1)

            def score_max(u):
                part, step, br, last_br, at, qt, n = UNITS[u]
                e, s = prob[:, u % 2], stat[:, u % 2]
                dve.wait_ge(sc_ready, u + 1)
                if u >= 2:
                    dve.wait_ge(tr_ready, rounds_before(u - 1))
                if part == "a":
                    for g in range(AG):
                        ins = V.scalar_tensor_tensor(e[:, g, 0:n], sc[g // 2][:, S * (g % 2):S * (g % 2) + n], P ** -0.5,
                                                     dil_bias[:, g, at, S - n:S], ALU.mult, ALU.add)
                    ins.then_inc(sc_free, 1)
                    dve.wait_ge(sc_free, u + 1)
                    own.did(V.tensor_reduce(s[:, 0:1], e[:, 0:AG, 0:n], AX.XY, ALU.max))
                    own.settle()
                    V.tensor_scalar(s[:, 4:5], s[:, 0:1], -1.0, None, ALU.mult).then_inc(mx_ready, 1)
                    return
                for f in range(2):
                    h0 = 4 * at + f if part == "b" else 2 * at + 4 * f
                    step_h = 2 if part == "b" else 1
                    heads = slice(h0, h0 + step_h + 1, step_h)
                    if part == "c" and br == 0:
                        bias = cmp_bias[:, qt, heads, :]
                    else:
                        bias = (swa if part == "d" else alibi)[:, heads, S - n:S]
                    ins = V.tensor_tensor(e[:, 2 * f:2 * f + 2, 0:n], cut(sc[f][:], S)[:, :, 0:n], bias, ALU.add)
                ins.then_inc(sc_free, 1)
                dve.wait_ge(sc_free, u + 1)
                own.did(V.tensor_reduce(s[:, 0:4], e[:, :, 0:n], AX.X, ALU.max))
                own.settle()
                if part == "d":
                    sk = sinks8[:].rearrange("p (f b) -> p f b", f=2)[:, :, 2 * at:2 * at + 2]
                    own.did(V.tensor_tensor(cut(s[:, 0:4], 2), cut(s[:, 0:4], 2), sk, ALU.max))
                    own.settle()
                ins = V.tensor_scalar(s[:, 4:8], s[:, 0:4], -1e28, -0.125, ALU.max, ALU.mult)
                if part == "d":
                    own.did(ins)
                    own.settle()
                    sk = sinks[:].rearrange("p (f b) -> p f b", f=2)[:, :, 2 * at:2 * at + 2]
                    ins = V.tensor_tensor(cut(s[:, 16:20], 2), cut(s[:, 4:8], 2), sk, ALU.add)
                ins.then_inc(mx_ready, 1)

            def normalise(u):
                part, step, br, last_br, at, qt, n = UNITS[u]
                e, s = prob[:, u % 2], stat[:, u % 2]
                m = 1 if part == "a" else 4
                dve.wait_ge(exp_done, u + 1)
                if part == "d":
                    own.did(V.tensor_tensor(s[:, 8:12], s[:, 8:12], s[:, 16:20], ALU.add))
                    own.settle()
                own.did(V.tensor_scalar(s[:, 8:8 + m], s[:, 8:8 + m], 1e-30, None, ALU.max))
                own.settle()
                own.did(V.reciprocal(s[:, 12:12 + m], s[:, 8:8 + m]))
                own.settle()
                if part == "a":
                    V.tensor_scalar(e[:, 0:AG, 0:n], e[:, 0:AG, 0:n], s[:, 12:13], None, ALU.mult).then_inc(p_ready, 1)
                    return
                if part == "c":
                    gate = gates[:, qt, 8 * br:8 * br + 8].rearrange("p (f b) -> p f b", f=2)[:, :, 2 * at:2 * at + 2]
                    own.did(V.tensor_tensor(cut(s[:, 12:16], 2), cut(s[:, 12:16], 2), gate, ALU.mult))
                    own.settle()
                V.tensor_tensor(e[:, :, 0:n], e[:, :, 0:n], s[:, 12:16].unsqueeze(2).broadcast_to([P, 4, n]), ALU.mult) \
                    .then_inc(p_ready, 1)

            def mixed_out(u):
                part, step, br, last_br, at, qt, n = UNITS[u]
                dve.wait_ge(pv_ready, step + 1)
                if part == "a":
                    V.tensor_copy(attT[:, at, P * qt:P * qt + P], po[:, 0:P]).then_inc(po_free, 1)
                    return
                y, c = dict(b=(yT0, 4), c=(yT1, 0), d=(yT1, 4))[part]
                y = y[:, c + 2 * at:c + 2 * at + 2, P * qt:P * qt + P]
                V.tensor_tensor(y, cut(po[:, 0:S], P), y, ALU.mult).then_inc(po_free, 1)

            def attention(units, fill, done):
                score_max(units[0])
                ended = None
                for i, u in enumerate(units):
                    if i + 1 < len(units):
                        score_max(units[i + 1])
                    normalise(u)
                    for name in fill[i]:
                        done(name)
                    if ended is not None:
                        mixed_out(ended)
                    ended = u if UNITS[u][3] else None
                mixed_out(ended)

            fl = lambda ap: ap.rearrange("p k t -> p (k t)")
            b = ready("vec")
            own.did(V.tensor_copy(cols[:, 0:N_ROWS_A], b[:, 0:N_ROWS_A]))
            own.did(V.tensor_copy(cols[:, N_ROWS_A:N_ROWS_A + N_ROWS_B], b[:, 128:128 + N_ROWS_B]))
            V.tensor_copy(cut(cols[:, N_ROWS_A + N_ROWS_B:], TAPS), cut(b[:, 256:384], 32)[:, :, 0:TAPS]).then_inc(free_of("vec"), 1)
            for g in range(AG):
                b = ready(f"dl{g}")
                V.tensor_tensor(line[:, g, :], b[0:AH, 0:LINE], linemask[0:AH, g, :], ALU.add).then_inc(free_of(f"dl{g}"), 1)
            dve.wait_ge(*evacuated("dl2"))
            dve.wait_ge(*evacuated("dl1"))
            dve.wait_ge(*evacuated("dl0"))
            own.did(V.tensor_scalar(sinks8[:], sinks[:], 8.0, None, ALU.mult))
            V.tensor_copy(bn[0:AH, 1, 9:10], line[:, 0, 0:1]).then_inc(sem("line_ready"), AG)
            for i in range(4):
                b = ready(f"x{i}")
                V.tensor_copy(fl(xT[:, 2 * i:2 * i + 2]), b[:]).then_inc(free_of(f"x{i}"), 1)
            dve.wait_ge(sem("c_exp"), 1)
            own.did(V.tensor_scalar(silu_c[:], silu_c[:], 1.0, None, ALU.add))
            own.settle()
            own.did(V.reciprocal(silu_c[:], silu_c[:]))
            own.settle()
            V.tensor_tensor(silu_c[:], silu_c[:], col("c_2", 0, 8), ALU.mult).then_inc(sem("silu_c_ready"), 1)

            own.did(V.memset(hpad[:, :, 0:TAPS - 1], 0.0))
            stream_norm("x0", col("norm_g", 0, 8))
            for i in range(2):
                t = sigmoid(f"ug{i}")
                own.did(V.reciprocal(t, t))
                own.settle()
                dve.wait_ge(*evacuated(f"uv{i}"))
                V.tensor_tensor(hpad[:, 2 * i:2 * i + 2, TAPS - 1:], cut(t, S), u_val[:, 2 * i:2 * i + 2], ALU.mult) \
                    .then_inc(free_of(f"ug{i}"), 1)
            dve.wait_ge(*evacuated("ug0"))
            dve.wait_ge(*evacuated("ug1"))
            own.settle()

            def taps(lo, hi):
                for tap in range(lo, hi):
                    for c in range(4):
                        y, h = yT0[:, c, :], hpad[:, c, tap:tap + S]
                        if tap == 0:
                            own.did(V.tensor_scalar(y, h, conv_col(c, 0), col("a_conv_b", c), ALU.mult, ALU.add))
                        else:
                            dve.wait_ge(own.sem, own.n - 3)
                            ins = V.scalar_tensor_tensor(y, h, conv_col(c, tap), y, ALU.mult, ALU.add)
                            own.did(ins)

            taps(0, 7)
            for i, (name, dst, gain) in enumerate((("bq0", bqT[:, 0:2], "b_qnorm_g"), ("bq1", bqT[:, 2:4], "b_qnorm_g"),
                                                   ("bk0", bkT[:, 0:2], "b_knorm_g"), ("bk1", bkT[:, 2:4], "b_knorm_g"))):
                variance(name, HD)
                taps(7 + 6 * i, 13 + 6 * i)
                head_norm_end(name, name, fl(dst), gain)
            own.settle()
            V.tensor_copy(bn[:, 1, 9:10], yT0[:, 0, 0:1]).then_inc(sem("conv_done"), 1)

            def z_done(name):
                if name[:2] == "zb":
                    silu(name, fl(yT0[:, 4 + 2 * int(name[2]):6 + 2 * int(name[2])]))
                else:
                    silu(name, tmp[:, SILU.index(name) % 2])

            dve.wait_ge(const_in, 16 * 6)
            attention(PART["b"], FILL_B, z_done)
            dve.wait_ge(sem("ln_mean"), 1)
            own.did(V.tensor_scalar(rstd[:, 0:S], st[:, 0:S], 1.0 / GW, None, ALU.mult))
            own.settle()
            over = lambda ap: ap.unsqueeze(1).broadcast_to([P, 4, S])
            y_a = yT0[:, 0:4]
            V.tensor_tensor(y_a, y_a, over(rstd[:, 0:S]), ALU.subtract).then_inc(sem("ln_centred"), 1)
            dve.wait_ge(sem("ln_sum"), 1)
            dve.wait_ge(sem("ln_centred"), 1)
            V.tensor_scalar(rstd[:, 0:S], st[:, 0:S], 1.0 / GW, EPS, ALU.mult, ALU.add).then_inc(sem("ln_var"), 1)
            dve.wait_ge(sem("ln_sqrt"), 1)
            own.did(V.reciprocal(rstd[:, 0:S], rstd[:, 0:S]))
            own.settle()
            V.tensor_tensor(y_a, y_a, over(rstd[:, 0:S]), ALU.mult).then_inc(sem("ln_scaled"), 1)
            dve.wait_ge(sem("ln_exp"), 1)
            e = wide[:, 0:1024]
            own.did(V.tensor_scalar(e, e, 1.0, None, ALU.add))
            own.settle()
            own.did(V.reciprocal(e, e))
            own.settle()
            own.did(V.tensor_tensor(e, e, fl(y_a), ALU.mult))
            own.settle()
            dve.wait_ge(*evacuated("za0"))
            dve.wait_ge(*evacuated("za1"))
            V.tensor_tensor(fl(y_a), e, tmp[:].rearrange("p z n -> p (z n)"), ALU.mult).then_inc(sem("y_a_ready"), 1)

            def residual(names):
                for i, name in enumerate(names):
                    b = ready(name)
                    x = fl(xT[:, 2 * i:2 * i + 2])
                    V.tensor_tensor(x, b[:], x, ALU.add).then_inc(free_of(name), 1)

            residual([f"wo0_{i}" for i in range(4)])

            stream_norm("x1", col("norm_g", 8, 8))
            variance("ks", HD, S)
            dve.wait_ge(sem("pairs_in"), 64)
            for v, pos in enumerate(("c_pos_k", "c_pos_v")):
                for g in range(2):
                    src = pairs[:, v, g, :]
                    ov = bass.AP(src.tensor, src.offset, [list(src.ap[0]), [2, 16], [16, NCMP]])
                    V.tensor_tensor(blocks[:, v, :, NCMP * g:NCMP * g + NCMP], ov,
                                    col(pos, 0, 16).unsqueeze(2).broadcast_to([P, 16, NCMP]), ALU.add) \
                        .then_inc(sem("blocks_ready"), 1)
            head_norm_end("ks", "ks", ksT, "c_knorm_slc_g", S)
            variance("qc0", HD)
            head_norm_end("qc0", "qc0", fl(qcT[:, 0:2]), "c_qnorm_g")
            variance("qc1", HD)
            head_norm_end("qc1", "qc1", fl(qcT[:, 2:4]), "c_qnorm_g")
            dve.wait_ge(sem("gate_exp"), 1)
            own.did(V.tensor_scalar(gates, gates, 1.0, None, ALU.add))
            own.settle()
            own.did(V.reciprocal(gates, gates))
            variance("kw", HD, S)
            head_norm_end("kw", "kw", kwT, "c_knorm_win_g", S)
            for v in range(2):
                dve.wait_ge(sem("hid_exp"), v + 1)
                own.did(V.tensor_scalar(hid_e[:, v], hid_e[:, v], 1.0, None, ALU.add))
                own.settle()
                own.did(V.reciprocal(hid_e[:, v], hid_e[:, v]))
                own.settle()
                V.tensor_tensor(hid_x[:, v], hid_x[:, v], hid_e[:, v], ALU.mult).then_inc(sem("hid_ready"), 1)
            b = ready("vc2")
            V.tensor_tensor(vcn[0:NCMP, :], b[0:NCMP, 0:P], vb2[:].rearrange("p g d -> p (g d)"), ALU.add).then_inc(free_of("vc2"), 1)
            variance("cmp", HD, 30)
            head_norm_end("cmp", "kc2", kcn, "c_knorm_cmp_g", 30)
            variance("qd0", HD)
            head_norm_end("qd0", "qd0", fl(qdT[:, 0:2]), "d_qnorm_g")
            variance("qd1", HD)
            head_norm_end("qd1", "qd1", fl(qdT[:, 2:4]), "d_qnorm_g")
            variance("kd", HD, S)
            head_norm_end("kd", "kd", kdT, "d_knorm_g", S)

            def z_done1(name):
                c = (0 if name[1] == "c" else 4) + 2 * int(name[2])
                silu(name, fl(yT1[:, c:c + 2]))

            attention(PART["c"] + PART["d"], FILL_CD, z_done1)
            b = ready("mod")
            V.tensor_tensor(mod[:], b[:, 0:48], col("b_ada_2", 0, 48), ALU.add).then_inc(free_of("mod"), 1)
            dve.wait_ge(*evacuated("mod"))
            own.did(V.scalar_tensor_tensor(gain1[:], mod[:, 8:16], 1.0, col("norm1_g_2", 0, 8), ALU.add, ALU.mult))
            own.did(V.scalar_tensor_tensor(gain2[:], mod[:, 32:40], 1.0, col("norm2_g_2", 0, 8), ALU.add, ALU.mult))
            own.settle()
            residual([f"wo1_{i}" for i in range(4)])

            stream_norm("x2", gain1[:], shifted=True)
            both = lambda ap: ap.unsqueeze(1).broadcast_to([P, 2, S])
            for c, dst in (("rq", rqT), ("rk", rkT)):
                for h in range(RH):
                    b = ready(f"{c}{h}")
                    own.did(V.tensor_tensor(cut(tmp[:, 0], S), cut(b[:], S), both(cos_t[:]), ALU.mult))
                    own.did(V.tensor_tensor(cut(tmp[:, 1], S), cut(b[:], S), both(sin_t[:]), ALU.mult))
                    own.settle()
                    own.did(V.tensor_tensor(dst[:, 2 * h, :], tmp[:, 0, 0:S], tmp[:, 1, S:], ALU.subtract))
                    V.tensor_tensor(dst[:, 2 * h + 1, :], tmp[:, 1, 0:S], tmp[:, 0, S:], ALU.add).then_inc(free_of(f"{c}{h}"), 1)
                    dve.wait_ge(*evacuated(f"{c}{h}"))
            for h in range(RH):
                dve.wait_ge(sem("ret_scores"), h + 1)
                if h >= 2:
                    dve.wait_ge(sem("ret_out"), 2 * h - 2)
                e = prob[:, h % 2].rearrange("p i j -> p (i j)")[:, 0:LINE]
                V.tensor_tensor(e, sc[h % 2][:, 0:LINE], decay[:, h, :], ALU.mult).then_inc(sem("ret_decayed"), 1)
                for t, src in enumerate((pt, po)):
                    dve.wait_ge(sem("ret_out"), 2 * h + t + 1)
                    own.did(V.bn_stats(bn[:, t, 0:6], src[:]))
                    own.settle()
                    own.did(V.bn_aggr(bn[:, t, 6:8], bn[:, t, 0:6]))
                    own.settle()
                    V.tensor_scalar(bn[:, t, 8:9], bn[:, t, 7:8], GN_EPS, None, ALU.add).then_inc(sem("ret_var"), 1)
                for t, src in enumerate((pt, po)):
                    dve.wait_ge(sem("ret_sqrt"), 2 * h + t + 1)
                    own.did(V.reciprocal(bn[:, t, 8:9], bn[:, t, 8:9]))
                    own.settle()
                    if h >= 2 and t == 0:
                        dve.wait_ge(proj_ready, GROUP_AT[f"rt{h - 2}_1"] + 1)
                    V.tensor_scalar(ron[:, h % 2, t, :], src[:], bn[:, t, 6:7], bn[:, t, 8:9], ALU.subtract, ALU.mult) \
                        .then_inc(sem("ret_normed"), 1)
                dve.wait_ge(sem("ret_normed"), 2 * h + 2)

            def gate_done(name):
                i = int(name[2])
                if name[0:2] == "rg":
                    y = fl(yretT[:, 2 * i:2 * i + 2])
                    dve.wait_ge(*evacuated(f"rt{i // 2}_{i % 2}"))
                    silu(name, y, other=y)
                else:
                    t = sigmoid(name)
                    g = (gaT if name[1] == "a" else gbT)[:, 2 * i:2 * i + 2]
                    V.reciprocal(fl(g), t).then_inc(free_of(name), 1)

            dve.wait_ge(sem("dil_in"), 16)
            attention(PART["a"], FILL_A, gate_done)
            for i in range(4):
                b = ready(f"wr{i}")
                dve.wait_ge(*evacuated(f"ga{i}"))
                V.tensor_tensor(fl(mT[:, 2 * i:2 * i + 2]), b[:], fl(gaT[:, 2 * i:2 * i + 2]), ALU.mult).then_inc(free_of(f"wr{i}"), 1)
            for i in range(4):
                b = ready(f"wa{i}")
                dve.wait_ge(*evacuated(f"gb{i}"))
                V.tensor_tensor(tmp[:, i % 2], b[:], fl(gbT[:, 2 * i:2 * i + 2]), ALU.mult).then_inc(free_of(f"wa{i}"), 1)
                dve.wait_ge(*evacuated(f"wa{i}"))
                dve.wait_ge(*evacuated(f"wr{i}"))
                m = fl(mT[:, 2 * i:2 * i + 2])
                ins = V.tensor_tensor(m, m, tmp[:, i % 2], ALU.add)
                if i < 3:
                    own.did(ins)
                else:
                    ins.then_inc(sem("merged"), 1)

            def gated_residual(names, per, gate):
                for i, name in enumerate(names):
                    b = ready(name)
                    for j in range(per):
                        k = per * i + j
                        ins = V.scalar_tensor_tensor(xT[:, k, :], b[:, S * j:S * j + S], mod[:, gate + k:gate + k + 1], xT[:, k, :],
                                                     ALU.mult, ALU.add)
                    ins.then_inc(free_of(name), 1)

            gated_residual([f"wo2_{i}" for i in range(4)], 2, 16)
            stream_norm("x3", gain2[:], shifted=True)
            for i in range(16):
                dve.wait_ge(*evacuated(f"f1_{i}"))
                h = fl(hidT[:, 2 * i:2 * i + 2])
                V.tensor_tensor(h, h, h, ALU.mult).then_inc(sem("hid_sq"), 1)
            gated_residual([f"f2_{i}" for i in range(8)], 1, 40)
            stream_norm("xf", col("norm_f_g_2", 0, 8))


def shape_constants():
    f = np.float32
    p = np.arange(P)
    both = (p[:, None] // HD == p[None, :] // HD).astype(f)
    slopes = np.power(2.0, -8.0 * np.arange(1, NH + 1) / NH).astype(f)
    dist = (P + p[:, None] - np.arange(S)[None, :]).astype(f)
    lin = -8.0 * slopes[None, :, None] * dist[:, None, :]
    alibi = np.where(dist[:, None, :] >= 0, lin, -1e30).astype(f)
    swa = np.where((dist[:, None, :] >= 0) & (dist[:, None, :] < 128), lin, -1e30).astype(f)
    t = (np.arange(2)[None, :] * P + p[:, None])[:, :, None, None]
    dc = (t - (16 * np.arange(NCMP) + 31)).astype(f)
    cmp_bias = np.where(dc >= 0, -8.0 * slopes[None, None, :, None] * dc, -1e30).astype(f)
    log_g = np.log1p(-(f(2.0) ** (-5.0 - np.arange(RH, dtype=f)))).astype(f)
    i = np.arange(LINE)
    j = np.where(i < S, 0, P)[None, :] + p[:, None]
    rel = (np.where(i < S, i, i - P)[None, :] - j).astype(f)
    decay = np.where(rel[:, None, :] >= 0, np.exp(log_g[None, :, None] * np.maximum(rel, 0)[:, None, :]), 0) / 16
    inv = f(10000.0) ** (-np.arange(P, dtype=f) / f(P))
    ang = np.arange(S, dtype=f)[None, :] * inv.astype(f)[:, None]
    d = 255 - np.arange(LINE)
    onehot = np.zeros((32, AG, LINE), f)
    mask = np.full((AH, AG, LINE), -1e30, f)
    for g, (win, dil) in enumerate(((128, 1), (512, 4), (2048, 16))):
        ok = (d >= 0) & (d <= win) & (d % dil == 0)
        dd = np.maximum(d, 1).astype(f)
        large = 16 + (np.log(dd / f(16)) / f(np.log(2048 / 16)) * f(16)).astype(np.int32)
        bucket = np.where(d < 16, d, np.minimum(large, 31))
        for u in np.nonzero(ok)[0]:
            onehot[bucket[u], g, u] = 1
            mask[:, g, u] = 0
    return dict(ident=np.eye(P, dtype=f), ones=np.ones((P, P), f), halves=both, alibi=alibi, swa=swa, cmp_bias=cmp_bias,
                decay=decay.astype(f), cos=np.cos(ang).astype(f), sin=np.sin(ang).astype(f), onehot=onehot, linemask=mask)


INPUTS = ("x norm_g w_out e_w_in a_conv_w a_conv_b a_ln_g a_ln_b b_qnorm_g b_knorm_g o_w_in c_qnorm_g c_knorm_cmp_g "
          "c_knorm_slc_g c_knorm_win_g c_pos_k c_pos_v c_k_w1 c_k_b1 c_k_w2 c_k_b2 c_v_w1 c_v_b1 c_v_w2 c_v_b2 d_qnorm_g "
          "d_knorm_g d_sinks c_2 w_ada_2 b_ada_2 norm1_g_2 w_in_2 rel_bias_2 ret_gn_g_2 ret_gn_b_2 w_ret_out_2 "
          "w_att_out_2 w_o_2 norm2_g_2 w_ff1_2 w_ff2_2 norm_f_g_2").split()


def kernel(**inputs):
    import concourse.bacc as bacc
    from concourse.bass_utils import run_bass_kernel_spmd as run

    nc = bacc.Bacc("TRN2", target_bir_lowering=False, num_devices=1)
    arrays = {n: np.ascontiguousarray(inputs[n]) for n in INPUTS}
    arrays.update(shape_constants())
    arrays = {f"in_{n}": v for n, v in arrays.items()}
    aps = {n[3:]: nc.dram_tensor(n, v.shape, mybir.dt.from_np(v.dtype), kind="ExternalInput").ap() for n, v in arrays.items()}
    out = nc.dram_tensor("y", (1, S, D), F32, kind="ExternalOutput").ap()
    mixer_kernel(nc, aps, out)
    return run(nc, [arrays], core_ids=[0]).results[0]["y"]
```

```python
import numpy as np
import concourse.bass as bass
from concourse import mybir
from contextlib import ExitStack

F32 = mybir.dt.float32
F32R = mybir.dt.float32r
ALU = mybir.AluOpType
ACT = mybir.ActivationFunctionType
AX = mybir.AxisListType

P = 128
S = 256
TT = S // P
D = 1024
KD = D // P
GW = 512
HD = 64
NH = 8
TAPS = 31
NCMP = 15
RH, RDK, RDV = 4, 256, 512
AG, AH = 3, 4
EPS = 1e-6
GN_EPS = 1e-5
LINE = 384
UNIT = 2048
NRAW = 4
NHI = 3
NPP = 3
PADW = S + TAPS - 1
ADA = 6 * D // P
ADA_DVE = 30
ADA_FIRST = 8
ADA_POOL = dict(zb0=1, zb1=1, za0=1, za1=1, gt=6, qd0=1, zc0=1, qd1=1, kdvd=1, zc1=1, zd0=1, zd1=2)
CONV_DVE = 22
ARENA = 18568


EV = dict(uv=0, ug=512, za=1024, bq=1536, bk=2048, bv=2560, zb=3072)
OD = dict(qc=0, zc=1304, qd=1816, zd=2584)
OD_ONE = dict(kcvc=(512, 256), ksvs=(768, 256), kwvw=(1024, 256), gt=(1280, 24), kdvd=(2328, 256))
IN2 = dict(rq=0, rk=1024, rv=2048, rg=4096, ga=10752, gb=11776)
IN2_ATT = 6144
PAIRED = ("qc0", "qc1", "qd0", "qd1", "zc0", "zc1", "zd0", "zd1")

RET_FILL = [f"a{n}{g}_{i}" for g in range(AG) for n in "qk" for i in range(2)] + \
    [f"av{g}_{i}" for g in range(AG) for i in range(2)]
FILL_B = [["zb0"], ["zb1"], ["za0", "L:mean"], ["za1", "L:sq"]]
FILL_CD = [["zc0"], ["qd1", "S:qd0"], ["kd", "S:qd1"], ["vd", "S:kd"], ["zc1"], ["zd0"], ["zd1"], [], [], [], [], [],
           ["M:0"], ["M:1"], ["M:2"], ["M:3"]]
GATED = [f"rg{i}" for i in range(8)] + [f"ga{i}" for i in range(4)] + [f"gb{i}" for i in range(4)]
FILL_A = [GATED[2 * i:2 * i + 2] for i in range(8)]


def fills_of(fill):
    out = [x for items in fill for x in items if x[:2] not in ("S:", "L:", "M:")]
    return out + ["mod"] * any(x[:2] == "M:" for items in fill for x in items)


def group_plan():
    own = lambda names: [(n, [n]) for n in names]
    out = own(["uv0", "uv1", "ug0", "ug1", "bq0", "bq1", "bk0", "bk1"]) + [("conv0", []), ("conv1", [])]
    out += own(["bv0", "bv1"]) + own(fills_of(FILL_B))
    out += own([f"wo0_{i}" for i in range(4)])
    out += [("kcvc", ["kcvc"]), ("ks", ["ksvs"]), ("vs", ["ksvs"])] + own(["qc0", "qc1"])
    out += [("kw", ["kwvw"]), ("vw", ["kwvw"]), ("gt", ["gt"]), ("hidk", ["ck0", "ck1"]), ("hidv", ["cv0", "cv1"]),
            ("kc2", []), ("vc2", []), ("qd0", ["qd0"])]
    out += [(n, [] if n == "mod" else ["kdvd"] if n in ("kd", "vd") else [n]) for n in fills_of(FILL_CD)]
    out += own([f"wo1_{i}" for i in range(4)])
    out += own([f"rq{i}" for i in range(4)] + [f"rk{i}" for i in range(4)] + [f"rv{i}" for i in range(8)])
    out += [(f"dl{g}", []) for g in range(AG)]
    for h in range(RH):
        out += own(RET_FILL[4 * h:4 * h + 4]) + [(f"rt{h}_0", []), (f"rt{h}_1", [])]
    out += own(RET_FILL[16:]) + own(GATED)
    out += [(f"wr{i}", [f"wr{i}a", f"wr{i}b"]) for i in range(4)] + [(f"wa{i}", [f"wa{i // 2}"]) for i in range(4)]
    out += own([f"wo2_{i}" for i in range(4)] + [f"f1_{i}" for i in range(16)])
    out += [(f"f2_{i}", [f"f2_{i}a", f"f2_{i}b"]) for i in range(8)]
    return out


PLAN = group_plan()
GROUPS = [g for g, _ in PLAN]
GROUP_AT = {n: i for i, n in enumerate(GROUPS)}
UNITS_OF = dict(PLAN)
WEIGHTS = list(dict.fromkeys(u for _, us in PLAN for u in us))
WEIGHT_AT = {n: i for i, n in enumerate(WEIGHTS)}
LAST_READ = {u: max(i for i, (_, us) in enumerate(PLAN) if u in us) for u in WEIGHTS}
SPLIT = [u for u in WEIGHTS if u[:2] not in ("ck", "cv")]
SPLIT_AT = {n: i for i, n in enumerate(SPLIT)}


def unit_shape(u):
    if u in OD_ONE:
        return 8, OD_ONE[u][1]
    if u[:2] in ("ck", "cv", "wr", "f2"):
        return 16, 128
    return (4, 512) if u[:2] == "wa" else (8, 256)


def take_slots(units, slots, more, start):
    at, before, last = [], [], {}
    for n in range(len(units)):
        free = list(range(slots + (more if n >= units.index(start) else 0)))
        at.append(min(free, key=lambda x: last.get(x, -1)))
        before.append(last.get(at[-1]))
        last[at[-1]] = n
    return at, before


RAW_AT, RAW_BEFORE = take_slots(WEIGHTS, NRAW, 2, "wr2a")
HI_AT, HI_BEFORE = take_slots(SPLIT, NHI, 2, "wr1b")


def raw_target(n):
    return 16 * RAW_AT[:n + 1].count(RAW_AT[n])


ADA_NAMES = [f"ada{j}" for j in range(ADA_DVE)]
SLAB_AT, SLAB_BEFORE = take_slots(ADA_NAMES, 3, 2, f"ada{ADA_FIRST}")


def ada_sends():
    k = WEIGHT_AT["kcvc"]
    out = {2: [0, 1, 2], 4: [3, 4], 6: [5, 6], 8: [7], k + 1: [8, 9, 10, 11, 12]}
    for i in range((ADA_DVE - 13 + 1) // 2):
        out[k + 5 + i] = [j for j in (13 + 2 * i, 14 + 2 * i) if j < ADA_DVE]
    return out


HALF = ("b_qnorm_g", "b_knorm_g", "c_qnorm_g", "c_knorm_cmp_g", "c_knorm_slc_g", "c_knorm_win_g",
        "d_qnorm_g", "d_knorm_g", "c_k_b2")
FULL = (("norm_g", 16), ("c_2", 8), ("a_conv_b", 4), ("a_ln_g", 4), ("a_ln_b", 4), ("norm1_g_2", 8), ("norm2_g_2", 8),
        ("norm_f_g_2", 8), ("c_k_b1", 2), ("c_v_b1", 2), ("c_pos_k", 16), ("c_pos_v", 16), ("ret_gn_g_2", 16),
        ("ret_gn_b_2", 16), ("b_ada_2", 48))
COL_AT, CONV_AT = {}, 0
for _name, _c in FULL + tuple((n, 1) for n in HALF):
    COL_AT[_name] = CONV_AT, _c
    CONV_AT += _c


def attention_units():
    out, step = [], 0
    for bp in range(2):
        for qt in range(2):
            out.append(("b", step, 0, True, bp, qt, P * (qt + 1)))
            step += 1
    for bp in range(2):
        for qt in range(2):
            for br in (1, 2, 0):
                out.append(("c", step, br, br == 0, bp, qt, NCMP if br == 0 else P * (qt + 1)))
            step += 1
    for bp in range(2):
        for qt in range(2):
            out.append(("d", step, 0, True, bp, qt, P * (qt + 1)))
            step += 1
    for hh in range(AH):
        for qt in range(2):
            out.append(("a", step, 0, True, hh, qt, P * (qt + 1)))
            step += 1
    return out


UNITS = attention_units()


def key_tiles(u):
    return -(-UNITS[u][6] // P)


def rounds_before(u):
    return sum(key_tiles(i) for i in range(u))


PART = {p: [u for u in range(len(UNITS)) if UNITS[u][0] == p] for p in "bcda"}
STEPS_TO = {p: UNITS[PART[p][-1]][1] + 1 for p in "bcda"}

NORMS = ["x0", "bq0", "bq1", "bk0", "bk1", "x1", "ks", "qc0", "qc1", "kw", "cmp", "qd0", "qd1", "kd", "x2", "x3", "xf"]
NORM_AT = {n: i for i, n in enumerate(NORMS)}
STREAM = {n: i for i, n in enumerate(n for n in NORMS if n[0] == "x")}
Q_NORMS = ("bq0", "bq1", "qc0", "qc1", "qd0", "qd1")
Q_GAIN = dict(b="b_qnorm_g", c="c_qnorm_g", d="d_qnorm_g")
NORM_W = dict(ks=S, kw=S, kd=S, cmp=2 * NCMP)


def mixer_kernel(nc, a, out):
    ctx = ExitStack()
    with ctx:
        sems = {}

        def sem(name):
            if name not in sems:
                sems[name] = ctx.enter_context(nc.semaphore(name))
            return sems[name]

        def sb(name, shape, dt=F32):
            return ctx.enter_context(nc.sbuf_tensor(name, shape, dt))

        def over(name, under, at, shape):
            return nc.alloc_sbuf_tensor_at(name, shape, F32R, offset=nc.lookup_mloc(under).addr + 4 * at)

        def cut(ap, n):
            return ap.rearrange("p (k n) -> p k n", n=n)

        def fl(ap):
            return ap.rearrange("p k t -> p (k t)")

        raw = sb("raw", [P, NRAW, UNIT])
        w_lo = over("w_lo", raw, 0, [P, NRAW, UNIT])
        w_hi = sb("w_hi", [P, NHI, UNIT], F32R)
        xT = sb("xT", [P, KD, S])
        parts = sb("parts", [P, 2, KD, S], F32R)
        wide = sb("wide", [P, KD * S])
        ident = sb("ident", [P, P])
        ones = sb("ones", [P, P])
        halves = sb("halves", [P, P])
        cols = sb("cols", [P, CONV_AT + 4 * TAPS])
        silu_c = sb("silu_c", [P, KD])
        mod = sb("mod", [P, ADA])
        gain1 = sb("gain1", [P, KD])
        gain2 = sb("gain2", [P, KD])
        sinks = sb("sinks", [P, NH])
        cmp_bias = sb("cmp_bias", [P, 2, NH, NCMP])
        cos_t = sb("cos_t", [P, S])
        sin_t = sb("sin_t", [P, S])
        dil_bias = sb("dil_bias", [P, AG, AH, S])
        prob2 = sb("prob2", [P, 2, 4, S])
        probT = sb("probT", [P, 2560])
        sq = sb("sq", [P, 512])
        rstd = sb("rstd", [P, 512])
        q_rstd = sb("q_rstd", [P, 3, 2, 8])
        stat = sb("stat", [P, 3, 20])
        bn = sb("bn", [P, 2, 10])
        tmp = sb("tmp", [P, 2, 512])
        rel = sb("rel", [32, AG * AH])
        vb2 = sb("vb2", [NCMP, 2, HD])
        kw2 = sb("kw2", [P, 2, 2, HD])
        vw2 = sb("vw2", [P, 2, HD])
        arena = sb("arena", [P, ARENA])

        def place(at, *shape):
            n = int(np.prod(shape))
            assert at + n <= ARENA
            v = arena[:, at:at + n]
            if len(shape) == 2:
                return cut(v, shape[1])
            if len(shape) == 3:
                return v.rearrange("p (a b c) -> p a b c", b=shape[1], c=shape[2])
            return v

        alibi = place(0, NH, S)
        swa = place(2048, NH, S)
        ada_acc = place(4096, 6 * D)
        ada_slab = place(10240, 2, KD, P)
        L = 12288
        bqT, bkT, bv = place(L, 4, S), place(L + 1024, 4, S), place(L + 2048, 2, GW)
        hpad = place(L + 3072, 4, PADW)
        yT0 = place(L + 4232, KD, S)
        u_val = cut(wide[:, 0:1024], S)
        slabs = [cut(dil_bias[:].rearrange("p g h j -> p (g h j)")[:, KD * P * i:KD * P * i + KD * P], P)
                 for i in range(3)] + [cut(fl(prob2[:, i]), P) for i in range(2)]
        diags = [fl(prob2[:, i // 8])[:, P * (i % 8):P * (i % 8) + P] if i < 16 else probT[:, P * (i - 16):P * (i - 15)]
                 for i in range(4 * (TAPS - CONV_DVE))]
        qcT, qdT = place(L, 4, S), place(L + 1024, 4, S)
        ksT, kwT, kdT = place(L + 2048, S), place(L + 2304, S), place(L + 2560, S)
        vs, vw, vd = place(L + 2816, 2, P), place(L + 3072, 2, P), place(L + 3328, 2, P)
        gates = place(L + 3584, 2, 24)
        kcn = place(L + 3632, 2 * NCMP)
        vcn = place(L + 3664, P)
        yT1 = place(L + 4232, KD, S)
        kcv = cut(wide[:, 0:512], S)
        pairs = wide[:, 512:1536].rearrange("p (v g t) -> p v g t", v=2, g=2)
        blocks = probT[:, 0:960].rearrange("p (v j n) -> p v j n", v=2, j=16)
        hid_x = probT[:, 960:1080].rearrange("p (v k n) -> p v k n", v=2, k=2)
        yretT = place(0, 16, S)
        rqT, rkT, rv = place(4096, 8, S), place(6144, 8, S), place(8192, 2, RH * RDV)
        av = place(4096, AG, 2, GW)
        gaT, gbT = place(8192, 8, S), place(10240, 8, S)
        aqT, akT = place(12288, AG, AH * S), place(15360, AG, AH * S)
        mT = place(4096, 8, S)
        line = dil_bias[0:AH].rearrange("p g h j -> p (g h j)")[:, 0:AG * LINE].rearrange("p (g u) -> p g u", g=AG)
        linemask = dil_bias[0:AH].rearrange("p g h j -> p (g h j)")[:, AG * LINE:2 * AG * LINE].rearrange("p (g u) -> p g u", g=AG)
        onehot = prob2[0:32].rearrange("p i j t -> p (i j t)")[:, 0:AG * LINE].rearrange("p (g u) -> p g u", g=AG)
        ron = cut(probT[:, 0:1024], GW)
        decay = cut(probT[:, 1024:2560], LINE)
        yret_hi = parts[:].rearrange("p h k t -> p (h k) t")
        yret_lo = over("yret_lo", arena, 12288, [P, 16, S])
        att_hi = over("att_hi", arena, 7168, [P, AH, S])
        att_lo = over("att_lo", wide, 1024, [P, AH, S])
        hid_hi = over("hid_hi", arena, 0, [P, 32, S])
        hid_lo = over("hid_lo", arena, 8192, [P, 32, S])

        raw_slots = [raw[:, i] for i in range(NRAW)] + [arena[:, 16384:16384 + UNIT], probT[:, 0:UNIT]]
        lo_slots = [w_lo[:, i] for i in range(NRAW)] + \
            [over("w_lo_a", arena, 16384, [P, UNIT])[:], over("w_lo_b", probT, 0, [P, UNIT])[:]]
        hi_slots = [w_hi[:, i] for i in range(NHI)] + \
            [over("w_hi_a", prob2, 0, [P, UNIT])[:], over("w_hi_b", dil_bias, 0, [P, UNIT])[:]]

        def prob(u):
            return cut(wide[:, 0:1024], S) if u % 3 == 2 else prob2[:, u % 3]

        def pT(u, br, r):
            if UNITS[u][0] == "c":
                at = 0 if br == 0 else 512 + 1024 * (br - 1) + 512 * r
            else:
                at = 512 + 1024 * (u % 2) + 512 * r
            return cut(probT[:, at:at + 512], P)

        pp = [ctx.enter_context(nc.psum_tensor(f"proj{i}", [P, 512], F32)) for i in range(NPP)]
        st = ctx.enter_context(nc.psum_tensor("sums", [P, 512], F32))
        sc = [ctx.enter_context(nc.psum_tensor(f"scores{i}", [P, 512], F32)) for i in range(2)]
        pt = ctx.enter_context(nc.psum_tensor("transposed", [P, 512], F32))
        po = ctx.enter_context(nc.psum_tensor("mixed", [P, 512], F32))
        lines_d = nc.dram_tensor("dil_lines", (AG * AH, P, LINE), F32, kind="Internal").ap()

        raw_in = [sem(f"raw_in{i}") for i in range(NRAW + 2)]
        hi_ready, lo_ready = sem("hi_ready"), sem("lo_ready")
        bank_free = [sem(f"bank_free{i}") for i in range(NPP)]
        proj_ready = sem("proj_ready")
        first_in, setup_in = sem("first_in"), sem("setup_in")
        x_in = [sem("x_in0"), sem("x_in1")]
        const_in, rot_in = sem("const_in"), sem("rot_in")
        h_full, h_hi, h_ready = sem("h_full"), sem("h_hi"), sem("h_ready")
        stream_sq = sem("stream_sq")
        norm_sq, norm_sum = sem("norm_sq"), sem("norm_sum")
        norm_var, norm_sqrt, norm_done = sem("norm_var"), sem("norm_sqrt"), sem("norm_done")
        sc_ready, sc_free = sem("sc_ready"), sem("sc_free")
        mx_ready, exp_done, p_ready = sem("mx_ready"), sem("exp_done"), sem("p_ready")
        tr_ready, pt_ready = sem("tr_ready"), sem("pt_ready")
        pv_ready, po_free = sem("pv_ready"), sem("po_free")
        y_hi, y_ready = sem("y_hi"), sem("y_ready")

        N_SETUP = 9

        def col(name, k=0, n=1):
            return cols[:, COL_AT[name][0] + k:COL_AT[name][0] + k + n]

        def conv_col(c, tap):
            at = CONV_AT + c * TAPS + tap
            return cols[:, at:at + 1]

        def bank(name):
            return pp[GROUP_AT[name] % NPP]

        def evacuated(name):
            m = GROUP_AT[name]
            return bank_free[m % NPP], m // NPP + 1

        def free_of(name):
            return bank_free[GROUP_AT[name] % NPP]

        def norms_before(name):
            return sum(n not in STREAM for n in NORMS[:NORM_AT[name]])

        def rstd_of(name):
            return q_rstd[:, dict(b=0, c=1, d=2)[name[1] if name[0] == "q" else "b"], int(name[2])]

        class Steps:

            def __init__(self, eng, name):
                self.eng, self.sem, self.n = eng, sem(name), 0

            def did(self, ins):
                ins.then_inc(self.sem, 1)
                self.n += 1

            def settle(self):
                self.eng.wait_ge(self.sem, self.n)

        block = ctx.enter_context(nc.Block())

        @block.sync
        def _(sp):
            for i in range(2):
                sp.dma_start(xT[:, 4 * i:4 * i + 4], cut(a["x"], S)[:, 4 * i:4 * i + 4]).then_inc(x_in[i], 16)
            sends = ada_sends()
            for n, u in enumerate(WEIGHTS):
                before = RAW_BEFORE[n]
                if before is not None:
                    sp.wait_ge(proj_ready, LAST_READ[WEIGHTS[before]] + 1)
                elif n >= NRAW:
                    sp.wait_ge(po_free, STEPS_TO["a"])
                size = int(np.prod(unit_shape(u)))
                sp.dma_start(raw_slots[RAW_AT[n]][:, 0:size], a["weights"][n][:, 0:size]).then_inc(raw_in[RAW_AT[n]], 16)
                for j in sends.get(n, []):
                    if SLAB_BEFORE[j] is not None:
                        sp.wait_ge(sem("ada_dve"), SLAB_BEFORE[j] + 1)
                    elif j >= ADA_FIRST:
                        sp.wait_ge(tr_ready, rounds_before(PART["c"][0]))
                    sp.dma_start(slabs[SLAB_AT[j]], a["w_ada"][ADA - ADA_DVE + j].rearrange("p (k n) -> p k n", n=P)) \
                        .then_inc(sem(f"slab_in{SLAB_AT[j]}"), 16)
                if u == "bq1":
                    sp.dma_start(alibi, a["alibi"]).then_inc(const_in, 16)
                if u == "bv1":
                    for dst, src in ((cmp_bias[:], a["cmp_bias"]), (swa, a["swa"])):
                        sp.dma_start(dst, src).then_inc(const_in, 16)
                if u == "wo0_0":
                    for dst, src in ((cos_t[:], a["cos"]), (sin_t[:], a["sin"])):
                        sp.dma_start(dst, src).then_inc(rot_in, 16)
                if u == "rq3":
                    sp.wait_ge(po_free, STEPS_TO["d"])
                    sp.dma_start(decay, a["decay"]).then_inc(sem("decay_in"), 16)
                    sp.dma_start(onehot, a["onehot"]).then_inc(sem("line_const_in"), 16)
                    sp.wait_ge(sem("ada_dve"), ADA_DVE)
                    sp.dma_start(linemask, a["linemask"]).then_inc(sem("line_const_in"), 16)
                if u == RET_FILL[6]:
                    sp.wait_ge(sem("line_ready"), 1)
                    for g in range(AG):
                        sp.dma_start(lines_d[AH * g:AH * g + AH], line[:, g, :].unsqueeze(1).broadcast_to([AH, P, LINE])) \
                            .then_inc(sem("lines_out"), 16)
                if u == RET_FILL[8]:
                    sp.wait_ge(sem("lines_out"), 16 * AG)
                    flat = lines_d.rearrange("h r u -> (h r u)")
                    skew = bass.AP(flat.tensor, P - 1, [[LINE - 1, P], [P * LINE, AG * AH], [1, S]])
                    sp.dma_start(dil_bias[:].rearrange("p g h j -> p (g h) j"), skew).then_inc(sem("dil_in"), 16)

        @block.gpsimd
        def _(pool):
            ada_in = [sem("ada_in0"), sem("ada_in1")]
            own = Steps(pool, "pool_step")
            state = dict(ada=0)
            n_ada = ADA - ADA_DVE

            def low(u):
                n, m = WEIGHT_AT[u], SPLIT_AT[u]
                kt, w = unit_shape(u)
                pool.wait_ge(hi_ready, m + 1)
                nc.gpsimd.tensor_tensor(lo_slots[RAW_AT[n]][:, 0:kt * w], raw_slots[RAW_AT[n]][:, 0:kt * w],
                                        hi_slots[HI_AT[m]][:, 0:kt * w].bitcast(F32), ALU.subtract).then_inc(lo_ready, 1)

            def ada_block():
                j = state["ada"]
                state["ada"] += 1
                w = ada_slab[:, j % 2]
                pool.wait_ge(ada_in[j % 2], 16 * (j // 2 + 1))
                own.did(nc.gpsimd.tensor_tensor(w, w, silu_c[:].unsqueeze(2).broadcast_to([P, KD, P]), ALU.mult))
                own.settle()
                for half in (4, 2):
                    own.did(nc.gpsimd.tensor_tensor(w[:, 0:half], w[:, 0:half], w[:, half:2 * half], ALU.add))
                    own.settle()
                nc.gpsimd.tensor_tensor(ada_acc[:, P * j:P * j + P], w[:, 0], w[:, 1], ALU.add).then_inc(sem("ada_sum"), 1)
                if j + 2 < n_ada:
                    pool.wait_ge(sem("ada_sum"), j + 1)
                    load(j + 2)

            def load(j):
                pool.dma_start(ada_slab[:, j % 2], cut(a["w_ada"][j], P)).then_inc(ada_in[j % 2], 16)

            assert sum(ADA_POOL.values()) == n_ada
            for u in SPLIT:
                low(u)
                if u == "bv0":
                    pool.wait_ge(sem("silu_c_ready"), 1)
                    load(0)
                    load(1)
                for _ in range(ADA_POOL.get(u, 0)):
                    ada_block()

        @block.tensor
        def _(pe):
            state = dict(filled=0, norm=0, head=0, stream=0)

            def begin(name):
                m = state["filled"]
                assert GROUPS[m] == name, (GROUPS[m], name)
                if m >= NPP:
                    pe.wait_ge(bank_free[m % NPP], m // NPP)
                return pp[m % NPP]

            def end(last):
                last.then_inc(proj_ready, 1)
                state["filled"] += 1

            def weight(u):
                n, m = WEIGHT_AT[u], SPLIT_AT[u]
                kt, w = unit_shape(u)
                pe.wait_ge(lo_ready, m + 1)
                return cut(hi_slots[HI_AT[m]][:, 0:kt * w], w), cut(lo_slots[RAW_AT[n]][:, 0:kt * w], w)

            def features(name, hi, lo, chunks, wait=None):
                b = begin(name)
                for j, pieces in enumerate(chunks):
                    todo = []
                    for u, c, k0 in pieces:
                        whi, wlo = weight(u)
                        todo += [(whi[:, k, c:c + P], wlo[:, k, c:c + P], k0 + k) for k in range(unit_shape(u)[0])]
                    for i, (whi, wlo, k) in enumerate(todo):
                        if wait is not None and j == 0:
                            wait(k)
                        dst = b[:, S * j:S * j + S]
                        nc.tensor.matmul(dst, whi, hi[:, k, :], start=i == 0, stop=False)
                        nc.tensor.matmul(dst, whi, lo[:, k, :], start=False, stop=False)
                        last = nc.tensor.matmul(dst, wlo, hi[:, k, :], start=False, stop=i == len(todo) - 1)
                end(last)

            h_parts = parts[:, 0], parts[:, 1]

            def project(name, fresh=None):
                wait = None if fresh is None else lambda k: pe.wait_ge(h_ready, KD * fresh + k + 1)
                u = UNITS_OF[name][0]
                one = name in ("ks", "kw", "kd")
                features(name, *h_parts, [[(u, P * j, 0)] for j in range(1 if one else 2)], wait)

            def tokens(name, c, n):
                b = begin(name)
                whi, wlo = weight(UNITS_OF[name][0])
                for t in range(TT):
                    for k in range(KD):
                        dst, at = b[:, S * t:S * t + n], slice(P * t, P * t + P)
                        nc.tensor.matmul(dst, parts[:, 0, k, at], whi[:, k, c:c + n], start=k == 0, stop=False)
                        nc.tensor.matmul(dst, parts[:, 0, k, at], wlo[:, k, c:c + n], start=False, stop=False)
                        last = nc.tensor.matmul(dst, parts[:, 1, k, at], whi[:, k, c:c + n], start=False, stop=k == KD - 1)
                end(last)

            def stream_sums(name, lo, hi):
                n = NORM_AT[name]
                assert n == state["norm"]
                for k in range(lo, hi):
                    pe.wait_ge(stream_sq, KD * STREAM[name] + k + 1)
                    if k == 0 and n:
                        pe.wait_ge(norm_var, n)
                    last = nc.tensor.matmul(st[:, 0:S], ones[:], wide[:, S * k:S * k + S], start=k == 0, stop=k == KD - 1)
                if hi == KD:
                    last.then_inc(norm_sum, 1)
                    state["norm"] += 1

            def head_sums(name):
                n, w = NORM_AT[name], NORM_W.get(name, 512)
                assert n == state["norm"]
                state["norm"] += 1
                pe.wait_ge(norm_sq, norms_before(name) + 1)
                pe.wait_ge(norm_var, n)
                if name in Q_NORMS:
                    for i in range(4):
                        t, c = divmod(i, 2)
                        last = nc.tensor.matmul(st[:, 2 * i:2 * i + 2], sq[:, S * c + P * t:S * c + P * t + P],
                                                cut(halves[:], HD)[:, :, 0], start=True, stop=True)
                    last.then_inc(norm_sum, 1)
                else:
                    nc.tensor.matmul(st[:, 0:w], halves[:], sq[:, 0:w], start=True, stop=True).then_inc(norm_sum, 1)

            def scores(u):
                part, step, br, last_br, at, qt, n = UNITS[u]
                if part in "cd" and (u == 0 or UNITS[u - 1][0] != part or br == 0):
                    pe.wait_ge(norm_done, NORM_AT["kd" if part == "d" else "cmp" if br == 0 else "kw"] + 1)
                if u:
                    pe.wait_ge(sc_free, u)
                if part == "a":
                    for g in range(AG):
                        q = aqT[:, g, S * at + P * qt:S * at + P * qt + P]
                        last = nc.tensor.matmul(sc[g // 2][:, S * (g % 2):S * (g % 2) + n], q,
                                                akT[:, g, S * at:S * at + n], start=True, stop=True)
                else:
                    q = dict(b=bqT, c=qcT, d=qdT)[part]
                    for bi in range(2):
                        for f in range(2):
                            lo, b = HD * f, 2 * at + bi
                            if part == "b":
                                keys = bkT[lo:lo + HD, b, 0:n]
                            elif part == "c" and br == 0:
                                keys = kcn[lo:lo + HD, NCMP * f:NCMP * f + n]
                            else:
                                keys = (kdT if part == "d" else (None, ksT, kwT)[br])[lo:lo + HD, 0:n]
                            last = nc.tensor.matmul(sc[f][:, S * bi:S * bi + n], q[lo:lo + HD, b, P * qt:P * qt + P],
                                                    keys, start=True, stop=True)
                last.then_inc(sc_ready, 1)

            def transposes(u, r):
                part, step, br, last_br, at, qt, n = UNITS[u]
                if r == 0:
                    pe.wait_ge(p_ready, u + 1)
                if rounds_before(u) + r:
                    pe.wait_ge(pt_ready, rounds_before(u) + r)
                for i in range(3 if part == "a" else 4):
                    w = min(n - P * r, P)
                    last = nc.tensor.transpose(pt[0:w, P * i:P * i + P], prob(u)[:, i, P * r:P * r + w], ident[:])
                last.then_inc(tr_ready, 1)

            def mix(u):
                part, step, br, last_br, at, qt, n = UNITS[u]
                pe.wait_ge(pt_ready, rounds_before(u + 1))
                if step:
                    pe.wait_ge(po_free, step)
                if part == "a":
                    todo = [(g, r) for g in range(AG) for r in range(qt + 1)]
                    for i, (g, r) in enumerate(todo):
                        last = nc.tensor.matmul(po[:, 0:P], av[:, g, r, P * at:P * at + P], pT(u, 0, r)[:, g, :],
                                                start=i == 0, stop=i == len(todo) - 1)
                else:
                    for bi in range(2):
                        for f in range(2):
                            b, i4 = 2 * at + bi, 2 * f + bi
                            todo = []
                            for r in range(qt + 1):
                                if part == "b":
                                    h = 2 * b + f
                                    todo.append((bv[:, r, HD * h:HD * h + HD], pT(u, 0, r)[:, i4, :]))
                                elif part == "d":
                                    todo.append((vd[:, r, HD * f:HD * f + HD], pT(u, 0, r)[:, i4, :]))
                                else:
                                    todo += [(v[:, r, HD * f:HD * f + HD], pT(u, x, r)[:, i4, :]) for x, v in ((1, vs), (2, vw))]
                            if part == "c":
                                todo.append((vcn[0:NCMP, HD * f:HD * f + HD], pT(u, 0, 0)[0:NCMP, i4, :]))
                            for i, (v, p) in enumerate(todo):
                                last = nc.tensor.matmul(po[HD * f:HD * f + HD, P * bi:P * bi + P], v, p,
                                                        start=i == 0, stop=i == len(todo) - 1)
                last.then_inc(pv_ready, 1)

            def token_sums(chunks, done):
                for c in range(4):
                    last = nc.tensor.matmul(st[:, 0:S], ones[:], chunks[:, c, :], start=c == 0, stop=c == 3)
                last.then_inc(sem(done), 1)

            def convolution(i):
                b = begin(f"conv{i}")
                for j in range(2):
                    c = 2 * i + j
                    for k in range(TAPS - CONV_DVE):
                        tap = CONV_DVE + k
                        last = nc.tensor.matmul(b[:, S * j:S * j + S], diags[4 * k + c], hpad[:, c, tap:tap + S],
                                                start=k == 0, stop=tap == TAPS - 1)
                end(last)

            def between(name):
                if name[:2] == "S:":
                    head_sums(name[2:])
                elif name[:2] == "M:":
                    modulation(int(name[2:]))
                elif name == "L:mean":
                    pe.wait_ge(sem("conv_done"), 1)
                    token_sums(yT0[:, 0:4], "ln_mean")
                elif name == "L:sq":
                    pe.wait_ge(sem("ln_sq"), 1)
                    token_sums(cut(wide[:, 1024:2048], S), "ln_sum")
                elif name == "vd":
                    tokens("vd", P, P)
                else:
                    project(name)

            def attention(units, fill):
                scores(units[0])
                scores(units[1])
                for i, u in enumerate(units):
                    if i + 2 < len(units):
                        scores(units[i + 2])
                    for name in fill[i]:
                        between(name)
                    transposes(u, 0)
                    if i and UNITS[u - 1][3]:
                        mix(u - 1)
                    if key_tiles(u) == 2:
                        transposes(u, 1)
                mix(units[-1])

            def modulation(q):
                if q == 0:
                    pe.wait_ge(sem("ada_sum"), ADA - ADA_DVE)
                    pe.wait_ge(sem("ada_dve"), ADA_DVE)
                    begin("mod")
                b = bank("mod")
                for j in range(ADA // 4 * q, ADA // 4 * (q + 1)):
                    last = nc.tensor.matmul(b[:, j:j + 1], ada_acc[:, P * j:P * j + P], ones[:, 0:1], start=True, stop=True)
                if q == 3:
                    end(last)

            pe.wait_ge(first_in, 32)
            stream_sums("x0", 0, KD)
            project("uv0", fresh=0)
            for name in ("uv1", "ug0", "ug1", "bq0", "bq1"):
                project(name)
            pe.wait_ge(setup_in, 16 * N_SETUP)
            head_sums("bq0")
            project("bk0")
            head_sums("bq1")
            project("bk1")
            head_sums("bk0")
            pe.wait_ge(sem("diags_ready"), len(diags))
            pe.wait_ge(sem("hpad_ready"), 2)
            convolution(0)
            head_sums("bk1")
            convolution(1)
            tokens("bv0", 0, 256)
            tokens("bv1", 0, 256)
            pe.wait_ge(norm_done, NORM_AT["bk1"] + 1)
            pe.wait_ge(*evacuated("bv1"))
            attention(PART["b"], FILL_B)

            def output(layer, stream, pieces):
                for i in range(4):
                    wait = (lambda k: pe.wait_ge(y_ready, pieces + k // 2 + 1)) if i == 0 else None
                    u = f"wo{layer}_{i}"
                    features(u, *h_parts, [[(u, P * j, 0)] for j in range(2)], wait)
                    if i:
                        stream_sums(stream, 2 * i - 2, 2 * i)
                stream_sums(stream, 6, 8)

            output(0, "x1", 0)

            project("kcvc", fresh=1)
            project("ks")
            tokens("vs", P, P)
            head_sums("ks")
            project("qc0")
            project("qc1")
            head_sums("qc0")
            project("kw")
            head_sums("qc1")
            tokens("vw", P, P)
            head_sums("kw")
            tokens("gt", 0, 24)
            pe.wait_ge(sem("blocks_ready"), 4)
            for v, (name, group) in enumerate((("ck", "hidk"), ("cv", "hidv"))):
                b = begin(group)
                for nb in range(2):
                    n = WEIGHT_AT[f"{name}{nb}"]
                    pe.wait_ge(raw_in[RAW_AT[n]], raw_target(n))
                    w = cut(raw_slots[RAW_AT[n]], P)
                    for j in range(16):
                        last = nc.tensor.matmul(b[:, 32 * nb:32 * nb + 30], w[:, j, :], blocks[:, v, j, :],
                                                start=j == 0, stop=j == 15)
                end(last)
            pe.wait_ge(*evacuated("hidk"))
            b = begin("kc2")
            for k in range(2):
                last = nc.tensor.matmul(b[:, 0:30], kw2[:, k].rearrange("p g d -> p (g d)"), hid_x[:, 0, k, :],
                                        start=k == 0, stop=k == 1)
            end(last)
            pe.wait_ge(*evacuated("hidv"))
            b = begin("vc2")
            for g in range(2):
                for k in range(2):
                    last = nc.tensor.matmul(b[0:NCMP, HD * g:HD * g + HD], hid_x[:, 1, k, NCMP * g:NCMP * g + NCMP],
                                            vw2[:, k, :], start=k == 0, stop=k == 1)
            end(last)
            project("qd0")
            head_sums("cmp")
            pe.wait_ge(*evacuated("vs"))
            pe.wait_ge(*evacuated("vw"))
            pe.wait_ge(*evacuated("vc2"))
            attention(PART["c"] + PART["d"], FILL_CD)
            output(1, "x2", 4)

            project("rq0", fresh=2)
            for name in [f"rq{i}" for i in range(1, 4)] + [f"rk{i}" for i in range(4)]:
                project(name)
            for i in range(8):
                tokens(f"rv{i}", 0, 256)
            pe.wait_ge(sem("line_const_in"), 32)
            for g in range(AG):
                b = begin(f"dl{g}")
                end(nc.tensor.matmul(b[0:AH, 0:LINE], rel[:, AH * g:AH * g + AH], onehot[:, g, :], start=True, stop=True))

            def dilated_fill(name):
                if name[1] == "v":
                    tokens(name, 0, 256)
                else:
                    project(name)

            for h in range(RH):
                pe.wait_ge(*evacuated(f"rk{h}"))
                if h >= 2:
                    pe.wait_ge(sem("ret_decayed"), h - 1)
                for jt in range(2):
                    n, at = (S, 0) if jt == 0 else (P, S)
                    for k in range(2):
                        last = nc.tensor.matmul(sc[h % 2][:, at:at + n], rkT[:, 2 * h + k, P * jt:P * jt + P],
                                                rqT[:, 2 * h + k, S - n:S], start=k == 0, stop=k == 1)
                last.then_inc(sem("ret_scores"), 1)
                for i in range(2):
                    dilated_fill(RET_FILL[4 * h + i])
                pe.wait_ge(sem("ret_decayed"), h + 1)
                pe.wait_ge(*evacuated(f"rv{2 * h + 1}"))
                if h:
                    pe.wait_ge(sem("ret_normed"), 2 * h)
                e = prob2[:, h % 2].rearrange("p i j -> p (i j)")
                for t, dst in enumerate((pt, po)):
                    for jt in range(t + 1):
                        at = P * t if jt == 0 else S
                        last = nc.tensor.matmul(dst[:], e[:, at:at + P], rv[:, jt, RDV * h:RDV * h + RDV],
                                                start=jt == 0, stop=jt == t)
                    last.then_inc(sem("ret_out"), 1)
                for i in range(2, 4):
                    dilated_fill(RET_FILL[4 * h + i])
                pe.wait_ge(sem("ret_normed"), 2 * h + 2)
                for half in range(2):
                    b = begin(f"rt{h}_{half}")
                    for j in range(2):
                        for t in range(TT):
                            c = P * (2 * half + j)
                            last = nc.tensor.transpose(b[:, S * j + P * t:S * j + P * t + P], ron[:, t, c:c + P], ident[:])
                    end(last)
            for name in RET_FILL[16:]:
                dilated_fill(name)

            pe.wait_ge(*evacuated("av2_1"))
            attention(PART["a"], FILL_A)

            for i in range(4):
                wait = (lambda k: pe.wait_ge(y_ready, 8 + k // 2 + 1)) if i == 0 else None
                features(f"wr{i}", yret_hi, yret_lo, [[(f"wr{i}{x}", 0, 0)] for x in "ab"], wait)
            pe.wait_ge(po_free, STEPS_TO["a"])
            for i in range(4):
                features(f"wa{i}", att_hi, att_lo, [[(f"wa{i // 2}", 256 * (i % 2) + P * j, 0)] for j in range(2)])
            output(2, "x3", 16)

            for i in range(16):
                project(f"f1_{i}", fresh=3 if i == 0 else None)
            for i in range(8):
                wait = (lambda k: pe.wait_ge(sem("hid_ready"), k // 2 + 1)) if i == 0 else None
                features(f"f2_{i}", hid_hi, hid_lo, [[(f"f2_{i}a", 0, 0), (f"f2_{i}b", 0, 16)]], wait)
                if i:
                    stream_sums("xf", i - 1, i)
            stream_sums("xf", 7, 8)
            assert state["filled"] == len(GROUPS) and state["norm"] == len(NORMS)

        @block.scalar
        def _(act):
            state = dict(hi=0)

            def passing(name):
                def left(units, before):
                    if before is None:
                        return state["hi"] < NHI or GROUP_AT[name] >= GROUP_AT["wr0"]
                    return LAST_READ[units[before]] < GROUP_AT[name]

                while state["hi"] < len(SPLIT):
                    m = state["hi"]
                    v = SPLIT[m]
                    n = WEIGHT_AT[v]
                    if not (left(SPLIT, HI_BEFORE[m]) and (n < NRAW or left(WEIGHTS, RAW_BEFORE[n]))):
                        break
                    kt, w = unit_shape(v)
                    if HI_BEFORE[m] is not None:
                        act.wait_ge(proj_ready, LAST_READ[SPLIT[HI_BEFORE[m]]] + 1)
                    elif m >= NHI:
                        act.wait_ge(po_free, STEPS_TO["a"])
                    act.wait_ge(raw_in[RAW_AT[n]], raw_target(n))
                    nc.scalar.activation(hi_slots[HI_AT[m]][:, 0:kt * w], raw_slots[RAW_AT[n]][:, 0:kt * w], ACT.Copy) \
                        .then_inc(hi_ready, 1)
                    state["hi"] += 1

            def ready(name):
                passing(name)
                act.wait_ge(proj_ready, GROUP_AT[name] + 1)
                return bank(name)

            def copy_out(name, dst, fn=ACT.Copy, scale=1.0):
                b = ready(name)
                nc.scalar.activation(dst, b[:], fn, scale=scale).then_inc(free_of(name), 1)

            def copy_tokens(name, dst, n=256, fn=ACT.Copy):
                b = ready(name)
                nc.scalar.activation(dst, cut(b[:], S)[:, :, 0:n], fn).then_inc(free_of(name), 1)

            def head_squares(name, dst):
                w = NORM_W.get(name, 512)
                b = ready(name)
                act.wait_ge(norm_sum, NORM_AT[name])
                nc.scalar.activation(sq[:, 0:w], b[:, 0:w], ACT.Square).then_inc(norm_sq, 1)
                if name in Q_NORMS:
                    nc.scalar.activation(dst, b[:], ACT.Copy, scale=col(Q_GAIN[name[1] if name[0] == "q" else "b"])) \
                        .then_inc(free_of(name), 1)
                else:
                    nc.scalar.activation(dst, b[:, 0:w], ACT.Copy).then_inc(free_of(name), 1)

            def root(name):
                w = S if name in STREAM else NORM_W.get(name, 512)
                v = rstd_of(name) if name in Q_NORMS else rstd[:, 0:w]
                act.wait_ge(norm_var, NORM_AT[name] + 1)
                nc.scalar.activation(v, v, ACT.Sqrt).then_inc(norm_sqrt, 1)

            def table(fn):
                nc.scalar.activation(stat[:, 2, 19:20], ones[:, 0:1], fn).then_inc(sem("table"), 1)
                state["table"] = state.get("table", 0) + 1
                act.wait_ge(sem("table"), state["table"])

            def stream_squares(lo, hi, after):
                act.wait_ge(*(evacuated(after) if isinstance(after, str) else after))
                for k in range(lo, hi):
                    nc.scalar.activation(wide[:, S * k:S * k + S], xT[:, k, :], ACT.Square).then_inc(stream_sq, 1)

            def high_parts(name, shift=None):
                n = STREAM[name]
                for k in range(KD):
                    act.wait_ge(h_full, KD * n + k + 1)
                    h = wide[:, S * k:S * k + S]
                    if shift is None:
                        ins = nc.scalar.activation(parts[:, 0, k, :], h, ACT.Copy)
                    else:
                        ins = nc.scalar.activation(parts[:, 0, k, :], h, ACT.Identity, bias=mod[:, shift + k:shift + k + 1])
                    ins.then_inc(h_hi, 1)

            def exps(u):
                part, step, br, last_br, at, qt, n = UNITS[u]
                act.wait_ge(mx_ready, u + 1)
                s, e = stat[:, u % 3], prob(u)
                if part == "a":
                    nc.scalar.activation(e[:, 0:AG, 0:n], e[:, 0:AG, 0:n], ACT.Exp, bias=s[:, 4:5],
                                         accum_out=s[:, 8:9]).then_inc(exp_done, 1)
                    return
                for i in range(4):
                    last = nc.scalar.activation(e[:, i, 0:n], e[:, i, 0:n], ACT.Exp, bias=s[:, 4 + i:5 + i],
                                                accum_out=s[:, 8 + i:9 + i])
                if part == "d":
                    last = nc.scalar.activation(s[:, 12:16], s[:, 12:16], ACT.Exp)
                last.then_inc(exp_done, 1)

            def transposed_out(u):
                part, step, br, last_br, at, qt, n = UNITS[u]
                m = 3 if part == "a" else 4
                for r in range(key_tiles(u)):
                    act.wait_ge(tr_ready, rounds_before(u) + r + 1)
                    old = step if part == "c" or "c" in (UNITS[max(u - 1, 0)][0], UNITS[max(u - 2, 0)][0]) else step - 1
                    if old > 0:
                        act.wait_ge(pv_ready, old)
                    w = min(n - P * r, P)
                    nc.scalar.activation(pT(u, br, r)[0:w, 0:m, :], cut(pt[0:w, 0:P * m], P), ACT.Copy).then_inc(pt_ready, 1)

            def between(name):
                if name[:2] == "S:":
                    root(name[2:])
                elif name[0] == "z":
                    i = int(name[2])
                    dst = tmp[:, i] if name[1] == "a" else \
                        fl((yT0 if name[1] == "b" else yT1)[:, (0 if name[1] == "c" else 4) + 2 * i:][:, 0:2])
                    copy_out(name, dst, fn=ACT.Silu)
                elif name == "L:sq":
                    act.wait_ge(sem("ln_centred"), 1)
                    nc.scalar.activation(wide[:, 1024:2048], fl(yT0[:, 0:4]), ACT.Square).then_inc(sem("ln_sq"), 1)
                elif name in ("qd1", "kd"):
                    head_squares(name, kdT if name == "kd" else fl(qdT[:, 2:4]))
                elif name == "vd":
                    copy_tokens(name, vd, P)
                elif name[:2] == "rg":
                    i = int(name[2])
                    if i >= 2:
                        act.wait_ge(sem("rg_done"), i - 1)
                    copy_out(name, tmp[:, i % 2], fn=ACT.Silu)
                elif name[0] == "g":
                    i = int(name[2])
                    copy_out(name, fl((gaT if name[1] == "a" else gbT)[:, 2 * i:2 * i + 2]), fn=ACT.Sigmoid)

            def attention(units, fill):
                exps(units[0])
                for i, u in enumerate(units):
                    for name in fill[i]:
                        if name[:2] not in ("S:", "L:", "M:"):
                            passing(name)
                    if i + 1 < len(units):
                        exps(units[i + 1])
                    for name in fill[i]:
                        between(name)
                    transposed_out(u)

            def operand_high(pieces):
                for i, (dst, src, wait) in enumerate(pieces):
                    for w in wait:
                        act.wait_ge(*w)
                    nc.scalar.activation(dst, src, ACT.Copy).then_inc(y_hi, 1)

            act.dma_start(cols[:], a["vectors"]).then_inc(first_in, 16)
            act.dma_start(ones[:], a["ones"]).then_inc(first_in, 16)
            loads = ((ident[:], a["ident"]), (halves[:], a["halves"]), (rel[:], a["rel_bias_2"]),
                     (sinks[:], a["d_sinks"][0].partition_broadcast(P)),
                     (kw2[:, :, 0, :], a["c_k_w2"][0].rearrange("(k p) d -> p k d", p=P)),
                     (kw2[:, :, 1, :], a["c_k_w2"][0].rearrange("(k p) d -> p k d", p=P)),
                     (vw2[:], a["c_v_w2"][0].rearrange("(k p) d -> p k d", p=P)),
                     (vb2[:, 0, :], a["c_v_b2"][0].partition_broadcast(NCMP)),
                     (vb2[:, 1, :], a["c_v_b2"][0].partition_broadcast(NCMP)))
            assert len(loads) == N_SETUP
            for dst, src in loads:
                act.dma_start(dst, src).then_inc(setup_in, 16)
            act.wait_ge(first_in, 32)
            nc.scalar.activation(silu_c[:], col("c_2", 0, 8), ACT.Silu).then_inc(sem("silu_c_ready"), 1)
            table(ACT.Sqrt)
            for i in range(2):
                stream_squares(4 * i, 4 * i + 4, (x_in[i], 16))
            passing("uv0")

            def diagonals(lo, hi):
                for i in range(lo, hi):
                    k, c = divmod(i, 4)
                    nc.scalar.activation(diags[i], ident[:], ACT.Copy, scale=conv_col(c, CONV_DVE + k)).then_inc(sem("diags_ready"), 1)

            root("x0")
            high_parts("x0")
            table(ACT.Sigmoid)
            act.wait_ge(setup_in, 16 * N_SETUP)
            diagonals(0, 16)
            copy_out("uv0", wide[:, 0:512])
            diagonals(16, len(diags))
            copy_out("uv1", wide[:, 512:1024])
            copy_out("ug0", tmp[:, 0], fn=ACT.Sigmoid)
            copy_out("ug1", tmp[:, 1], fn=ACT.Sigmoid)
            table(ACT.Sqrt)
            head_squares("bq0", fl(bqT[:, 0:2]))
            head_squares("bq1", fl(bqT[:, 2:4]))
            root("bq0")
            head_squares("bk0", fl(bkT[:, 0:2]))
            root("bq1")
            head_squares("bk1", fl(bkT[:, 2:4]))
            root("bk0")
            root("bk1")
            copy_tokens("bv0", bv[:, :, 0:256])
            copy_tokens("bv1", bv[:, :, 256:512])
            table(ACT.Exp)
            attention(PART["b"], FILL_B)
            passing("wo0_0")
            table(ACT.Sqrt)
            act.wait_ge(sem("ln_var"), 1)
            nc.scalar.activation(rstd[:, 0:S], rstd[:, 0:S], ACT.Sqrt).then_inc(sem("ln_sqrt"), 1)
            table(ACT.Silu)
            act.wait_ge(sem("ln_scaled"), 1)
            for c in range(4):
                nc.scalar.activation(wide[:, 1024 + S * c:1024 + S * c + S], yT0[:, c, :], ACT.Silu, bias=col("a_ln_b", c),
                                     scale=col("a_ln_g", c)).then_inc(sem("ln_silu"), 1)
            two = lambda t, i: fl(t[:, 2 * i:2 * i + 2])
            hi_of = lambda i: fl(parts[:, 0, 2 * i:2 * i + 2])
            operand_high([(hi_of(i), two(yT0, i), [(sem("y_a_ready"), i + 1)] if i < 2 else
                           [(po_free, STEPS_TO["b"])]) for i in range(4)])
            table(ACT.Sqrt)

            def output_squares(layer, stream):
                for i in range(4):
                    passing(f"wo{layer}_{i}")
                    stream_squares(2 * i, 2 * i + 2, f"wo{layer}_{i}")
                root(stream)

            output_squares(0, "x1")

            high_parts("x1")
            copy_out("kcvc", fl(kcv))
            act.wait_ge(*evacuated("kcvc"))
            for f in range(2):
                for g in range(2):
                    act.dma_start(pairs[HD * f:HD * f + HD, :, g, 0:S - f], kcv[HD * g:HD * g + HD, :, f:S]) \
                        .then_inc(sem("pairs_in"), 16)
            head_squares("ks", ksT)
            copy_tokens("vs", vs, P)
            root("ks")
            head_squares("qc0", fl(qcT[:, 0:2]))
            head_squares("qc1", fl(qcT[:, 2:4]))
            root("qc0")
            head_squares("kw", kwT)
            root("qc1")
            copy_tokens("vw", vw, P)
            root("kw")
            copy_tokens("gt", gates, 24, fn=ACT.Sigmoid)
            for v, (group, bias) in enumerate((("hidk", "c_k_b1"), ("hidv", "c_v_b1"))):
                b = ready(group)
                for k in range(2):
                    last = nc.scalar.activation(hid_x[:, v, k, :], b[:, 32 * k:32 * k + 30], ACT.Silu, bias=col(bias, k))
                last.then_inc(free_of(group), 1)
            b = ready("kc2")
            nc.scalar.activation(kcn, b[:, 0:30], ACT.Identity, bias=col("c_k_b2")).then_inc(free_of("kc2"), 1)
            act.wait_ge(*evacuated("kc2"))
            act.wait_ge(norm_sum, NORM_AT["cmp"])
            nc.scalar.activation(sq[:, 0:30], kcn, ACT.Square).then_inc(norm_sq, 1)
            table(ACT.Sqrt)
            head_squares("qd0", fl(qdT[:, 0:2]))
            root("cmp")
            table(ACT.Exp)
            attention(PART["c"] + PART["d"], FILL_CD)
            operand_high([(hi_of(i), two(yT1, i), [(po_free, STEPS_TO["d"])]) for i in range(4)])
            table(ACT.Sqrt)
            output_squares(1, "x2")

            high_parts("x2", 0)
            for name in [f"rq{i}" for i in range(4)] + [f"rk{i}" for i in range(4)]:
                passing(name)
            for i in range(8):
                copy_tokens(f"rv{i}", rv[:, :, 256 * i:256 * i + 256])

            def dilated_out(name):
                g, i = int(name[2]), int(name[-1])
                if name[1] == "v":
                    copy_tokens(name, av[:, g, :, 256 * i:256 * i + 256])
                else:
                    copy_out(name, (aqT if name[1] == "q" else akT)[:, g, 512 * i:512 * i + 512],
                             scale=P ** -0.5 if name[1] == "q" else 1.0)

            for h in range(RH):
                for i in range(2):
                    dilated_out(RET_FILL[4 * h + i])
                passing(RET_FILL[4 * h + 2])
                for t in range(TT):
                    act.wait_ge(sem("ret_var"), 2 * h + t + 1)
                    nc.scalar.activation(bn[:, t, 8:9], bn[:, t, 8:9], ACT.Sqrt).then_inc(sem("ret_sqrt"), 1)
                for i in range(2, 4):
                    dilated_out(RET_FILL[4 * h + i])
                for half in range(2):
                    b = ready(f"rt{h}_{half}")
                    for j in range(2):
                        c = 4 * h + 2 * half + j
                        last = nc.scalar.activation(yretT[:, c, :], b[:, S * j:S * j + S], ACT.Identity,
                                                    bias=col("ret_gn_b_2", c), scale=col("ret_gn_g_2", c))
                    last.then_inc(free_of(f"rt{h}_{half}"), 1)
            for name in RET_FILL[16:]:
                dilated_out(name)
            attention(PART["a"], FILL_A)
            passing("wr0")
            operand_high([(fl(yret_hi[:, 2 * i:2 * i + 2]), two(yretT, i), [(sem("rg_done"), i + 1)]) for i in range(8)])
            for name in [f"wr{i}" for i in range(4)] + [f"wa{i}" for i in range(4)]:
                passing(name)
            operand_high([(hi_of(i), two(mT, i), [(sem("merged"), i + 1)]) for i in range(4)])
            table(ACT.Sqrt)
            output_squares(2, "x3")
            high_parts("x3", 24)
            for i in range(16):
                if i >= 2:
                    act.wait_ge(sem("hid_ready"), i - 1)
                copy_out(f"f1_{i}", tmp[:, i % 2], fn=ACT.Relu)
                act.wait_ge(*evacuated(f"f1_{i}"))
                nc.scalar.activation(two(hid_hi, i), tmp[:, i % 2], ACT.Square).then_inc(sem("hid_high"), 1)
            for i in range(8):
                passing(f"f2_{i}")
                stream_squares(i, i + 1, f"f2_{i}")
            root("xf")
            for i in range(4):
                act.wait_ge(h_full, KD * 4 + 2 * i + 2)
                act.dma_start(out[:, 512 * i:512 * i + 512], wide[:, 512 * i:512 * i + 512]).then_inc(sem("stored"), 16)
            act.wait_ge(sem("stored"), 64)

        @block.vector
        def _(dve):
            own = Steps(dve, "dve_step")
            V = nc.vector

            def ready(name):
                dve.wait_ge(proj_ready, GROUP_AT[name] + 1)
                return bank(name)

            def variance(name):
                n = NORM_AT[name]
                w, width = (S, D) if name in STREAM else (NORM_W.get(name, 512), HD)
                dve.wait_ge(norm_sum, n + 1)
                if n:
                    dve.wait_ge(norm_done, n)
                if name in Q_NORMS:
                    V.tensor_scalar(rstd_of(name), st[:, 0:8], HD * EPS, None, ALU.add).then_inc(norm_var, 1)
                    return
                V.tensor_scalar(rstd[:, 0:w], st[:, 0:w], 1.0 / width, EPS, ALU.mult, ALU.add).then_inc(norm_var, 1)

            def inverse(name, w):
                dve.wait_ge(norm_sqrt, NORM_AT[name] + 1)
                own.did(V.reciprocal(rstd[:, 0:w], rstd[:, 0:w]))
                own.settle()

            def stream_norm(name, gain, shift=None, split=True):
                n = STREAM[name]

                def low(k):
                    dve.wait_ge(h_hi, KD * n + k + 1)
                    h, hi = wide[:, S * k:S * k + S], parts[:, 0, k, :].bitcast(F32)
                    if shift is None:
                        ins = V.tensor_tensor(parts[:, 1, k, :], h, hi, ALU.subtract)
                    else:
                        ins = V.scalar_tensor_tensor(parts[:, 1, k, :], h, mod[:, shift + k:shift + k + 1], hi, ALU.add, ALU.subtract)
                    ins.then_inc(h_ready, 1)

                variance(name)
                inverse(name, S)
                for k in range(KD):
                    V.scalar_tensor_tensor(wide[:, S * k:S * k + S], xT[:, k, :], gain[:, k:k + 1], rstd[:, 0:S],
                                           ALU.mult, ALU.mult).then_inc(h_full, 1)
                    if split and k >= 2:
                        low(k - 2)
                if split:
                    low(KD - 2)
                    low(KD - 1)
                V.tensor_copy(bn[:, 0, 9:10], rstd[:, 0:1]).then_inc(norm_done, 1)

            def head_norm_end(name, src, dst, gain):
                w = NORM_W.get(name, 512)
                if name in Q_NORMS:
                    dve.wait_ge(norm_sqrt, NORM_AT[name] + 1)
                    dve.wait_ge(*evacuated(src))
                    V.reciprocal(rstd_of(name), rstd_of(name)).then_inc(norm_done, 1)
                    return
                inverse(name, w)
                dve.wait_ge(*evacuated(src))
                V.scalar_tensor_tensor(dst, dst, col(gain), rstd[:, 0:w], ALU.mult, ALU.mult).then_inc(norm_done, 1)

            def score_max(u):
                part, step, br, last_br, at, qt, n = UNITS[u]
                e, s = prob(u), stat[:, u % 3]
                dve.wait_ge(sc_ready, u + 1)
                if u >= 3:
                    dve.wait_ge(tr_ready, rounds_before(u - 2))
                if part != "a":
                    dve.wait_ge(norm_done, NORM_AT[f"{'bq' if part == 'b' else 'q' + part}{at}"] + 1)
                if part == "a":
                    for g in range(AG):
                        ins = V.tensor_tensor_reduce(out=e[:, g, 0:n], in0=sc[g // 2][:, S * (g % 2):S * (g % 2) + n],
                                                     in1=dil_bias[:, g, at, S - n:S], scale=1.0, scalar=-3e38,
                                                     op0=ALU.add, op1=ALU.max, accum_out=s[:, g:g + 1])
                    ins.then_inc(sc_free, 1)
                    dve.wait_ge(sc_free, u + 1)
                    V.tensor_reduce(s[:, 4:5], s[:, 0:3], AX.X, ALU.max, negate=True).then_inc(mx_ready, 1)
                    return
                for i in range(4):
                    f, bi = divmod(i, 2)
                    h = 2 * (2 * at + bi) + f if part == "b" else 2 * at + bi + 4 * f
                    bias = cmp_bias[:, qt, h, :] if part == "c" and br == 0 else (swa if part == "d" else alibi)[:, h, S - n:S]
                    i8 = 4 * qt + 2 * bi + f
                    ins = V.scalar_tensor_tensor(e[:, i, 0:n], sc[f][:, S * bi:S * bi + n],
                                                 q_rstd[:, "bcd".index(part), at, i8:i8 + 1], bias, ALU.mult, ALU.add)
                    if i < 3:
                        own.did(ins)
                    else:
                        ins.then_inc(sc_free, 1)
                own.settle()
                dve.wait_ge(sc_free, u + 1)
                if part == "b" or part == "c" and br:
                    V.tensor_reduce(s[:, 4:8], e[:, :, 0:n], AX.X, ALU.max, negate=True).then_inc(mx_ready, 1)
                    return
                own.did(V.tensor_reduce(s[:, 0:4], e[:, :, 0:n], AX.X, ALU.max))
                own.settle()
                sk = sinks[:].rearrange("p (f b) -> p f b", f=2)[:, :, 2 * at:2 * at + 2]
                if part == "d":
                    own.did(V.tensor_tensor(cut(s[:, 0:4], 2), cut(s[:, 0:4], 2), sk, ALU.max))
                    own.settle()
                ins = V.tensor_scalar(s[:, 4:8], s[:, 0:4], -1e28, -1.0, ALU.max, ALU.mult)
                if part == "d":
                    own.did(ins)
                    own.settle()
                    ins = V.tensor_tensor(cut(s[:, 12:16], 2), cut(s[:, 4:8], 2), sk, ALU.add)
                ins.then_inc(mx_ready, 1)

            def normalise(u):
                part, step, br, last_br, at, qt, n = UNITS[u]
                e, s = prob(u), stat[:, u % 3]
                m = 1 if part == "a" else 4
                dve.wait_ge(exp_done, u + 1)
                if part == "d":
                    own.did(V.tensor_tensor(s[:, 8:12], s[:, 8:12], s[:, 12:16], ALU.add))
                    own.settle()
                if part == "c" and br == 0:
                    own.did(V.tensor_scalar(s[:, 8:8 + m], s[:, 8:8 + m], 1e-30, None, ALU.max))
                    own.settle()
                own.did(V.reciprocal(s[:, 8:8 + m], s[:, 8:8 + m]))
                own.settle()
                if part == "a":
                    V.tensor_scalar(e[:, 0:AG, 0:n], e[:, 0:AG, 0:n], s[:, 8:9], None, ALU.mult).then_inc(p_ready, 1)
                    return
                if part == "c":
                    gate = gates[:, qt, 8 * br:8 * br + 8].rearrange("p (f b) -> p f b", f=2)[:, :, 2 * at:2 * at + 2]
                    own.did(V.tensor_tensor(cut(s[:, 8:12], 2), cut(s[:, 8:12], 2), gate, ALU.mult))
                    own.settle()
                V.tensor_tensor(e[:, :, 0:n], e[:, :, 0:n], s[:, 8:12].unsqueeze(2).broadcast_to([P, 4, n]), ALU.mult) \
                    .then_inc(p_ready, 1)

            def mixed_out(u):
                part, step, br, last_br, at, qt, n = UNITS[u]
                dve.wait_ge(pv_ready, step + 1)
                if part == "a":
                    hi, lo = att_hi[:, at, P * qt:P * qt + P], att_lo[:, at, P * qt:P * qt + P]
                    own.did(V.tensor_copy(hi, po[:, 0:P]))
                    own.settle()
                    V.tensor_tensor(lo, po[:, 0:P], hi.bitcast(F32), ALU.subtract).then_inc(po_free, 1)
                    return
                y, c = dict(b=(yT0, 4), c=(yT1, 0), d=(yT1, 4))[part]
                gate = dict(b="zb", c="zc", d="zd")[part] + str(at)
                dve.wait_ge(*evacuated(gate))
                y = y[:, c + 2 * at:c + 2 * at + 2, P * qt:P * qt + P]
                V.tensor_tensor(y, cut(po[:, 0:S], P), y, ALU.mult).then_inc(po_free, 1)

            def between(name):
                if name[:2] == "S:":
                    variance(name[2:])
                    dst, gain = dict(qd0=(fl(qdT[:, 0:2]), "d_qnorm_g"), qd1=(fl(qdT[:, 2:4]), "d_qnorm_g"),
                                     kd=(kdT, "d_knorm_g"))[name[2:]]
                    head_norm_end(name[2:], name[2:], dst, gain)
                elif name[:2] == "rg":
                    i = int(name[2])
                    y = fl(yretT[:, 2 * i:2 * i + 2])
                    dve.wait_ge(*evacuated(f"rt{i // 2}_{i % 2}"))
                    dve.wait_ge(*evacuated(name))
                    V.tensor_tensor(y, y, tmp[:, i % 2], ALU.mult).then_inc(sem("rg_done"), 1)

            def attention(units, fill):
                score_max(units[0])
                score_max(units[1])
                for i, u in enumerate(units):
                    normalise(u)
                    for name in fill[i]:
                        between(name)
                    if i + 2 < len(units):
                        score_max(units[i + 2])
                    if i and UNITS[u - 1][3]:
                        mixed_out(u - 1)
                mixed_out(units[-1])

            two = lambda t, i: fl(t[:, 2 * i:2 * i + 2])
            state = dict(y=0)

            def operand_low(pieces):
                for dst, src, hi in pieces:
                    state["y"] += 1
                    dve.wait_ge(y_hi, state["y"])
                    V.tensor_tensor(dst, src, hi.bitcast(F32), ALU.subtract).then_inc(y_ready, 1)

            def parts_low(src):
                operand_low([(two(parts[:, 1], i), two(src, i), two(parts[:, 0], i)) for i in range(4)])

            dve.wait_ge(first_in, 32)
            for i in range(2):
                dve.wait_ge(x_in[i], 16)
            stream_norm("x0", col("norm_g", 0, 8))

            def ada_pair(j0):
                for j in (j0, j0 + 1):
                    dve.wait_ge(sem(f"slab_in{SLAB_AT[j]}"), 16 * SLAB_AT[:j + 1].count(SLAB_AT[j]))
                for k in range(KD):
                    for j in (j0, j0 + 1):
                        at = P * (ADA - ADA_DVE + j)
                        acc, w, c = ada_acc[:, at:at + P], slabs[SLAB_AT[j]][:, k, :], silu_c[:, k:k + 1]
                        if k == 0:
                            own.did(V.tensor_scalar(acc, w, c, None, ALU.mult))
                            continue
                        dve.wait_ge(own.sem, own.n - 1 if k < KD - 1 or j == j0 else own.n)
                        ins = V.scalar_tensor_tensor(acc, w, c, acc, ALU.mult, ALU.add)
                        if k < KD - 1:
                            own.did(ins)
                        else:
                            ins.then_inc(sem("ada_dve"), 1)

            dve.wait_ge(sem("silu_c_ready"), 1)
            for j in range(0, ADA_FIRST, 2):
                ada_pair(j)
            own.did(V.memset(hpad[:, :, 0:TAPS - 1], 0.0))
            own.settle()
            for i in range(2):
                dve.wait_ge(*evacuated(f"uv{i}"))
                dve.wait_ge(*evacuated(f"ug{i}"))
                V.tensor_tensor(hpad[:, 2 * i:2 * i + 2, TAPS - 1:], cut(tmp[:, i], S), u_val[:, 2 * i:2 * i + 2], ALU.mult) \
                    .then_inc(sem("hpad_ready"), 1)
            dve.wait_ge(sem("hpad_ready"), 2)

            def taps(lo, hi):
                for tap in range(lo, hi):
                    for c in range(4):
                        y, h = yT0[:, c, :], hpad[:, c, tap:tap + S]
                        if tap == 0:
                            own.did(V.tensor_scalar(y, h, conv_col(c, 0), None, ALU.mult))
                        else:
                            dve.wait_ge(own.sem, own.n - 3)
                            own.did(V.scalar_tensor_tensor(y, h, conv_col(c, tap), y, ALU.mult, ALU.add))

            taps(0, 4)
            for i, (name, dst, gain) in enumerate((("bq0", None, None), ("bq1", None, None),
                                                   ("bk0", bkT[:, 0:2], "b_knorm_g"), ("bk1", bkT[:, 2:4], "b_knorm_g"))):
                variance(name)
                taps(4 + 3 * i, 7 + 3 * i)
                head_norm_end(name, name, None if dst is None else fl(dst), gain)
            own.settle()
            for c in range(4):
                b = ready(f"conv{c // 2}")
                ins = V.scalar_tensor_tensor(yT0[:, c, :], b[:, S * (c % 2):S * (c % 2) + S], col("a_conv_b", c),
                                             yT0[:, c, :], ALU.add, ALU.add)
                if c % 2:
                    ins.then_inc(free_of(f"conv{c // 2}"), 1)
                else:
                    own.did(ins)
            own.settle()
            for c in range(2):
                dve.wait_ge(*evacuated(f"conv{c}"))
            dve.wait_ge(const_in, 16 * 3)
            every = lambda ap: ap.unsqueeze(1).broadcast_to([P, 4, S])
            y_a = yT0[:, 0:4]

            def conv_between(units):
                score_max(units[0])
                score_max(units[1])
                for i, u in enumerate(units):
                    if i < 2:
                        taps(16 + 3 * i, 19 + 3 * i)
                    normalise(u)
                    if i + 2 < len(units):
                        score_max(units[i + 2])
                    if i:
                        mixed_out(u - 1)
                    if i == 1:
                        own.settle()
                        V.tensor_copy(bn[:, 1, 9:10], yT0[:, 0, 0:1]).then_inc(sem("conv_done"), 1)
                    if i == 2:
                        dve.wait_ge(sem("ln_mean"), 1)
                        own.did(V.tensor_scalar(rstd[:, 0:S], st[:, 0:S], 1.0 / GW, None, ALU.mult))
                        own.settle()
                        V.tensor_tensor(y_a, y_a, every(rstd[:, 0:S]), ALU.subtract).then_inc(sem("ln_centred"), 1)
                mixed_out(units[-1])

            assert CONV_DVE == 22
            conv_between(PART["b"])
            dve.wait_ge(sem("ln_sum"), 1)
            dve.wait_ge(sem("ln_centred"), 1)
            V.tensor_scalar(rstd[:, 0:S], st[:, 0:S], 1.0 / GW, EPS, ALU.mult, ALU.add).then_inc(sem("ln_var"), 1)
            dve.wait_ge(sem("ln_sqrt"), 1)
            own.did(V.reciprocal(rstd[:, 0:S], rstd[:, 0:S]))
            own.settle()
            V.tensor_tensor(y_a, y_a, every(rstd[:, 0:S]), ALU.mult).then_inc(sem("ln_scaled"), 1)
            for i in range(2):
                dve.wait_ge(sem("ln_silu"), 2 * i + 2)
                dve.wait_ge(*evacuated(f"za{i}"))
                V.tensor_tensor(two(yT0, i), wide[:, 1024 + 512 * i:1536 + 512 * i], tmp[:, i], ALU.mult).then_inc(sem("y_a_ready"), 1)
            parts_low(yT0)

            def residual(layer):
                for i in range(4):
                    b = ready(f"wo{layer}_{i}")
                    x = fl(xT[:, 2 * i:2 * i + 2])
                    V.tensor_tensor(x, b[:], x, ALU.add).then_inc(free_of(f"wo{layer}_{i}"), 1)

            residual(0)

            stream_norm("x1", col("norm_g", 8, 8))
            ada_pair(ADA_FIRST)
            variance("ks")
            dve.wait_ge(sem("pairs_in"), 64)
            for v, pos in enumerate(("c_pos_k", "c_pos_v")):
                for g in range(2):
                    src = pairs[:, v, g, :]
                    ov = bass.AP(src.tensor, src.offset, [list(src.ap[0]), [2, 16], [16, NCMP]])
                    V.tensor_tensor(blocks[:, v, :, NCMP * g:NCMP * g + NCMP], ov,
                                    col(pos, 0, 16).unsqueeze(2).broadcast_to([P, 16, NCMP]), ALU.add) \
                        .then_inc(sem("blocks_ready"), 1)
            head_norm_end("ks", "ks", ksT, "c_knorm_slc_g")
            ada_pair(ADA_FIRST + 2)
            for i, (name, dst, gain) in enumerate((("qc0", None, None), ("qc1", None, None), ("kw", kwT, "c_knorm_win_g"))):
                variance(name)
                head_norm_end(name, name, dst, gain)
                ada_pair(ADA_FIRST + 4 + 2 * i)
            for j in range(ADA_FIRST + 10, ADA_DVE, 2):
                ada_pair(j)
            b = ready("vc2")
            V.tensor_tensor(vcn[0:NCMP, :], b[0:NCMP, 0:P], vb2[:].rearrange("p g d -> p (g d)"), ALU.add).then_inc(free_of("vc2"), 1)
            variance("cmp")
            head_norm_end("cmp", "kc2", kcn, "c_knorm_cmp_g")
            dve.wait_ge(*evacuated("gt"))
            attention(PART["c"] + PART["d"], FILL_CD)
            parts_low(yT1)
            b = ready("mod")
            V.tensor_tensor(mod[:], b[:, 0:48], col("b_ada_2", 0, 48), ALU.add).then_inc(free_of("mod"), 1)
            dve.wait_ge(*evacuated("mod"))
            own.did(V.scalar_tensor_tensor(gain1[:], mod[:, 8:16], 1.0, col("norm1_g_2", 0, 8), ALU.add, ALU.mult))
            own.did(V.scalar_tensor_tensor(gain2[:], mod[:, 32:40], 1.0, col("norm2_g_2", 0, 8), ALU.add, ALU.mult))
            own.settle()
            residual(1)

            stream_norm("x2", gain1[:], shift=0)
            dve.wait_ge(rot_in, 32)
            both = lambda ap: ap.unsqueeze(1).broadcast_to([P, 2, S])
            for c, dst in (("rq", rqT), ("rk", rkT)):
                for h in range(RH):
                    b = ready(f"{c}{h}")
                    own.did(V.tensor_tensor(cut(tmp[:, 0], S), cut(b[:], S), both(cos_t[:]), ALU.mult))
                    own.did(V.tensor_tensor(cut(tmp[:, 1], S), cut(b[:], S), both(sin_t[:]), ALU.mult))
                    own.settle()
                    own.did(V.tensor_tensor(dst[:, 2 * h, :], tmp[:, 0, 0:S], tmp[:, 1, S:], ALU.subtract))
                    V.tensor_tensor(dst[:, 2 * h + 1, :], tmp[:, 1, 0:S], tmp[:, 0, S:], ALU.add).then_inc(free_of(f"{c}{h}"), 1)
                    dve.wait_ge(*evacuated(f"{c}{h}"))
            dve.wait_ge(sem("line_const_in"), 32)
            for g in range(AG):
                b = ready(f"dl{g}")
                V.tensor_tensor(line[:, g, :], b[0:AH, 0:LINE], linemask[:, g, :], ALU.add).then_inc(free_of(f"dl{g}"), 1)
            for g in range(AG):
                dve.wait_ge(*evacuated(f"dl{g}"))
            V.tensor_copy(bn[0:AH, 1, 9:10], line[:, 0, 0:1]).then_inc(sem("line_ready"), 1)
            dve.wait_ge(sem("decay_in"), 16)
            for h in range(RH):
                dve.wait_ge(sem("ret_scores"), h + 1)
                if h >= 2:
                    dve.wait_ge(sem("ret_out"), 2 * h - 2)
                e = prob2[:, h % 2].rearrange("p i j -> p (i j)")[:, 0:LINE]
                V.tensor_tensor(e, sc[h % 2][:, 0:LINE], decay[:, h, :], ALU.mult).then_inc(sem("ret_decayed"), 1)
                for t, src in enumerate((pt, po)):
                    dve.wait_ge(sem("ret_out"), 2 * h + t + 1)
                    own.did(V.bn_stats(bn[:, t, 0:6], src[:]))
                    own.settle()
                    own.did(V.bn_aggr(bn[:, t, 6:8], bn[:, t, 0:6]))
                    own.settle()
                    V.tensor_scalar(bn[:, t, 8:9], bn[:, t, 7:8], GN_EPS, None, ALU.add).then_inc(sem("ret_var"), 1)
                for t, src in enumerate((pt, po)):
                    dve.wait_ge(sem("ret_sqrt"), 2 * h + t + 1)
                    own.did(V.reciprocal(bn[:, t, 8:9], bn[:, t, 8:9]))
                    own.settle()
                    if h and t == 0:
                        dve.wait_ge(proj_ready, GROUP_AT[f"rt{h - 1}_1"] + 1)
                    V.tensor_scalar(ron[:, t, :], src[:], bn[:, t, 6:7], bn[:, t, 8:9], ALU.subtract, ALU.mult) \
                        .then_inc(sem("ret_normed"), 1)
                dve.wait_ge(sem("ret_normed"), 2 * h + 2)
            dve.wait_ge(sem("dil_in"), 16)
            attention(PART["a"], FILL_A)
            operand_low([(two(yret_lo, i), two(yretT, i), two(yret_hi, i)) for i in range(8)])
            for i in range(4):
                b = ready(f"wr{i}")
                dve.wait_ge(*evacuated(f"ga{i}"))
                V.tensor_tensor(two(mT, i), b[:], two(gaT, i), ALU.mult).then_inc(free_of(f"wr{i}"), 1)
            for i in range(4):
                b = ready(f"wa{i}")
                dve.wait_ge(*evacuated(f"gb{i}"))
                V.tensor_tensor(tmp[:, i % 2], b[:], two(gbT, i), ALU.mult).then_inc(free_of(f"wa{i}"), 1)
                dve.wait_ge(*evacuated(f"wa{i}"))
                dve.wait_ge(*evacuated(f"wr{i}"))
                V.tensor_tensor(two(mT, i), two(mT, i), tmp[:, i % 2], ALU.add).then_inc(sem("merged"), 1)
            parts_low(mT)

            def gated_residual(names, per, gate):
                for i, name in enumerate(names):
                    b = ready(name)
                    for j in range(per):
                        k = per * i + j
                        ins = V.scalar_tensor_tensor(xT[:, k, :], b[:, S * j:S * j + S], mod[:, gate + k:gate + k + 1], xT[:, k, :],
                                                     ALU.mult, ALU.add)
                    ins.then_inc(free_of(name), 1)

            gated_residual([f"wo2_{i}" for i in range(4)], 2, 16)
            stream_norm("x3", gain2[:], shift=24)
            for i in range(16):
                r = tmp[:, i % 2]
                dve.wait_ge(sem("hid_high"), i + 1)
                own.did(V.tensor_tensor(r, r, r, ALU.mult))
                own.settle()
                V.tensor_tensor(two(hid_lo, i), r, two(hid_hi, i).bitcast(F32), ALU.subtract).then_inc(sem("hid_ready"), 1)
            gated_residual([f"f2_{i}" for i in range(8)], 1, 40)
            stream_norm("xf", col("norm_f_g_2", 0, 8), split=False)


def shape_constants():
    f = np.float32
    p = np.arange(P)
    both = (p[:, None] // HD == p[None, :] // HD).astype(f)
    slopes = np.power(2.0, -8.0 * np.arange(1, NH + 1) / NH).astype(f)
    dist = (P + p[:, None] - np.arange(S)[None, :]).astype(f)
    lin = -slopes[None, :, None] * dist[:, None, :]
    alibi = np.where(dist[:, None, :] >= 0, lin, -1e30).astype(f)
    swa = np.where((dist[:, None, :] >= 0) & (dist[:, None, :] < 128), lin, -1e30).astype(f)
    t = (np.arange(2)[None, :] * P + p[:, None])[:, :, None, None]
    dc = (t - (16 * np.arange(NCMP) + 31)).astype(f)
    cmp_bias = np.where(dc >= 0, -slopes[None, None, :, None] * dc, -1e30).astype(f)
    log_g = np.log1p(-(f(2.0) ** (-5.0 - np.arange(RH, dtype=f)))).astype(f)
    i = np.arange(LINE)
    j = np.where(i < S, 0, P)[None, :] + p[:, None]
    rel = (np.where(i < S, i, i - P)[None, :] - j).astype(f)
    decay = np.where(rel[:, None, :] >= 0, np.exp(log_g[None, :, None] * np.maximum(rel, 0)[:, None, :]), 0) / 16
    inv = f(10000.0) ** (-np.arange(P, dtype=f) / f(P))
    ang = np.arange(S, dtype=f)[None, :] * inv.astype(f)[:, None]
    d = 255 - np.arange(LINE)
    onehot = np.zeros((32, AG, LINE), f)
    mask = np.full((AH, AG, LINE), -1e30, f)
    for g, (win, dil) in enumerate(((128, 1), (512, 4), (2048, 16))):
        ok = (d >= 0) & (d <= win) & (d % dil == 0)
        dd = np.maximum(d, 1).astype(f)
        large = 16 + (np.log(dd / f(16)) / f(np.log(2048 / 16)) * f(16)).astype(np.int32)
        bucket = np.where(d < 16, d, np.minimum(large, 31))
        for u in np.nonzero(ok)[0]:
            onehot[bucket[u], g, u] = 1
            mask[:, g, u] = 0
    return dict(ident=np.eye(P, dtype=f), ones=np.ones((P, P), f), halves=both, alibi=alibi, swa=swa, cmp_bias=cmp_bias,
                decay=decay.astype(f), cos=np.cos(ang).astype(f), sin=np.sin(ang).astype(f), onehot=onehot, linemask=mask)


def lay_out(inputs):
    v = {n: np.asarray(inputs[n]) for n in inputs}
    tiles = lambda w: w.reshape(-1, P, w.shape[-1]).transpose(1, 0, 2).reshape(P, -1)

    def unit(u):
        kt, w = unit_shape(u)
        i = 0 if u in OD_ONE else int(u.rstrip("ab")[-1])
        if u in OD_ONE:
            return tiles(v["o_w_in"][0][:, OD_ONE[u][0]:OD_ONE[u][0] + w])
        if u in PAIRED:
            heads = [2 * i + j // 2 + 4 * (j % 2) for j in range(4)]
            return tiles(np.concatenate([v["o_w_in"][0][:, OD[u[:2]] + HD * h:OD[u[:2]] + HD * h + HD] for h in heads], axis=1))
        if u[:2] in ("ck", "cv"):
            return tiles(v[f"c_{u[1]}_w1"][0][:, P * i:P * i + P])
        if u[:2] == "wr":
            c = 256 * i + P * (u[-1] == "b")
            return tiles(v["w_ret_out_2"][0][:, c:c + P])
        if u[:2] == "f2":
            k = 2048 * (u[-1] == "b")
            return tiles(v["w_ff2_2"][0][k:k + 2048, P * i:P * i + P])
        if u[:2] == "wa":
            return tiles(v["w_att_out_2"][0][:, 512 * i:512 * i + 512])
        if u[:3] == "wo1":
            c = 256 * int(u[-1])
            return tiles(v["w_out"][1][:, c:c + 256].reshape(2, 2, 4, HD, 256).transpose(0, 2, 1, 3, 4).reshape(D, 256))
        if u[:2] == "wo":
            src, c = (v["w_out"][0] if u[2] == "0" else v["w_o_2"][0]), 0
        elif u[:2] == "f1":
            src, c, i = v["w_ff1_2"][0], 0, int(u[3:])
        elif u[:2] in EV:
            src, c = v["e_w_in"][0], EV[u[:2]]
        elif u[:2] in IN2:
            src, c = v["w_in_2"][0], IN2[u[:2]]
        else:
            src, c = v["w_in_2"][0], IN2_ATT + 1536 * int(u[2]) + 512 * "qkv".index(u[1])
        return tiles(src[:, c + 256 * i:c + 256 * i + 256])

    weights = np.zeros((len(WEIGHTS), P, UNIT), np.float32)
    for n, u in enumerate(WEIGHTS):
        part = unit(u)
        weights[n, :, 0:part.shape[1]] = part
    columns = [v[n].reshape(c, P).T for n, c in FULL] + [np.tile(v[n].reshape(HD), 2)[:, None] for n in HALF]
    columns.append(v["a_conv_w"][0].T.reshape(4, P, TAPS).transpose(1, 0, 2).reshape(P, 4 * TAPS))
    out = {n: v[n] for n in ("rel_bias_2", "d_sinks", "c_k_w2", "c_v_w2", "c_v_b2")}
    out.update(x=tiles(v["x"][0].T), weights=weights, vectors=np.concatenate(columns, axis=1),
               w_ada=v["w_ada_2"][0].reshape(KD, P, ADA, P).transpose(2, 1, 0, 3).reshape(ADA, P, KD * P))
    return out


def kernel(**inputs):
    import concourse.bacc as bacc
    from concourse.bass_utils import run_bass_kernel_spmd as run

    nc = bacc.Bacc("TRN2", target_bir_lowering=False, num_devices=1)
    arrays = lay_out(inputs)
    arrays.update(shape_constants())
    arrays = {f"in_{n}": np.ascontiguousarray(v) for n, v in arrays.items()}
    aps = {n[3:]: nc.dram_tensor(n, v.shape, mybir.dt.from_np(v.dtype), kind="ExternalInput").ap() for n, v in arrays.items()}
    out = nc.dram_tensor("y", (P, KD * S), F32, kind="ExternalOutput").ap()
    mixer_kernel(nc, aps, out)
    y = run(nc, [arrays], core_ids=[0]).results[0]["y"]
    return y.reshape(P, KD, S).transpose(2, 1, 0).reshape(1, S, D)
```

```python
import numpy as np
import concourse.bass as bass
from concourse import mybir
from contextlib import ExitStack

F32 = mybir.dt.float32
F32R = mybir.dt.float32r
ALU = mybir.AluOpType
ACT = mybir.ActivationFunctionType
AX = mybir.AxisListType

P = 128
S = 256
TT = S // P
D = 1024
KD = D // P
GW = 512
HD = 64
NH = 8
TAPS = 31
NCMP = 15
RH, RDK, RDV = 4, 256, 512
AG, AH = 3, 4
EPS = 1e-6
GN_EPS = 1e-5
LINE = 384
UNIT = 2048
NRAW = 4
NHI = 3
NPP = 3
PADW = S + TAPS - 1
ADA = 6 * D // P
ADA_DVE = 26
ADA_FIRST = 14
ADA_ONE = 16
ADA_POOL = dict(zb0=2, zb1=2, za0=1, za1=1, vdgt=2, qd0=1, qd1=1, kd=1, zc1=1, zd0=2, zd1=2, wo1_1=6)
CONV_DVE = 22
ARENA = 18568


EV = dict(uv=0, ug=512, za=1024, bq=1536, bk=2048, bv=2560, zb=3072)
OD = dict(qc=0, zc=1304, qd=1816, zd=2584)
OD_ONE = dict(kcvc=((512, 256),), kskw=((768, P), (1024, P)), vsvw=((896, P), (1152, P)), vdgt=((2456, P), (1280, 24)),
              kd=((2328, P),))
IN2 = dict(rq=0, rk=1024, rv=2048, rg=4096, ga=10752, gb=11776)
IN2_ATT = 6144
PAIRED = ("qc0", "qc1", "qd0", "qd1", "zc0", "zc1", "zd0", "zd1")

RET_FILL = [f"a{n}{g}_{i}" for g in range(AG) for n in "qk" for i in range(2)] + \
    [f"av{g}_{i}" for g in range(AG) for i in range(2)]
FILL_B = [["zb0", "L:mean"], ["zb1", "L:sq"], ["za0", "L:act"], ["za1"]]
FILL_CD = [x.split() for x in (
    "/ qd1.0", "/ qd1.1", "/ E:qd1 kd.0", "S:qd1 / E:kd zc1.0", "S:kd / zc1.1", "/ E:zc1 zd0.0", "/ zd0.1", "/ E:zd0 zd1.0",
    "/ zd1.1", "/ E:zd1", "/ M:0", "/ M:1", "/ M:2", "/ M:3", "Y:c /", "")]
GATED = [f"rg{i}" for i in range(8)] + [f"ga{i}" for i in range(4)] + [f"gb{i}" for i in range(4)]
FILL_A = [[GATED[2 * i], "/", GATED[2 * i + 1]] for i in range(8)]


BRANCHES = ["wr0"] + [f"wa{i}" for i in range(4)] + [f"wr{i}" for i in range(1, 4)]


def fills_of(fill):
    out = list(dict.fromkeys(x.split(".")[0] for items in fill for x in items if x != "/" and x[1] != ":"))
    return out + ["modA"] * any(x[:2] == "M:" for items in fill for x in items)


def around(items):
    at = items.index("/") if "/" in items else len(items)
    return items[:at], items[at + 1:]


def group_plan():
    own = lambda names: [(n, [n]) for n in names]
    out = own(["uv0", "uv1", "ug0", "ug1", "bq0", "bq1", "bk0", "bk1"]) + own(["bv0", "bv1"])
    out += [("conv0", []), ("conv1", [])] + own(fills_of(FILL_B))
    out += own([f"wo0_{i}" for i in range(4)])
    out += own(["kcvc", "kskw", "vsvw", "qc0", "qc1", "vdgt"])
    out += [("hidk", ["ck0", "ck1"]), ("qd0", ["qd0"]), ("hTk", []), ("hidv", ["cv0", "cv1"]), ("kc2", []), ("hTv", []),
            ("zc0", ["zc0"]), ("vc2", [])]
    out += [(n, [] if n == "modA" else [n]) for n in fills_of(FILL_CD)]
    out += own([f"wo1_{i}" for i in range(4)]) + [("modB", [])]
    out += own([f"rq{i}" for i in range(4)] + [f"rk{i}" for i in range(4)] + [f"rv{i}" for i in range(8)])
    for h in range(RH):
        out += own(RET_FILL[4 * h:4 * h + 4]) + [(f"rt{h}_0", []), (f"rt{h}_1", [])]
        if h == 0:
            out += [(n, []) for n in ("modC", "dl0", "dl1", "dl2")]
    out += own(RET_FILL[16:]) + own(GATED)
    out += [(n, [f"{n}a", f"{n}b"] if n[1] == "r" else [f"wa{int(n[2]) // 2}"]) for n in BRANCHES]
    out += own([f"wo2_{i}" for i in range(4)] + [f"f1_{i}" for i in range(16)])
    out += [(f"f2_{i}", [f"f2_{i}a", f"f2_{i}b"]) for i in range(8)]
    return out


PLAN = group_plan()
GROUPS = [g for g, _ in PLAN]
GROUP_AT = {n: i for i, n in enumerate(GROUPS)}
UNITS_OF = dict(PLAN)
WEIGHTS = list(dict.fromkeys(u for _, us in PLAN for u in us))
WEIGHT_AT = {n: i for i, n in enumerate(WEIGHTS)}
LAST_READ = {u: max(i for i, (_, us) in enumerate(PLAN) if u in us) for u in WEIGHTS}
SPLIT = [u for u in WEIGHTS if u[:2] not in ("ck", "cv")]
SPLIT_AT = {n: i for i, n in enumerate(SPLIT)}


def unit_shape(u):
    if u in OD_ONE:
        return 8, sum(n for _, n in OD_ONE[u])
    if u[:2] in ("wr", "f2"):
        return 16, 128
    return (4, 512) if u[:2] == "wa" else (8, 256)


def take_slots(units, slots, more):
    at, before, last = [], [], {}
    for n in range(len(units)):
        free = range(slots + sum(n >= units.index(start) for start in more))
        at.append(min(free, key=lambda x: last.get(x, -1)))
        before.append(last.get(at[-1]))
        last[at[-1]] = n
    return at, before


RAW_MORE, HI_MORE = ("wr1a", "f1_0"), ("wa1", "wr1a")
RAW_AT, RAW_BEFORE = take_slots(WEIGHTS, NRAW, RAW_MORE)
HI_AT, HI_BEFORE = take_slots(SPLIT, NHI, HI_MORE)


def raw_target(n):
    return 16 * RAW_AT[:n + 1].count(RAW_AT[n])


SLAB_AT = [j % 5 if j < ADA_FIRST else (j - ADA_FIRST) % 3 for j in range(ADA_DVE)]
SLAB_BEFORE = [max((i for i in range(j) if SLAB_AT[i] == SLAB_AT[j]), default=None) for j in range(ADA_DVE)]


def ada_sends():
    out = {WEIGHT_AT["kcvc"] + 1: [0, 1, 2, 3, 4], WEIGHT_AT["rq0"]: list(range(ADA_FIRST, ADA_FIRST + 3))}
    out.update({WEIGHT_AT[u]: list(js) for u, js in (("vdgt", (5, 6)), ("ck1", (7, 8)), ("cv0", (9, 10)), ("zc0", (11, 12)),
                                                        ("qd1", (13,)))})
    for i in range((ADA_DVE - ADA_FIRST - 3 + 1) // 2):
        j = ADA_FIRST + 3 + 2 * i
        out[WEIGHT_AT["rv4"] + i] = list(range(j, min(j + 2, ADA_DVE)))
    assert ADA_FIRST == 14
    return out


HALF = ("b_qnorm_g", "b_knorm_g", "c_qnorm_g", "c_knorm_cmp_g", "c_knorm_slc_g", "c_knorm_win_g",
        "d_qnorm_g", "d_knorm_g", "c_k_b2")
FULL = (("norm_g", 16), ("c_2", 8), ("a_conv_b", 4), ("a_ln_g", 4), ("a_ln_b", 4), ("norm1_g_2", 8), ("norm2_g_2", 8),
        ("norm_f_g_2", 8), ("c_k_b1", 2), ("c_v_b1", 2), ("c_pos_k", 16), ("c_pos_v", 16), ("ret_gn_g_2", 16),
        ("ret_gn_b_2", 16), ("b_ada_2", 48))
COL_AT, CONV_AT = {}, 0
for _name, _c in FULL + tuple((n, 1) for n in HALF):
    COL_AT[_name] = CONV_AT, _c
    CONV_AT += _c
ONES_AT = CONV_AT + 4 * TAPS
IDENT_AT = ONES_AT + P
SINKS_AT = IDENT_AT + P
N_COLS = SINKS_AT + NH
SMALL = dict(halves=P, kw2=4 * HD, vw2=2 * HD, vb2=2 * HD, rel=AG * AH)


def attention_units():
    out, step = [], 0
    for bp in range(2):
        for qt in range(2):
            out.append(("b", step, 0, True, bp, qt, P * (qt + 1)))
            step += 1
    for bp in range(2):
        for qt in range(2):
            for br in (1, 2, 0):
                out.append(("c", step, br, br == 0, bp, qt, NCMP if br == 0 else P * (qt + 1)))
            step += 1
    for bp in range(2):
        for qt in range(2):
            out.append(("d", step, 0, True, bp, qt, P * (qt + 1)))
            step += 1
    for hh in range(AH):
        for qt in range(2):
            out.append(("a", step, 0, True, hh, qt, P * (qt + 1)))
            step += 1
    return out


UNITS = attention_units()


def key_tiles(u):
    return -(-UNITS[u][6] // P)


def rounds_before(u):
    return sum(key_tiles(i) for i in range(u))


PART = {p: [u for u in range(len(UNITS)) if UNITS[u][0] == p] for p in "bcda"}
STEPS_TO = {p: UNITS[PART[p][-1]][1] + 1 for p in "bcda"}

NORMS = ["x0", "bq0", "bq1", "bk0", "bk1", "x1", "kskw", "qc0", "qc1", "qd0", "cmp", "qd1", "kd", "x2", "x3", "xf"]
NORM_AT = {n: i for i, n in enumerate(NORMS)}
STREAM = {n: i for i, n in enumerate(n for n in NORMS if n[0] == "x")}
Q_NORMS = ("bq0", "bq1", "qc0", "qc1", "qd0", "qd1")
Q_GAIN = dict(b="b_qnorm_g", c="c_qnorm_g", d="d_qnorm_g")
NORM_W = dict(kd=S, cmp=2 * NCMP)


def mixer_kernel(nc, a, out):
    ctx = ExitStack()
    with ctx:
        sems = {}

        def sem(name):
            if name not in sems:
                sems[name] = ctx.enter_context(nc.semaphore(name))
            return sems[name]

        def sb(name, shape, dt=F32):
            return ctx.enter_context(nc.sbuf_tensor(name, shape, dt))

        def over(name, under, at, shape):
            return nc.alloc_sbuf_tensor_at(name, shape, F32R, offset=nc.lookup_mloc(under).addr + 4 * at)

        def cut(ap, n):
            return ap.rearrange("p (k n) -> p k n", n=n)

        def fl(ap):
            return ap.rearrange("p k t -> p (k t)")

        raw = sb("raw", [P, NRAW, UNIT])
        w_lo = over("w_lo", raw, 0, [P, NRAW, UNIT])
        w_hi = sb("w_hi", [P, NHI, UNIT], F32R)
        xT = sb("xT", [P, KD, S])
        parts = sb("parts", [P, 2, KD, S], F32R)
        wide = sb("wide", [P, KD * S])
        cols = sb("cols", [P, N_COLS])
        small = sb("small", [P, sum(SMALL.values())])
        silu_c = sb("silu_c", [P, KD])
        mod = sb("mod", [P, ADA])
        gain1 = sb("gain1", [P, KD])
        gain2 = sb("gain2", [P, KD])
        cmp_bias = sb("cmp_bias", [P, 2, NH, NCMP])
        cos_t = sb("cos_t", [P, S])
        sin_t = sb("sin_t", [P, S])
        dil_bias = sb("dil_bias", [P, AG, AH, S])
        prob2 = sb("prob2", [P, 2, 4, S])
        probT = sb("probT", [P, 2560])
        sq = sb("sq", [P, 512])
        rstd = sb("rstd", [P, 512])
        q_rstd = sb("q_rstd", [P, 3, 2, 8])
        token_rstd = sb("token_rstd", [P, TT])
        stat = sb("stat", [P, 3, 20])
        bn = sb("bn", [P, 2, 10])
        tmp = sb("tmp", [P, 2, 512])
        arena = sb("arena", [P, ARENA])

        ones, ident, sinks = (cols[:, at:at + n] for at, n in ((ONES_AT, P), (IDENT_AT, P), (SINKS_AT, NH)))
        at = np.cumsum([0] + list(SMALL.values())).tolist()
        halves, kw2, vw2, vb2, rel = (small[:, at[i]:at[i + 1]] for i in range(len(SMALL)))
        kw2, vw2, vb2, rel = cut(kw2, 2 * HD), cut(vw2, HD), vb2[0:NCMP], rel[0:32]

        def place(at, *shape):
            n = int(np.prod(shape))
            assert at + n <= ARENA
            v = arena[:, at:at + n]
            if len(shape) == 2:
                return cut(v, shape[1])
            if len(shape) == 3:
                return v.rearrange("p (a b c) -> p a b c", b=shape[1], c=shape[2])
            return v

        alibi = place(0, NH, S)
        swa = place(2048, NH, S)
        ada_acc = place(4096, 6 * D)
        ada_acc2 = place(2048, (ADA_DVE - ADA_FIRST) * P)
        ada_slab = place(10240, 2, KD, P)
        L = 12288
        bqT, bkT, bv = place(L, 4, S), place(L + 1024, 4, S), place(L + 2048, 2, GW)
        hpad = place(L + 3072, 4, PADW)
        yT0 = place(L + 4232, KD, S)
        u_val = cut(wide[:, 0:1024], S)
        slabs = [cut(dil_bias[:].rearrange("p g h j -> p (g h j)")[:, KD * P * i:KD * P * i + KD * P], P)
                 for i in range(3)] + [cut(fl(prob2[:, i]), P) for i in range(2)]
        diags = [fl(prob2[:, i // 8])[:, P * (i % 8):P * (i % 8) + P] if i < 16 else probT[:, P * (i - 16):P * (i - 15)]
                 for i in range(4 * (TAPS - CONV_DVE))]
        qcT, qdT = place(L, 4, S), place(L + 1024, 4, S)
        ksT, kwT, kdT = place(L + 2048, S), place(L + 2304, S), place(L + 2560, S)
        vs, vw, vd = place(L + 2816, 2, P), place(L + 3072, 2, P), place(L + 3328, 2, P)
        gates = place(L + 3584, 2, 24)
        kcn = place(L + 3632, 2 * NCMP)
        vcn = place(L + 3664, P)
        yT1 = place(L + 4232, KD, S)
        kcv = cut(wide[:, 0:512], S)
        pairs = wide[:, 512:1536].rearrange("p (v g t) -> p v g t", v=2, g=2)
        hid_row = cut(wide[0:2 * NCMP, 1536:2048], 2 * P)
        blocks = probT[:, 0:960].rearrange("p (v j n) -> p v j n", v=2, j=16)
        hid_x = probT[:, 960:1080].rearrange("p (v k n) -> p v k n", v=2, k=2)
        yretT = place(0, 16, S)
        rqT, rkT, rv = place(4096, 8, S), place(6144, 8, S), place(8192, 2, RH * RDV)
        av = place(4096, AG, 2, GW)
        gaT, gbT = place(8192, 8, S), place(10240, 8, S)
        aqT, akT = place(12288, AG, AH * S), place(15360, AG, AH * S)
        mT = place(4096, 8, S)
        line = dil_bias[0:AH].rearrange("p g h j -> p (g h j)")[:, 0:AG * LINE].rearrange("p (g u) -> p g u", g=AG)
        linemask = dil_bias[0:AH].rearrange("p g h j -> p (g h j)")[:, AG * LINE:2 * AG * LINE].rearrange("p (g u) -> p g u", g=AG)
        onehot = wide[0:32, 0:AG * LINE].rearrange("p (g u) -> p g u", g=AG)
        ron = cut(probT[:, 0:1024], GW)
        decay = cut(probT[:, 1024:2560], LINE)
        yret_lo = over("yret_lo", arena, 0, [P, 16, S])
        yret_hi = over("yret_hi", arena, 12288, [P, 2, AG, AH * S])
        att_hi = over("att_hi", arena, 7168, [P, AH, S])
        att_lo = over("att_lo", wide, 1024, [P, AH, S])
        hid_hi = over("hid_hi", arena, 0, [P, 32, S])
        hid_lo = over("hid_lo", arena, 8192, [P, 32, S])

        raw_slots = [raw[:, i] for i in range(NRAW)] + [probT[:, 0:UNIT], arena[:, 16384:16384 + UNIT]]
        lo_slots = [w_lo[:, i] for i in range(NRAW)] + \
            [over("w_lo_a", probT, 0, [P, UNIT])[:], over("w_lo_b", arena, 16384, [P, UNIT])[:]]
        hi_slots = [w_hi[:, i] for i in range(NHI)] + \
            [over("w_hi_a", prob2, 0, [P, UNIT])[:], over("w_hi_b", dil_bias, 0, [P, UNIT])[:]]

        def yret_piece(i):
            hh, g = divmod(i, AG)
            return yret_hi[:, :, g, S * hh:S * hh + S]

        YRET_AFTER = {4: (0, 1, 2), 5: (3, 4, 5), 6: (6, 7)}

        def prob(u):
            return cut(wide[:, 0:1024], S) if u % 3 == 2 else prob2[:, u % 3]

        def pT(u, br, r):
            if UNITS[u][0] == "c":
                at = 0 if br == 0 else 512 + 1024 * (br - 1) + 512 * r
            else:
                at = 512 + 1024 * (u % 2) + 512 * r
            return cut(probT[:, at:at + 512], P)

        pp = [ctx.enter_context(nc.psum_tensor(f"proj{i}", [P, 512], F32)) for i in range(NPP)]
        st = ctx.enter_context(nc.psum_tensor("sums", [P, 512], F32))
        sc = [ctx.enter_context(nc.psum_tensor(f"scores{i}", [P, 512], F32)) for i in range(2)]
        pt = ctx.enter_context(nc.psum_tensor("transposed", [P, 512], F32))
        po = ctx.enter_context(nc.psum_tensor("mixed", [P, 512], F32))
        lines_d = nc.dram_tensor("dil_lines", (AG * AH, P, LINE), F32, kind="Internal").ap()

        raw_in = [sem(f"raw_in{i}") for i in range(NRAW + 2)]
        hi_ready, lo_ready = sem("hi_ready"), sem("lo_ready")
        bank_free = [sem(f"bank_free{i}") for i in range(NPP)]
        proj_ready = sem("proj_ready")
        first_in, setup_in = sem("first_in"), sem("setup_in")
        x_in = [sem("x_in0"), sem("x_in1")]
        const_in, rot_in = sem("const_in"), sem("rot_in")
        h_full, h_hi, h_ready = sem("h_full"), sem("h_hi"), sem("h_ready")
        stream_sq = sem("stream_sq")
        norm_sq, norm_sum = sem("norm_sq"), sem("norm_sum")
        norm_var, norm_sqrt, norm_done = sem("norm_var"), sem("norm_sqrt"), sem("norm_done")
        sc_ready, sc_free = sem("sc_ready"), sem("sc_free")
        mx_ready, exp_done, p_ready = sem("mx_ready"), sem("exp_done"), sem("p_ready")
        tr_ready, pt_ready = sem("tr_ready"), sem("pt_ready")
        pv_ready, po_free = sem("pv_ready"), sem("po_free")
        y_hi, y_ready = sem("y_hi"), sem("y_ready")

        def col(name, k=0, n=1):
            return cols[:, COL_AT[name][0] + k:COL_AT[name][0] + k + n]

        def conv_col(c, tap):
            at = CONV_AT + c * TAPS + tap
            return cols[:, at:at + 1]

        def bank(name):
            return pp[GROUP_AT[name] % NPP]

        def evacuated(name):
            m = GROUP_AT[name]
            return bank_free[m % NPP], m // NPP + 1

        def free_of(name):
            return bank_free[GROUP_AT[name] % NPP]

        def norms_before(name):
            return sum(n not in STREAM for n in NORMS[:NORM_AT[name]])

        def rstd_of(name):
            return q_rstd[:, dict(b=0, c=1, d=2)[name[1] if name[0] == "q" else "b"], int(name[2])]

        class Steps:

            def __init__(self, eng, name):
                self.eng, self.sem, self.n = eng, sem(name), 0

            def did(self, ins):
                ins.then_inc(self.sem, 1)
                self.n += 1

            def settle(self):
                self.eng.wait_ge(self.sem, self.n)

        block = ctx.enter_context(nc.Block())

        @block.sync
        def _(sp):
            for i in range(2):
                sp.dma_start(xT[:, 4 * i:4 * i + 4], cut(a["x"], S)[:, 4 * i:4 * i + 4]).then_inc(x_in[i], 16)
            sends = ada_sends()
            for n, u in enumerate(WEIGHTS):
                before = RAW_BEFORE[n]
                if before is not None:
                    sp.wait_ge(proj_ready, LAST_READ[WEIGHTS[before]] + 1)
                elif u == RAW_MORE[0]:
                    sp.wait_ge(po_free, STEPS_TO["a"])
                elif u == RAW_MORE[1]:
                    sp.wait_ge(proj_ready, GROUP_AT["wr3"] + 1)
                size = int(np.prod(unit_shape(u)))
                sp.dma_start(raw_slots[RAW_AT[n]][:, 0:size], a["weights"][n][:, 0:size]).then_inc(raw_in[RAW_AT[n]], 16)
                for j in sends.get(n, []):
                    if SLAB_BEFORE[j] is not None:
                        sp.wait_ge(sem("ada_dve"), SLAB_BEFORE[j] + 1)
                    elif j >= 3:
                        sp.wait_ge(tr_ready, rounds_before(PART["c"][0]))
                    sp.dma_start(slabs[SLAB_AT[j]], a["w_ada"][ADA - ADA_DVE + j].rearrange("p (k n) -> p k n", n=P)) \
                        .then_inc(sem(f"slab_in{SLAB_AT[j]}"), 16)
                if u == "bq1":
                    sp.dma_start(alibi, a["alibi"]).then_inc(const_in, 16)
                if u == "bv1":
                    for dst, src in ((cmp_bias[:], a["cmp_bias"]), (swa, a["swa"])):
                        sp.dma_start(dst, src).then_inc(const_in, 16)
                if u == "wo0_0":
                    for dst, src in ((cos_t[:], a["cos"]), (sin_t[:], a["sin"])):
                        sp.dma_start(dst, src).then_inc(rot_in, 16)
                if u == "rq3":
                    sp.wait_ge(po_free, STEPS_TO["d"])
                    sp.dma_start(decay, a["decay"]).then_inc(sem("decay_in"), 16)
                if u == RET_FILL[3]:
                    sp.wait_ge(h_ready, KD * (STREAM["x2"] + 1))
                    sp.dma_start(onehot, a["onehot"]).then_inc(sem("line_const_in"), 16)
                    sp.wait_ge(sem("ada_dve"), ADA_DVE)
                    sp.dma_start(linemask, a["linemask"]).then_inc(sem("line_const_in"), 16)
                if u == RET_FILL[10]:
                    sp.wait_ge(sem("line_ready"), 1)
                    for g in range(AG):
                        sp.dma_start(lines_d[AH * g:AH * g + AH], line[:, g, :].unsqueeze(1).broadcast_to([AH, P, LINE])) \
                            .then_inc(sem("lines_out"), 16)
                if u == RET_FILL[12]:
                    sp.wait_ge(sem("lines_out"), 16 * AG)
                    flat = lines_d.rearrange("h r u -> (h r u)")
                    skew = bass.AP(flat.tensor, P - 1, [[LINE - 1, P], [P * LINE, AG * AH], [1, S]])
                    sp.dma_start(dil_bias[:].rearrange("p g h j -> p (g h) j"), skew).then_inc(sem("dil_in"), 16)

        @block.gpsimd
        def _(pool):
            ada_in = [sem("ada_in0"), sem("ada_in1")]
            own = Steps(pool, "pool_step")
            state = dict(ada=0)
            n_ada = ADA - ADA_DVE

            def low(u):
                n, m = WEIGHT_AT[u], SPLIT_AT[u]
                kt, w = unit_shape(u)
                pool.wait_ge(hi_ready, m + 1)
                nc.gpsimd.tensor_tensor(lo_slots[RAW_AT[n]][:, 0:kt * w], raw_slots[RAW_AT[n]][:, 0:kt * w],
                                        hi_slots[HI_AT[m]][:, 0:kt * w].bitcast(F32), ALU.subtract).then_inc(lo_ready, 1)

            def ada_block():
                j = state["ada"]
                state["ada"] += 1
                w = ada_slab[:, j % 2]
                pool.wait_ge(ada_in[j % 2], 16 * (j // 2 + 1))
                own.did(nc.gpsimd.tensor_tensor(w, w, silu_c[:].unsqueeze(2).broadcast_to([P, KD, P]), ALU.mult))
                own.settle()
                for half in (4, 2):
                    own.did(nc.gpsimd.tensor_tensor(w[:, 0:half], w[:, 0:half], w[:, half:2 * half], ALU.add))
                    own.settle()
                nc.gpsimd.tensor_tensor(ada_acc[:, P * j:P * j + P], w[:, 0], w[:, 1], ALU.add).then_inc(sem("ada_sum"), 1)
                if j + 2 < n_ada:
                    pool.wait_ge(sem("ada_sum"), j + 1)
                    load(j + 2)

            def load(j):
                pool.dma_start(ada_slab[:, j % 2], cut(a["w_ada"][j], P)).then_inc(ada_in[j % 2], 16)

            assert sum(ADA_POOL.values()) == n_ada
            assert WEIGHTS[0] == SPLIT[0]
            kt, w = unit_shape(SPLIT[0])
            for half, made in enumerate((sem("hi_half"), hi_ready)):
                pool.wait_ge(made, 1)
                at = slice(kt * w // 2 * half, kt * w // 2 * (half + 1))
                ins = nc.gpsimd.tensor_tensor(lo_slots[RAW_AT[0]][:, at], raw_slots[RAW_AT[0]][:, at],
                                              hi_slots[HI_AT[0]][:, at].bitcast(F32), ALU.subtract)
            ins.then_inc(lo_ready, 1)
            for u in SPLIT:
                if u != SPLIT[0]:
                    low(u)
                if u == "bv0":
                    pool.wait_ge(sem("silu_c_ready"), 1)
                    load(0)
                    load(1)
                for _ in range(ADA_POOL.get(u, 0)):
                    ada_block()

        @block.tensor
        def _(pe):
            state = dict(filled=0, norm=0, head=0, stream=0)

            def begin(name):
                m = GROUP_AT[name]
                assert state["filled"] <= m < state["filled"] + NPP, name
                if m >= NPP:
                    pe.wait_ge(bank_free[m % NPP], m // NPP)
                return pp[m % NPP]

            def end(last):
                last.then_inc(proj_ready, 1)
                state["filled"] += 1

            def weight(u):
                n, m = WEIGHT_AT[u], SPLIT_AT[u]
                kt, w = unit_shape(u)
                pe.wait_ge(lo_ready, m + 1)
                return cut(hi_slots[HI_AT[m]][:, 0:kt * w], w), cut(lo_slots[RAW_AT[n]][:, 0:kt * w], w)

            def features(name, hi, lo, chunks, wait=None):
                b = begin(name)
                todo = []
                for j, pieces in enumerate(chunks):
                    for u, c, k0 in pieces:
                        whi, wlo = weight(u)
                        todo += [(j, k0 + k, whi[:, k, c:c + P], wlo[:, k, c:c + P]) for k in range(unit_shape(u)[0])]
                by_k = wait is not None and name[:2] not in ("wr", "f2")
                if by_k:
                    todo.sort(key=lambda x: x[1])
                for i, (j, k, whi, wlo) in enumerate(todo):
                    first = i == 0 or not by_k and todo[i - 1][0] != j
                    stop = i == len(todo) - 1 or not by_k and todo[i + 1][0] != j
                    if wait is not None and (todo[i - 1][1] != k if by_k and i else j == 0):
                        wait(k)
                    dst = b[:, S * j:S * j + S]
                    h = yret_piece(k // 2)[:, k % 2, :] if hi is None else hi[:, k, :]
                    nc.tensor.matmul(dst, whi, h, start=first, stop=False)
                    nc.tensor.matmul(dst, wlo, h, start=False, stop=False)
                    last = nc.tensor.matmul(dst, whi, lo[:, k, :], start=False, stop=stop)
                end(last)

            h_parts = parts[:, 0], parts[:, 1]

            def project(name, fresh=None):
                wait = None if fresh is None else lambda k: pe.wait_ge(h_ready, KD * fresh + k + 1)
                u = UNITS_OF[name][0]
                one = name == "kd"
                features(name, *h_parts, [[(u, P * j, 0)] for j in range(1 if one else 2)], wait)

            def tokens(name, c, n):
                b = begin(name)
                whi, wlo = weight(UNITS_OF[name][0])
                for t in range(TT):
                    for k in range(KD):
                        dst, at = b[:, S * t:S * t + n], slice(P * t, P * t + P)
                        nc.tensor.matmul(dst, parts[:, 0, k, at], whi[:, k, c:c + n], start=k == 0, stop=False)
                        nc.tensor.matmul(dst, parts[:, 0, k, at], wlo[:, k, c:c + n], start=False, stop=False)
                        last = nc.tensor.matmul(dst, parts[:, 1, k, at], whi[:, k, c:c + n], start=False, stop=k == KD - 1)
                end(last)

            def stream_sums(name, lo, hi):
                n = NORM_AT[name]
                assert n == state["norm"]
                for k in range(lo, hi):
                    pe.wait_ge(stream_sq, KD * STREAM[name] + k + 1)
                    if k == 0 and n:
                        pe.wait_ge(norm_done, n)
                    for t in range(TT):
                        c = S * k + P * t
                        last = nc.tensor.matmul(st[:, t:t + 1], wide[:, c:c + P], ones[:, 0:1],
                                                start=k + t == 0, stop=k == KD - 1 and t == TT - 1)
                if hi == KD:
                    last.then_inc(norm_sum, 1)
                    state["norm"] += 1

            def stream_spread(name):
                for t in range(TT):
                    pe.wait_ge(sem("norm_diag"), TT * STREAM[name] + t + 1)
                    last = nc.tensor.matmul(st[:, S + P * t:S + P * t + P], ones, rstd[:, P * t:P * t + P], start=True, stop=True)
                last.then_inc(sem("norm_spread"), 1)

            def head_sums(name):
                n, w = NORM_AT[name], NORM_W.get(name, 512)
                assert n == state["norm"]
                state["norm"] += 1
                pe.wait_ge(norm_sq, norms_before(name) + 1)
                pe.wait_ge(norm_var, n)
                if NORMS[n - 1] in STREAM:
                    pe.wait_ge(norm_done, n)
                if name in Q_NORMS:
                    for i in range(4):
                        t, c = divmod(i, 2)
                        last = nc.tensor.matmul(st[:, 2 * i:2 * i + 2], sq[:, S * c + P * t:S * c + P * t + P],
                                                cut(halves[:], HD)[:, :, 0], start=True, stop=True)
                    last.then_inc(norm_sum, 1)
                else:
                    nc.tensor.matmul(st[:, 0:w], halves[:], sq[:, 0:w], start=True, stop=True).then_inc(norm_sum, 1)

            def scores(u):
                part, step, br, last_br, at, qt, n = UNITS[u]
                if part in "cd" and (u == 0 or UNITS[u - 1][0] != part or br == 0):
                    pe.wait_ge(norm_done, NORM_AT["kd" if part == "d" else "cmp" if br == 0 else "qc1"] + 1)
                if u:
                    pe.wait_ge(sc_free, u)
                if part == "a":
                    for g in range(AG):
                        q = aqT[:, g, S * at + P * qt:S * at + P * qt + P]
                        last = nc.tensor.matmul(sc[g // 2][:, S * (g % 2):S * (g % 2) + n], q,
                                                akT[:, g, S * at:S * at + n], start=True, stop=True)
                else:
                    q = dict(b=bqT, c=qcT, d=qdT)[part]
                    for bi in range(2):
                        for f in range(2):
                            lo, b = HD * f, 2 * at + bi
                            if part == "b":
                                keys = bkT[lo:lo + HD, b, 0:n]
                            elif part == "c" and br == 0:
                                keys = kcn[lo:lo + HD, NCMP * f:NCMP * f + n]
                            else:
                                keys = (kdT if part == "d" else (None, ksT, kwT)[br])[lo:lo + HD, 0:n]
                            last = nc.tensor.matmul(sc[f][:, S * bi:S * bi + n], q[lo:lo + HD, b, P * qt:P * qt + P],
                                                    keys, start=True, stop=True)
                last.then_inc(sc_ready, 1)

            def transposes(u, r):
                part, step, br, last_br, at, qt, n = UNITS[u]
                if r == 0:
                    pe.wait_ge(p_ready, u + 1)
                if rounds_before(u) + r:
                    pe.wait_ge(pt_ready, rounds_before(u) + r)
                for i in range(3 if part == "a" else 4):
                    w = min(n - P * r, P)
                    last = nc.tensor.transpose(pt[0:w, P * i:P * i + P], prob(u)[:, i, P * r:P * r + w], ident[:])
                last.then_inc(tr_ready, 1)

            def mix(u):
                part, step, br, last_br, at, qt, n = UNITS[u]
                pe.wait_ge(pt_ready, rounds_before(u + 1))
                if step:
                    pe.wait_ge(po_free, step)
                if part == "a":
                    todo = [(g, r) for g in range(AG) for r in range(qt + 1)]
                    for i, (g, r) in enumerate(todo):
                        last = nc.tensor.matmul(po[:, 0:P], av[:, g, r, P * at:P * at + P], pT(u, 0, r)[:, g, :],
                                                start=i == 0, stop=i == len(todo) - 1)
                else:
                    for bi in range(2):
                        for f in range(2):
                            b, i4 = 2 * at + bi, 2 * f + bi
                            todo = []
                            for r in range(qt + 1):
                                if part == "b":
                                    h = 2 * b + f
                                    todo.append((bv[:, r, HD * h:HD * h + HD], pT(u, 0, r)[:, i4, :]))
                                elif part == "d":
                                    todo.append((vd[:, r, HD * f:HD * f + HD], pT(u, 0, r)[:, i4, :]))
                                else:
                                    todo += [(v[:, r, HD * f:HD * f + HD], pT(u, x, r)[:, i4, :]) for x, v in ((1, vs), (2, vw))]
                            if part == "c":
                                todo.append((vcn[0:NCMP, HD * f:HD * f + HD], pT(u, 0, 0)[0:NCMP, i4, :]))
                            for i, (v, p) in enumerate(todo):
                                last = nc.tensor.matmul(po[HD * f:HD * f + HD, P * bi:P * bi + P], v, p,
                                                        start=i == 0, stop=i == len(todo) - 1)
                last.then_inc(pv_ready, 1)

            def token_sums(chunks, done):
                for c in range(4):
                    last = nc.tensor.matmul(st[:, 0:S], ones[:], chunks[:, c, :], start=c == 0, stop=c == 3)
                last.then_inc(sem(done), 1)

            def convolution(i):
                b = begin(f"conv{i}")
                for j in range(2):
                    c = 2 * i + j
                    for k in range(TAPS - CONV_DVE):
                        tap = CONV_DVE + k
                        last = nc.tensor.matmul(b[:, S * j:S * j + S], diags[4 * k + c], hpad[:, c, tap:tap + S],
                                                start=k == 0, stop=tap == TAPS - 1)
                end(last)

            def between(name):
                if name[:2] == "S:":
                    head_sums(name[2:])
                elif name[:2] == "M:":
                    modulation(int(name[2:]))
                elif name == "L:mean":
                    pe.wait_ge(sem("conv_done"), 1)
                    token_sums(yT0[:, 0:4], "ln_mean")
                elif name == "L:sq":
                    pe.wait_ge(sem("ln_sq"), 1)
                    token_sums(cut(wide[:, 1024:2048], S), "ln_sum")
                elif "." in name:
                    chunk(*name.split("."))
                elif name[1] != ":":
                    project(name)

            def output_half(name, half, pieces):
                b = bank(name) if half else begin(name)
                whi, wlo = weight(name)
                for k in range(KD // 2 * half, KD // 2 * (half + 1)):
                    pe.wait_ge(y_ready, pieces + k // 2 + 1)
                    for j in range(2):
                        dst, c = b[:, S * j:S * j + S], P * j
                        nc.tensor.matmul(dst, whi[:, k, c:c + P], h_parts[0][:, k, :], start=k == 0 and j == 0, stop=False)
                        nc.tensor.matmul(dst, wlo[:, k, c:c + P], h_parts[0][:, k, :], start=False, stop=False)
                        last = nc.tensor.matmul(dst, whi[:, k, c:c + P], h_parts[1][:, k, :], start=False, stop=k == KD - 1 and j == 1)
                if half:
                    end(last)

            def chunk(name, j):
                b, c = begin(name) if j == "0" else bank(name), P * int(j)
                whi, wlo = weight(name)
                for k in range(KD):
                    dst = b[:, 2 * c:2 * c + S]
                    nc.tensor.matmul(dst, whi[:, k, c:c + P], h_parts[0][:, k, :], start=k == 0, stop=False)
                    nc.tensor.matmul(dst, wlo[:, k, c:c + P], h_parts[0][:, k, :], start=False, stop=False)
                    last = nc.tensor.matmul(dst, whi[:, k, c:c + P], h_parts[1][:, k, :], start=False, stop=k == KD - 1)
                if c + P == unit_shape(name)[1]:
                    end(last)

            def attention(units, fill):
                scores(units[0])
                scores(units[1])
                for i, u in enumerate(units):
                    if i + 2 < len(units):
                        scores(units[i + 2])
                    before, after = around(fill[i])
                    for name in before:
                        between(name)
                    transposes(u, 0)
                    for name in after:
                        between(name)
                    if i and UNITS[u - 1][3]:
                        mix(u - 1)
                    if key_tiles(u) == 2:
                        transposes(u, 1)
                mix(units[-1])

            def mod_columns(name, lo, hi, last_part=True):
                b = bank(name)
                for j in range(lo, hi):
                    k = j - (ADA - ADA_DVE + ADA_FIRST)
                    acc = ada_acc[:, P * j:P * j + P] if k < 0 else ada_acc2[:, P * k:P * k + P]
                    last = nc.tensor.matmul(b[:, j:j + 1], acc, ones[:, 0:1], start=True, stop=True)
                if last_part:
                    end(last)

            def modulation(q):
                if q == 0:
                    pe.wait_ge(sem("ada_sum"), ADA_ONE)
                    begin("modA")
                mod_columns("modA", ADA_ONE // 4 * q, ADA_ONE // 4 * (q + 1), q == 3)

            pe.wait_ge(first_in, 16)
            pe.wait_ge(sem("x_folded"), 1)
            for k in range(2):
                for t in range(TT):
                    last = nc.tensor.matmul(st[:, t:t + 1], wide[:, S * k + P * t:S * k + P * t + P], ones[:, 0:1],
                                            start=k + t == 0, stop=k + t == TT)
            last.then_inc(norm_sum, 1)
            state["norm"] += 1
            stream_spread("x0")
            project("uv0", fresh=0)
            for name in ("uv1", "ug0", "ug1", "bq0", "bq1"):
                project(name)
            pe.wait_ge(setup_in, 16)
            head_sums("bq0")
            project("bk0")
            head_sums("bq1")
            project("bk1")
            head_sums("bk0")
            tokens("bv0", 0, 256)
            head_sums("bk1")
            tokens("bv1", 0, 256)
            pe.wait_ge(sem("diags_ready"), len(diags))
            pe.wait_ge(sem("hpad_ready"), 2)
            convolution(0)
            convolution(1)
            pe.wait_ge(norm_done, NORM_AT["bk1"] + 1)
            pe.wait_ge(*evacuated("bv1"))
            attention(PART["b"], FILL_B)

            def output(layer, stream, pieces, between=lambda i: None, begun=()):
                for i in begun:
                    output_half(f"wo{layer}_{i}", 0, pieces)
                for i in range(4):
                    wait = (lambda k: pe.wait_ge(y_ready, pieces + k // 2 + 1)) if i == 0 else None
                    u = f"wo{layer}_{i}"
                    if i == 3:
                        between(0)
                    if i in begun:
                        output_half(u, 1, pieces)
                    else:
                        features(u, *h_parts, [[(u, P * j, 0)] for j in range(2)], wait)
                    if i:
                        stream_sums(stream, 2 * i - 2, 2 * i)
                between(1)
                stream_sums(stream, 6, 8)
                between(2)
                stream_spread(stream)
                between(3)

            output(0, "x1", 0)

            project("kcvc", fresh=1)
            project("kskw")
            tokens("vsvw", 0, 2 * P)
            head_sums("kskw")
            project("qc0")
            project("qc1")
            head_sums("qc0")
            tokens("vdgt", 0, P + 24)
            head_sums("qc1")
            pe.wait_ge(sem("blocks_ready"), 4)

            def hidden_rows(v, name, group):
                b = begin(group)
                for nb in range(2):
                    n = WEIGHT_AT[f"{name}{nb}"]
                    pe.wait_ge(raw_in[RAW_AT[n]], raw_target(n))
                    w = cut(raw_slots[RAW_AT[n]], 2 * P)
                    for j in range(8):
                        last = nc.tensor.matmul(b[0:2 * NCMP, 0:2 * P], blocks[:, v, 8 * nb + j, :], w[:, j, :],
                                                start=nb + j == 0, stop=nb == 1 and j == 7)
                end(last)

            def hidden_columns(v, name, group):
                pe.wait_ge(*evacuated(group))
                b = begin(name)
                for k in range(2):
                    last = nc.tensor.transpose(b[:, 32 * k:32 * k + 30], hid_row[:, v, P * k:P * k + P], ident[0:2 * NCMP, 0:2 * NCMP])
                end(last)

            hidden_rows(0, "ck", "hidk")
            project("qd0")
            hidden_columns(0, "hTk", "hidk")
            hidden_rows(1, "cv", "hidv")
            head_sums("qd0")
            pe.wait_ge(*evacuated("hTk"))
            b = begin("kc2")
            for k in range(2):
                last = nc.tensor.matmul(b[:, 0:30], kw2[:, k], hid_x[:, 0, k, :],
                                        start=k == 0, stop=k == 1)
            end(last)
            hidden_columns(1, "hTv", "hidv")
            project("zc0")
            head_sums("cmp")
            pe.wait_ge(*evacuated("hTv"))
            b = begin("vc2")
            for g in range(2):
                for k in range(2):
                    last = nc.tensor.matmul(b[0:NCMP, HD * g:HD * g + HD], hid_x[:, 1, k, NCMP * g:NCMP * g + NCMP],
                                            vw2[:, k, :], start=k == 0, stop=k == 1)
            end(last)
            pe.wait_ge(*evacuated("vsvw"))
            pe.wait_ge(*evacuated("vdgt"))
            pe.wait_ge(*evacuated("vc2"))
            attention(PART["c"] + PART["d"], FILL_CD)

            def modulation_rest(i):
                if i == 0:
                    pe.wait_ge(sem("ada_sum"), ADA - ADA_DVE)
                    pe.wait_ge(sem("ada_dve"), ADA_FIRST)
                    begin("modB")
                lo, n = ADA_ONE, ADA - ADA_DVE + ADA_FIRST - ADA_ONE
                cuts = [lo, lo + n // 4, lo + n // 2, lo + 3 * n // 4, lo + n]
                mod_columns("modB", cuts[i], cuts[i + 1], i == 3)

            output(1, "x2", 4, modulation_rest, (0, 1))

            project("rq0", fresh=2)
            for name in [f"rq{i}" for i in range(1, 4)] + [f"rk{i}" for i in range(4)]:
                project(name)
            for i in range(8):
                tokens(f"rv{i}", 0, 256)
            def dilated_fill(name):
                if name[1] == "v":
                    tokens(name, 0, 256)
                else:
                    project(name)

            for h in range(RH):
                pe.wait_ge(*evacuated(f"rk{h}"))
                if h >= 2:
                    pe.wait_ge(sem("ret_decayed"), h - 1)
                for jt in range(2):
                    n, at = (S, 0) if jt == 0 else (P, S)
                    for k in range(2):
                        last = nc.tensor.matmul(sc[h % 2][:, at:at + n], rkT[:, 2 * h + k, P * jt:P * jt + P],
                                                rqT[:, 2 * h + k, S - n:S], start=k == 0, stop=k == 1)
                last.then_inc(sem("ret_scores"), 1)
                for i in range(2):
                    dilated_fill(RET_FILL[4 * h + i])
                pe.wait_ge(sem("ret_decayed"), h + 1)
                pe.wait_ge(*evacuated(f"rv{2 * h + 1}"))
                if h:
                    pe.wait_ge(sem("ret_normed"), 2 * h)
                e = prob2[:, h % 2].rearrange("p i j -> p (i j)")
                for t, dst in enumerate((pt, po)):
                    for jt in range(t + 1):
                        at = P * t if jt == 0 else S
                        last = nc.tensor.matmul(dst[:], e[:, at:at + P], rv[:, jt, RDV * h:RDV * h + RDV],
                                                start=jt == 0, stop=jt == t)
                    last.then_inc(sem("ret_out"), 1)
                for i in range(2, 4):
                    dilated_fill(RET_FILL[4 * h + i])
                pe.wait_ge(sem("ret_normed"), 2 * h + 2)
                for half in range(2):
                    b = begin(f"rt{h}_{half}")
                    for j in range(2):
                        for t in range(TT):
                            c = P * (2 * half + j)
                            last = nc.tensor.transpose(b[:, S * j + P * t:S * j + P * t + P], ron[:, t, c:c + P], ident[:])
                    end(last)
                if h == 0:
                    pe.wait_ge(sem("ada_dve"), ADA_DVE)
                    begin("modC")
                    mod_columns("modC", ADA - ADA_DVE + ADA_FIRST, ADA)
                    pe.wait_ge(sem("line_const_in"), 32)
                    for g in range(AG):
                        b = begin(f"dl{g}")
                        end(nc.tensor.matmul(b[0:AH, 0:LINE], rel[:, AH * g:AH * g + AH], onehot[:, g, :], start=True, stop=True))
            for name in RET_FILL[16:]:
                dilated_fill(name)

            pe.wait_ge(*evacuated("av2_1"))
            attention(PART["a"], FILL_A)

            for name in BRANCHES:
                i = int(name[2])
                if name[1] == "r":
                    wait = (lambda k: pe.wait_ge(y_ready, 8 + k // 2 + 1)) if i == 0 else None
                    features(name, None, yret_lo, [[(f"{name}{x}", 0, 0)] for x in "ab"], wait)
                else:
                    pe.wait_ge(po_free, STEPS_TO["a"])
                    features(name, att_hi, att_lo, [[(f"wa{i // 2}", 256 * (i % 2) + P * j, 0)] for j in range(2)])
            output(2, "x3", 16)

            for i in range(16):
                project(f"f1_{i}", fresh=3 if i == 0 else None)
            for i in range(8):
                wait = (lambda k: pe.wait_ge(sem("hid_ready"), k // 2 + 1)) if i == 0 else None
                features(f"f2_{i}", hid_hi, hid_lo, [[(f"f2_{i}a", 0, 0), (f"f2_{i}b", 0, 16)]], wait)
                if i:
                    stream_sums("xf", i - 1, i)
            stream_sums("xf", 7, 8)
            stream_spread("xf")
            assert state["filled"] == len(GROUPS) and state["norm"] == len(NORMS)

        @block.scalar
        def _(act):
            state = dict(hi=0)

            def passing(name, most=len(SPLIT)):
                def left(units, before):
                    if before is None:
                        return n < NRAW or GROUP_AT[name] >= GROUP_AT["wr0"]
                    return LAST_READ[units[before]] < GROUP_AT[name]

                while state["hi"] < min(len(SPLIT), most):
                    m = state["hi"]
                    v = SPLIT[m]
                    n = WEIGHT_AT[v]
                    if not (left(SPLIT, HI_BEFORE[m]) and (n < NRAW or left(WEIGHTS, RAW_BEFORE[n]))):
                        break
                    kt, w = unit_shape(v)
                    if HI_BEFORE[m] is not None:
                        act.wait_ge(proj_ready, LAST_READ[SPLIT[HI_BEFORE[m]]] + 1)
                    elif v in HI_MORE:
                        act.wait_ge(po_free, STEPS_TO["a"])
                    act.wait_ge(raw_in[RAW_AT[n]], raw_target(n))
                    nc.scalar.activation(hi_slots[HI_AT[m]][:, 0:kt * w], raw_slots[RAW_AT[n]][:, 0:kt * w], ACT.Copy) \
                        .then_inc(hi_ready, 1)
                    state["hi"] += 1

            def ready(name, ahead=True):
                if ahead:
                    passing(name)
                act.wait_ge(proj_ready, GROUP_AT[name] + 1)
                return bank(name)

            def copy_out(name, dst, fn=ACT.Copy, scale=1.0):
                b = ready(name)
                nc.scalar.activation(dst, b[:], fn, scale=scale).then_inc(free_of(name), 1)

            def copy_tokens(name, dst, n=256, fn=ACT.Copy):
                b = ready(name)
                nc.scalar.activation(dst, cut(b[:], S)[:, :, 0:n], fn).then_inc(free_of(name), 1)

            def head_squares(name, dst):
                w = NORM_W.get(name, 512)
                b = ready(name)
                act.wait_ge(norm_sum, NORM_AT[name])
                nc.scalar.activation(sq[:, 0:w], b[:, 0:w], ACT.Square).then_inc(norm_sq, 1)
                if name in Q_NORMS:
                    nc.scalar.activation(dst, b[:], ACT.Copy, scale=col(Q_GAIN[name[1] if name[0] == "q" else "b"])) \
                        .then_inc(free_of(name), 1)
                else:
                    nc.scalar.activation(dst, b[:, 0:w], ACT.Copy).then_inc(free_of(name), 1)

            def root(name):
                v = token_rstd[:] if name in STREAM else rstd_of(name) if name in Q_NORMS else rstd[:, 0:NORM_W.get(name, 512)]
                act.wait_ge(norm_var, NORM_AT[name] + 1)
                nc.scalar.activation(v, v, ACT.Sqrt).then_inc(norm_sqrt, 1)

            def table(fn):
                nc.scalar.activation(stat[:, 2, 19:20], ones[:, 0:1], fn).then_inc(sem("table"), 1)
                state["table"] = state.get("table", 0) + 1
                act.wait_ge(sem("table"), state["table"])

            def stream_squares(lo, hi, after):
                act.wait_ge(*(evacuated(after) if isinstance(after, str) else after))
                for k in range(lo, hi):
                    nc.scalar.activation(wide[:, S * k:S * k + S], xT[:, k, :], ACT.Square).then_inc(stream_sq, 1)

            def high_parts(name, shift=None):
                n = STREAM[name]
                for k in range(KD):
                    act.wait_ge(h_full, KD * n + k + 1)
                    h = wide[:, S * k:S * k + S]
                    if shift is None:
                        ins = nc.scalar.activation(parts[:, 0, k, :], h, ACT.Copy)
                    else:
                        ins = nc.scalar.activation(parts[:, 0, k, :], h, ACT.Identity, bias=mod[:, shift + k:shift + k + 1])
                    ins.then_inc(h_hi, 1)

            def exps(u):
                part, step, br, last_br, at, qt, n = UNITS[u]
                act.wait_ge(mx_ready, u + 1)
                s, e = stat[:, u % 3], prob(u)
                if part == "a":
                    nc.scalar.activation(e[:, 0:AG, 0:n], e[:, 0:AG, 0:n], ACT.Exp, bias=s[:, 4:5],
                                         accum_out=s[:, 8:9]).then_inc(exp_done, 1)
                    return
                for i in range(4):
                    last = nc.scalar.activation(e[:, i, 0:n], e[:, i, 0:n], ACT.Exp, bias=s[:, 4 + i:5 + i],
                                                accum_out=s[:, 8 + i:9 + i])
                if part == "d":
                    last = nc.scalar.activation(s[:, 12:16], s[:, 12:16], ACT.Exp)
                last.then_inc(exp_done, 1)

            def transposed_out(u, rounds):
                part, step, br, last_br, at, qt, n = UNITS[u]
                m = 3 if part == "a" else 4
                for r in rounds:
                    act.wait_ge(tr_ready, rounds_before(u) + r + 1)
                    old = step if part == "c" or "c" in (UNITS[max(u - 1, 0)][0], UNITS[max(u - 2, 0)][0]) else step - 1
                    if old > 0:
                        act.wait_ge(pv_ready, old)
                    w = min(n - P * r, P)
                    nc.scalar.activation(pT(u, br, r)[0:w, 0:m, :], cut(pt[0:w, 0:P * m], P), ACT.Copy).then_inc(pt_ready, 1)

            two = lambda t, i: fl(t[:, 2 * i:2 * i + 2])
            hi_of = lambda i: fl(parts[:, 0, 2 * i:2 * i + 2])

            def between(name):
                if "." in name:
                    return
                if name[:2] == "Y:":
                    operand_high([(hi_of(i), two(yT1, i), [(po_free, STEPS_TO["c"])]) for i in range(2)])
                    passing("wo1_0")
                    return
                if name[:2] == "E:":
                    name = name[2:]
                if name[:2] == "S:":
                    root(name[2:])
                elif name[0] == "z":
                    i = int(name[2])
                    dst = tmp[:, i] if name[1] == "a" else \
                        fl((yT0 if name[1] == "b" else yT1)[:, (0 if name[1] == "c" else 4) + 2 * i:][:, 0:2])
                    copy_out(name, dst, fn=ACT.Silu)
                elif name == "L:mean":
                    act.wait_ge(sem("ln_centred"), 1)
                    nc.scalar.activation(wide[:, 1024:2048], fl(yT0[:, 0:4]), ACT.Square).then_inc(sem("ln_sq"), 1)
                elif name == "L:sq":
                    act.wait_ge(sem("ln_var"), 1)
                    nc.scalar.activation(rstd[:, 0:S], rstd[:, 0:S], ACT.Sqrt).then_inc(sem("ln_sqrt"), 1)
                elif name == "L:act":
                    act.wait_ge(sem("ln_scaled"), 1)
                    for c in range(4):
                        nc.scalar.activation(wide[:, 1024 + S * c:1024 + S * c + S], yT0[:, c, :], ACT.Silu, bias=col("a_ln_b", c),
                                             scale=col("a_ln_g", c)).then_inc(sem("ln_silu"), 1)
                elif name in ("qd1", "kd"):
                    head_squares(name, kdT if name == "kd" else fl(qdT[:, 2:4]))
                elif name[:2] == "rg":
                    i = int(name[2])
                    if i >= 2:
                        act.wait_ge(sem("rg_done"), i - 1)
                    copy_out(name, tmp[:, i % 2], fn=ACT.Silu)
                elif name[0] == "g":
                    i = int(name[2])
                    copy_out(name, fl((gaT if name[1] == "a" else gbT)[:, 2 * i:2 * i + 2]), fn=ACT.Sigmoid)

            def attention(units, fill):
                exps(units[0])
                for i, u in enumerate(units):
                    before, after = around(fill[i])
                    for name in before + after:
                        if name[1] != ":":
                            passing(name.split(".")[0])
                    if i + 1 < len(units):
                        exps(units[i + 1])
                    for name in before:
                        between(name)
                    transposed_out(u, [0])
                    for name in after:
                        between(name)
                    transposed_out(u, range(1, key_tiles(u)))
                    if UNITS[u][0] == "a":
                        operand_high([(yret_piece(j), yretT[:, 2 * j:2 * j + 2], [(sem("rg_done"), j + 1), (sc_ready, PART["a"][2 * (j // AG) + 1] + 1)])
                                      for j in YRET_AFTER.get(i, ())])

            def operand_high(pieces):
                for i, (dst, src, wait) in enumerate(pieces):
                    for w in wait:
                        act.wait_ge(*w)
                    nc.scalar.activation(dst, src, ACT.Copy).then_inc(y_hi, 1)

            act.dma_start(cols[:], a["vectors"]).then_inc(first_in, 16)
            act.wait_ge(first_in, 16)
            nc.scalar.activation(silu_c[:], col("c_2", 0, 8), ACT.Silu).then_inc(sem("silu_c_ready"), 1)
            for i in range(2):
                stream_squares(4 * i, 4 * i + 4, (x_in[i], 16))
            table(ACT.Sqrt)
            act.wait_ge(raw_in[RAW_AT[0]], raw_target(0))
            kt, w = unit_shape(SPLIT[0])
            for half, signal in enumerate((sem("hi_half"), hi_ready)):
                at = slice(kt * w // 2 * half, kt * w // 2 * (half + 1))
                nc.scalar.activation(hi_slots[HI_AT[0]][:, at], raw_slots[RAW_AT[0]][:, at], ACT.Copy).then_inc(signal, 1)
            state["hi"] += 1
            act.dma_start(small[:], a["small"]).then_inc(setup_in, 16)

            root("x0")
            passing("uv0", 2)
            high_parts("x0")
            table(ACT.Sigmoid)
            copy_out("uv0", wide[:, 0:512])
            copy_out("uv1", wide[:, 512:1024])
            copy_out("ug0", tmp[:, 0], fn=ACT.Sigmoid)
            copy_out("ug1", tmp[:, 1], fn=ACT.Sigmoid)
            table(ACT.Sqrt)
            head_squares("bq0", fl(bqT[:, 0:2]))
            head_squares("bq1", fl(bqT[:, 2:4]))
            root("bq0")
            head_squares("bk0", fl(bkT[:, 0:2]))
            root("bq1")
            head_squares("bk1", fl(bkT[:, 2:4]))
            root("bk0")
            root("bk1")
            copy_tokens("bv0", bv[:, :, 0:256])
            copy_tokens("bv1", bv[:, :, 256:512])
            table(ACT.Exp)
            attention(PART["b"], FILL_B)
            passing("wo0_0")
            operand_high([(hi_of(i), two(yT0, i), [(sem("y_a_ready"), i + 1)] if i < 2 else
                           [(po_free, STEPS_TO["b"])]) for i in range(4)])
            table(ACT.Sqrt)

            def output_squares(layer, stream):
                for i in range(4):
                    passing(f"wo{layer}_{i}")
                    stream_squares(2 * i, 2 * i + 2, f"wo{layer}_{i}")
                root(stream)

            output_squares(0, "x1")

            high_parts("x1")
            copy_out("kcvc", fl(kcv))
            act.wait_ge(*evacuated("kcvc"))
            for f in range(2):
                for g in range(2):
                    act.dma_start(pairs[HD * f:HD * f + HD, :, g, 0:S - f], kcv[HD * g:HD * g + HD, :, f:S]) \
                        .then_inc(sem("pairs_in"), 16)
            head_squares("kskw", arena[:, L + 2048:L + 2560])
            values = cut(ready("vsvw")[:], S)
            nc.scalar.activation(vs, values[:, :, 0:P], ACT.Copy).then_inc(sem("vs_ready"), 1)
            nc.scalar.activation(vw, values[:, :, P:2 * P], ACT.Copy).then_inc(free_of("vsvw"), 1)
            root("kskw")
            head_squares("qc0", fl(qcT[:, 0:2]))
            head_squares("qc1", fl(qcT[:, 2:4]))
            root("qc0")
            b = cut(ready("vdgt")[:], S)
            nc.scalar.activation(vd, b[:, :, 0:P], ACT.Copy).then_inc(sem("vd_ready"), 1)
            root("qc1")
            nc.scalar.activation(gates, b[:, :, P:P + 24], ACT.Sigmoid).then_inc(free_of("vdgt"), 1)

            def hidden_silu(v, group, bias):
                b = ready(group, False)
                for k in range(2):
                    last = nc.scalar.activation(hid_x[:, v, k, :], b[:, 32 * k:32 * k + 30], ACT.Silu, bias=col(bias, k))
                last.then_inc(free_of(group), 1)

            def hidden_copy(v, group):
                b = ready(group, v == 0)
                nc.scalar.activation(hid_row[:, v, :], b[0:2 * NCMP, 0:2 * P], ACT.Copy).then_inc(free_of(group), 1)

            hidden_copy(0, "hidk")
            head_squares("qd0", fl(qdT[:, 0:2]))
            hidden_silu(0, "hTk", "c_k_b1")
            hidden_copy(1, "hidv")
            b = ready("kc2", False)
            nc.scalar.activation(kcn, b[:, 0:30], ACT.Identity, bias=col("c_k_b2")).then_inc(free_of("kc2"), 1)
            act.wait_ge(*evacuated("kc2"))
            act.wait_ge(norm_sum, NORM_AT["cmp"])
            nc.scalar.activation(sq[:, 0:30], kcn, ACT.Square).then_inc(norm_sq, 1)
            hidden_silu(1, "hTv", "c_v_b1")
            table(ACT.Sqrt)
            root("qd0")
            root("cmp")
            between("zc0")
            table(ACT.Exp)
            attention(PART["c"] + PART["d"], FILL_CD)
            operand_high([(hi_of(i), two(yT1, i), [(po_free, STEPS_TO["d"])]) for i in range(2, 4)])
            table(ACT.Sqrt)
            output_squares(1, "x2")

            high_parts("x2", 0)
            for name in [f"rq{i}" for i in range(4)] + [f"rk{i}" for i in range(4)]:
                passing(name)
            for i in range(8):
                copy_tokens(f"rv{i}", rv[:, :, 256 * i:256 * i + 256])

            def dilated_out(name):
                g, i = int(name[2]), int(name[-1])
                if name[1] == "v":
                    copy_tokens(name, av[:, g, :, 256 * i:256 * i + 256])
                else:
                    copy_out(name, (aqT if name[1] == "q" else akT)[:, g, 512 * i:512 * i + 512],
                             scale=P ** -0.5 if name[1] == "q" else 1.0)

            for h in range(RH):
                for i in range(2):
                    dilated_out(RET_FILL[4 * h + i])
                passing(RET_FILL[4 * h + 2])
                for t in range(TT):
                    act.wait_ge(sem("ret_var"), 2 * h + t + 1)
                    nc.scalar.activation(bn[:, t, 8:9], bn[:, t, 8:9], ACT.Sqrt).then_inc(sem("ret_sqrt"), 1)
                for i in range(2, 4):
                    dilated_out(RET_FILL[4 * h + i])
                for half in range(2):
                    b = ready(f"rt{h}_{half}")
                    for j in range(2):
                        c = 4 * h + 2 * half + j
                        last = nc.scalar.activation(yretT[:, c, :], b[:, S * j:S * j + S], ACT.Identity,
                                                    bias=col("ret_gn_b_2", c), scale=col("ret_gn_g_2", c))
                    last.then_inc(free_of(f"rt{h}_{half}"), 1)
            for name in RET_FILL[16:]:
                dilated_out(name)
            attention(PART["a"], FILL_A)
            merged_high = lambda pieces: operand_high([(hi_of(i), two(mT, i), [(sem("merged"), i + 1)]) for i in pieces])
            for name in BRANCHES:
                if name == BRANCHES[-1]:
                    merged_high(range(3))
                passing(name)
            merged_high(range(3, 4))
            table(ACT.Sqrt)
            output_squares(2, "x3")
            high_parts("x3", 24)
            for i in range(16):
                if i >= 2:
                    act.wait_ge(sem("hid_ready"), i - 1)
                copy_out(f"f1_{i}", tmp[:, i % 2], fn=ACT.Relu)
                act.wait_ge(*evacuated(f"f1_{i}"))
                nc.scalar.activation(two(hid_hi, i), tmp[:, i % 2], ACT.Square).then_inc(sem("hid_high"), 1)
            for i in range(8):
                passing(f"f2_{i}")
                stream_squares(i, i + 1, f"f2_{i}")
            root("xf")
            for i in range(4):
                act.wait_ge(h_full, KD * 4 + 2 * i + 2)
                act.dma_start(out[:, 512 * i:512 * i + 512], wide[:, 512 * i:512 * i + 512]).then_inc(sem("stored"), 16)
            act.wait_ge(sem("stored"), 64)

        @block.vector
        def _(dve):
            own = Steps(dve, "dve_step")
            V = nc.vector

            def ready(name):
                dve.wait_ge(proj_ready, GROUP_AT[name] + 1)
                return bank(name)

            def variance(name):
                n = NORM_AT[name]
                w = NORM_W.get(name, 512)
                dve.wait_ge(norm_sum, n + 1)
                if n:
                    dve.wait_ge(norm_done, n)
                if name in Q_NORMS:
                    V.tensor_scalar(rstd_of(name), st[:, 0:8], HD * EPS, None, ALU.add).then_inc(norm_var, 1)
                    return
                if name in STREAM:
                    V.tensor_scalar(token_rstd[:], st[:, 0:TT], 1.0 / D, EPS, ALU.mult, ALU.add).then_inc(norm_var, 1)
                    return
                V.tensor_scalar(rstd[:, 0:w], st[:, 0:w], 1.0 / HD, EPS, ALU.mult, ALU.add).then_inc(norm_var, 1)

            def inverse(name, w):
                dve.wait_ge(norm_sqrt, NORM_AT[name] + 1)
                own.did(V.reciprocal(rstd[:, 0:w], rstd[:, 0:w]))
                own.settle()

            def stream_norm(name, gain, shift=None, split=True):
                n = STREAM[name]

                def low(k):
                    dve.wait_ge(h_hi, KD * n + k + 1)
                    h, hi = wide[:, S * k:S * k + S], parts[:, 0, k, :].bitcast(F32)
                    if shift is None:
                        ins = V.tensor_tensor(parts[:, 1, k, :], h, hi, ALU.subtract)
                    else:
                        ins = V.scalar_tensor_tensor(parts[:, 1, k, :], h, mod[:, shift + k:shift + k + 1], hi, ALU.add, ALU.subtract)
                    ins.then_inc(h_ready, 1)

                variance(name)
                dve.wait_ge(norm_sqrt, NORM_AT[name] + 1)
                own.did(V.reciprocal(token_rstd[:], token_rstd[:]))
                own.settle()
                for t in range(TT):
                    V.tensor_scalar(rstd[:, P * t:P * t + P], ident, token_rstd[:, t:t + 1], None, ALU.mult) \
                        .then_inc(sem("norm_diag"), 1)
                dve.wait_ge(sem("norm_spread"), n + 1)
                for k in range(KD):
                    V.scalar_tensor_tensor(wide[:, S * k:S * k + S], xT[:, k, :], gain[:, k:k + 1], st[:, S:2 * S],
                                           ALU.mult, ALU.mult).then_inc(h_full, 1)
                    if split and k >= 2:
                        low(k - 2)
                if split:
                    low(KD - 2)
                    low(KD - 1)
                V.tensor_copy(bn[:, 0, 9:10], st[:, S:S + 1]).then_inc(norm_done, 1)

            def head_norm_end(name, src, dst, gain):
                w = NORM_W.get(name, 512)
                if name in Q_NORMS:
                    dve.wait_ge(norm_sqrt, NORM_AT[name] + 1)
                    dve.wait_ge(*evacuated(src))
                    V.reciprocal(rstd_of(name), rstd_of(name)).then_inc(norm_done, 1)
                    return
                inverse(name, w)
                dve.wait_ge(*evacuated(src))
                if name == "kskw":
                    own.did(V.scalar_tensor_tensor(ksT, ksT, col("c_knorm_slc_g"), rstd[:, 0:S], ALU.mult, ALU.mult))
                    V.scalar_tensor_tensor(kwT, kwT, col("c_knorm_win_g"), rstd[:, S:2 * S], ALU.mult, ALU.mult).then_inc(norm_done, 1)
                    return
                V.scalar_tensor_tensor(dst, dst, col(gain), rstd[:, 0:w], ALU.mult, ALU.mult).then_inc(norm_done, 1)

            def score_max(u):
                part, step, br, last_br, at, qt, n = UNITS[u]
                e, s = prob(u), stat[:, u % 3]
                dve.wait_ge(sc_ready, u + 1)
                if u >= 3:
                    dve.wait_ge(tr_ready, rounds_before(u - 2))
                if part != "a":
                    dve.wait_ge(norm_done, NORM_AT[f"{'bq' if part == 'b' else 'q' + part}{at}"] + 1)
                if part == "a":
                    for g in range(AG):
                        ins = V.tensor_tensor_reduce(out=e[:, g, 0:n], in0=sc[g // 2][:, S * (g % 2):S * (g % 2) + n],
                                                     in1=dil_bias[:, g, at, S - n:S], scale=1.0, scalar=-3e38,
                                                     op0=ALU.add, op1=ALU.max, accum_out=s[:, g:g + 1])
                    ins.then_inc(sc_free, 1)
                    dve.wait_ge(sc_free, u + 1)
                    V.tensor_reduce(s[:, 4:5], s[:, 0:3], AX.X, ALU.max, negate=True).then_inc(mx_ready, 1)
                    return
                for i in range(4):
                    f, bi = divmod(i, 2)
                    h = 2 * (2 * at + bi) + f if part == "b" else 2 * at + bi + 4 * f
                    bias = cmp_bias[:, qt, h, :] if part == "c" and br == 0 else (swa if part == "d" else alibi)[:, h, S - n:S]
                    i8 = 4 * qt + 2 * bi + f
                    ins = V.scalar_tensor_tensor(e[:, i, 0:n], sc[f][:, S * bi:S * bi + n],
                                                 q_rstd[:, "bcd".index(part), at, i8:i8 + 1], bias, ALU.mult, ALU.add)
                    if i < 3:
                        own.did(ins)
                    else:
                        ins.then_inc(sc_free, 1)
                own.settle()
                dve.wait_ge(sc_free, u + 1)
                if part == "b" or part == "c" and br:
                    V.tensor_reduce(s[:, 4:8], e[:, :, 0:n], AX.X, ALU.max, negate=True).then_inc(mx_ready, 1)
                    return
                own.did(V.tensor_reduce(s[:, 0:4], e[:, :, 0:n], AX.X, ALU.max))
                own.settle()
                sk = sinks[:].rearrange("p (f b) -> p f b", f=2)[:, :, 2 * at:2 * at + 2]
                if part == "d":
                    own.did(V.tensor_tensor(cut(s[:, 0:4], 2), cut(s[:, 0:4], 2), sk, ALU.max))
                    own.settle()
                ins = V.tensor_scalar(s[:, 4:8], s[:, 0:4], -1e28, -1.0, ALU.max, ALU.mult)
                if part == "d":
                    own.did(ins)
                    own.settle()
                    ins = V.tensor_tensor(cut(s[:, 12:16], 2), cut(s[:, 4:8], 2), sk, ALU.add)
                ins.then_inc(mx_ready, 1)

            def normalise(u):
                part, step, br, last_br, at, qt, n = UNITS[u]
                e, s = prob(u), stat[:, u % 3]
                m = 1 if part == "a" else 4
                dve.wait_ge(exp_done, u + 1)
                if part == "d":
                    own.did(V.tensor_tensor(s[:, 8:12], s[:, 8:12], s[:, 12:16], ALU.add))
                    own.settle()
                if part == "c" and br == 0:
                    own.did(V.tensor_scalar(s[:, 8:8 + m], s[:, 8:8 + m], 1e-30, None, ALU.max))
                    own.settle()
                own.did(V.reciprocal(s[:, 8:8 + m], s[:, 8:8 + m]))
                own.settle()
                if part == "a":
                    V.tensor_scalar(e[:, 0:AG, 0:n], e[:, 0:AG, 0:n], s[:, 8:9], None, ALU.mult).then_inc(p_ready, 1)
                    return
                if part == "c":
                    gate = gates[:, qt, 8 * br:8 * br + 8].rearrange("p (f b) -> p f b", f=2)[:, :, 2 * at:2 * at + 2]
                    own.did(V.tensor_tensor(cut(s[:, 8:12], 2), cut(s[:, 8:12], 2), gate, ALU.mult))
                    own.settle()
                V.tensor_tensor(e[:, :, 0:n], e[:, :, 0:n], s[:, 8:12].unsqueeze(2).broadcast_to([P, 4, n]), ALU.mult) \
                    .then_inc(p_ready, 1)

            def mixed_out(u):
                part, step, br, last_br, at, qt, n = UNITS[u]
                dve.wait_ge(pv_ready, step + 1)
                if part == "a":
                    hi, lo = att_hi[:, at, P * qt:P * qt + P], att_lo[:, at, P * qt:P * qt + P]
                    own.did(V.tensor_copy(hi, po[:, 0:P]))
                    own.settle()
                    V.tensor_tensor(lo, po[:, 0:P], hi.bitcast(F32), ALU.subtract).then_inc(po_free, 1)
                    return
                y, c = dict(b=(yT0, 4), c=(yT1, 0), d=(yT1, 4))[part]
                gate = dict(b="zb", c="zc", d="zd")[part] + str(at)
                dve.wait_ge(*evacuated(gate))
                y = y[:, c + 2 * at:c + 2 * at + 2, P * qt:P * qt + P]
                V.tensor_tensor(y, cut(po[:, 0:S], P), y, ALU.mult).then_inc(po_free, 1)

            def between(name):
                if name[:2] == "Y:":
                    parts_low(yT1, range(2))
                elif name[:2] == "S:":
                    variance(name[2:])
                    head_norm_end(name[2:], name[2:], kdT, "d_knorm_g")
                elif name[:2] == "rg":
                    i = int(name[2])
                    y = fl(yretT[:, 2 * i:2 * i + 2])
                    dve.wait_ge(*evacuated(f"rt{i // 2}_{i % 2}"))
                    dve.wait_ge(*evacuated(name))
                    V.tensor_tensor(y, y, tmp[:, i % 2], ALU.mult).then_inc(sem("rg_done"), 1)

            two = lambda t, i: fl(t[:, 2 * i:2 * i + 2])
            state = dict(y=0)

            def attention(units, fill):
                score_max(units[0])
                score_max(units[1])
                for i, u in enumerate(units):
                    normalise(u)
                    if i + 2 < len(units):
                        score_max(units[i + 2])
                    for name in fill[i]:
                        between(name)
                    if i and UNITS[u - 1][3]:
                        mixed_out(u - 1)
                    if UNITS[u][0] == "a":
                        operand_low([(yret_lo[:, 2 * j:2 * j + 2], yretT[:, 2 * j:2 * j + 2], yret_piece(j)) for j in YRET_AFTER.get(i, ())])
                mixed_out(units[-1])

            def operand_low(pieces):
                for dst, src, hi in pieces:
                    state["y"] += 1
                    dve.wait_ge(y_hi, state["y"])
                    V.tensor_tensor(dst, src, hi.bitcast(F32), ALU.subtract).then_inc(y_ready, 1)

            def parts_low(src, pieces=range(4)):
                operand_low([(two(parts[:, 1], i), two(src, i), two(parts[:, 0], i)) for i in pieces])

            dve.wait_ge(first_in, 16)

            def diagonals(lo, hi):
                for i in range(lo, hi):
                    k, c = divmod(i, 4)
                    V.tensor_scalar(diags[i], ident, conv_col(c, CONV_DVE + k), None, ALU.mult).then_inc(sem("diags_ready"), 1)

            for i in range(2):
                dve.wait_ge(x_in[i], 16)
            for k in range(2, KD, 2):
                dve.wait_ge(stream_sq, k + 2)
                own.settle()
                ins = V.tensor_tensor(wide[:, 0:2 * S], wide[:, 0:2 * S], wide[:, S * k:S * k + 2 * S], ALU.add)
                if k < KD - 2:
                    own.did(ins)
            ins.then_inc(sem("x_folded"), 1)
            stream_norm("x0", col("norm_g", 0, 8))
            diagonals(0, len(diags))

            def ada_pair(j0):
                for j in (j0, j0 + 1):
                    dve.wait_ge(sem(f"slab_in{SLAB_AT[j]}"), 16 * SLAB_AT[:j + 1].count(SLAB_AT[j]))
                for k in range(KD):
                    for j in (j0, j0 + 1):
                        at = P * (ADA - ADA_DVE + j)
                        if j >= ADA_FIRST:
                            at = P * (j - ADA_FIRST)
                        acc = (ada_acc if j < ADA_FIRST else ada_acc2)[:, at:at + P]
                        w, c = slabs[SLAB_AT[j]][:, k, :], silu_c[:, k:k + 1]
                        if k == 0:
                            own.did(V.tensor_scalar(acc, w, c, None, ALU.mult))
                            continue
                        dve.wait_ge(own.sem, own.n - 1 if k < KD - 1 or j == j0 else own.n)
                        ins = V.scalar_tensor_tensor(acc, w, c, acc, ALU.mult, ALU.add)
                        if k < KD - 1:
                            own.did(ins)
                        else:
                            ins.then_inc(sem("ada_dve"), 1)

            dve.wait_ge(sem("silu_c_ready"), 1)
            own.did(V.memset(hpad[:, :, 0:TAPS - 1], 0.0))
            own.settle()
            for i in range(2):
                dve.wait_ge(*evacuated(f"uv{i}"))
                dve.wait_ge(*evacuated(f"ug{i}"))
                V.tensor_tensor(hpad[:, 2 * i:2 * i + 2, TAPS - 1:], cut(tmp[:, i], S), u_val[:, 2 * i:2 * i + 2], ALU.mult) \
                    .then_inc(sem("hpad_ready"), 1)
            dve.wait_ge(sem("hpad_ready"), 2)

            def taps(lo, hi):
                for tap in range(lo, hi):
                    for c in range(4):
                        y, h = yT0[:, c, :], hpad[:, c, tap:tap + S]
                        if tap == 0:
                            own.did(V.tensor_scalar(y, h, conv_col(c, 0), None, ALU.mult))
                        else:
                            dve.wait_ge(own.sem, own.n - 3)
                            own.did(V.scalar_tensor_tensor(y, h, conv_col(c, tap), y, ALU.mult, ALU.add))

            taps(0, 6)
            for i, (name, dst, gain) in enumerate((("bq0", None, None), ("bq1", None, None),
                                                   ("bk0", bkT[:, 0:2], "b_knorm_g"), ("bk1", bkT[:, 2:4], "b_knorm_g"))):
                variance(name)
                taps(6 + 4 * i, 10 + 4 * i)
                head_norm_end(name, name, None if dst is None else fl(dst), gain)
            own.settle()
            for c in range(4):
                b = ready(f"conv{c // 2}")
                ins = V.scalar_tensor_tensor(yT0[:, c, :], b[:, S * (c % 2):S * (c % 2) + S], col("a_conv_b", c),
                                             yT0[:, c, :], ALU.add, ALU.add)
                if c % 2:
                    ins.then_inc(free_of(f"conv{c // 2}"), 1)
                else:
                    own.did(ins)
            own.settle()
            for c in range(2):
                dve.wait_ge(*evacuated(f"conv{c}"))
            dve.wait_ge(const_in, 16 * 3)
            every = lambda ap: ap.unsqueeze(1).broadcast_to([P, 4, S])
            y_a = yT0[:, 0:4]

            def conv_between(units):
                score_max(units[0])
                score_max(units[1])
                for i, u in enumerate(units):
                    normalise(u)
                    if i + 2 < len(units):
                        score_max(units[i + 2])
                    if i:
                        mixed_out(u - 1)
                    if i == 0:
                        dve.wait_ge(sem("ln_mean"), 1)
                        own.did(V.tensor_scalar(rstd[:, 0:S], st[:, 0:S], 1.0 / GW, None, ALU.mult))
                        own.settle()
                        V.tensor_tensor(y_a, y_a, every(rstd[:, 0:S]), ALU.subtract).then_inc(sem("ln_centred"), 1)
                    elif i == 1:
                        dve.wait_ge(sem("ln_sum"), 1)
                        dve.wait_ge(sem("ln_centred"), 1)
                        V.tensor_scalar(rstd[:, 0:S], st[:, 0:S], 1.0 / GW, EPS, ALU.mult, ALU.add).then_inc(sem("ln_var"), 1)
                    elif i == 2:
                        dve.wait_ge(sem("ln_sqrt"), 1)
                        own.did(V.reciprocal(rstd[:, 0:S], rstd[:, 0:S]))
                        own.settle()
                        V.tensor_tensor(y_a, y_a, every(rstd[:, 0:S]), ALU.mult).then_inc(sem("ln_scaled"), 1)
                    else:
                        for c in range(2):
                            dve.wait_ge(sem("ln_silu"), 2 * c + 2)
                            dve.wait_ge(*evacuated(f"za{c}"))
                            V.tensor_tensor(two(yT0, c), wide[:, 1024 + 512 * c:1536 + 512 * c], tmp[:, c], ALU.mult) \
                                .then_inc(sem("y_a_ready"), 1)
                mixed_out(units[-1])

            assert CONV_DVE == 22
            V.tensor_copy(bn[:, 1, 9:10], yT0[:, 0, 0:1]).then_inc(sem("conv_done"), 1)
            conv_between(PART["b"])
            parts_low(yT0)

            def residual(layer):
                for i in range(4):
                    b = ready(f"wo{layer}_{i}")
                    x = fl(xT[:, 2 * i:2 * i + 2])
                    V.tensor_tensor(x, b[:], x, ALU.add).then_inc(free_of(f"wo{layer}_{i}"), 1)

            residual(0)

            stream_norm("x1", col("norm_g", 8, 8))
            ada_pair(0)
            variance("kskw")
            dve.wait_ge(sem("pairs_in"), 64)
            for v, pos in enumerate(("c_pos_k", "c_pos_v")):
                for g in range(2):
                    src = pairs[:, v, g, :]
                    ov = bass.AP(src.tensor, src.offset, [list(src.ap[0]), [2, 16], [16, NCMP]])
                    V.tensor_tensor(blocks[:, v, :, NCMP * g:NCMP * g + NCMP], ov,
                                    col(pos, 0, 16).unsqueeze(2).broadcast_to([P, 16, NCMP]), ALU.add) \
                        .then_inc(sem("blocks_ready"), 1)
            head_norm_end("kskw", "kskw", None, None)
            ada_pair(2)
            for i, name in enumerate(("qc0", "qc1")):
                variance(name)
                head_norm_end(name, name, None, None)
                ada_pair(4 + 2 * i)
            ada_pair(8)
            ada_pair(10)
            ada_pair(12)
            assert ADA_FIRST == 14
            variance("qd0")
            head_norm_end("qd0", "qd0", None, None)
            variance("cmp")
            head_norm_end("cmp", "kc2", kcn, "c_knorm_cmp_g")
            b = ready("vc2")
            V.tensor_tensor(vcn[0:NCMP, :], b[0:NCMP, 0:P], vb2, ALU.add).then_inc(free_of("vc2"), 1)
            dve.wait_ge(*evacuated("vdgt"))
            attention(PART["c"] + PART["d"], FILL_CD)
            parts_low(yT1, range(2, 4))

            def mod_out(name, lo, hi):
                b = ready(name)
                V.tensor_tensor(mod[:, lo:hi], b[:, lo:hi], col("b_ada_2", lo, hi - lo), ALU.add).then_inc(free_of(name), 1)
                dve.wait_ge(*evacuated(name))

            mod_out("modA", 0, ADA_ONE)
            own.did(V.scalar_tensor_tensor(gain1[:], mod[:, 8:16], 1.0, col("norm1_g_2", 0, 8), ALU.add, ALU.mult))
            own.settle()
            residual(1)

            stream_norm("x2", gain1[:], shift=0)
            mod_out("modB", ADA_ONE, ADA - ADA_DVE + ADA_FIRST)
            dve.wait_ge(rot_in, 32)
            both = lambda ap: ap.unsqueeze(1).broadcast_to([P, 2, S])
            for c, dst in (("rq", rqT), ("rk", rkT)):
                for h in range(RH):
                    b = ready(f"{c}{h}")
                    own.did(V.tensor_tensor(cut(tmp[:, 0], S), cut(b[:], S), both(cos_t[:]), ALU.mult))
                    own.did(V.tensor_tensor(cut(tmp[:, 1], S), cut(b[:], S), both(sin_t[:]), ALU.mult))
                    own.settle()
                    own.did(V.tensor_tensor(dst[:, 2 * h, :], tmp[:, 0, 0:S], tmp[:, 1, S:], ALU.subtract))
                    V.tensor_tensor(dst[:, 2 * h + 1, :], tmp[:, 1, 0:S], tmp[:, 0, S:], ALU.add).then_inc(free_of(f"{c}{h}"), 1)
                    dve.wait_ge(*evacuated(f"{c}{h}"))
            for j in range(ADA_FIRST, ADA_DVE, 2):
                ada_pair(j)
            dve.wait_ge(sem("decay_in"), 16)
            for h in range(RH):
                dve.wait_ge(sem("ret_scores"), h + 1)
                if h >= 2:
                    dve.wait_ge(sem("ret_out"), 2 * h - 2)
                e = prob2[:, h % 2].rearrange("p i j -> p (i j)")[:, 0:LINE]
                V.tensor_tensor(e, sc[h % 2][:, 0:LINE], decay[:, h, :], ALU.mult).then_inc(sem("ret_decayed"), 1)
                for t, src in enumerate((pt, po)):
                    dve.wait_ge(sem("ret_out"), 2 * h + t + 1)
                    own.did(V.bn_stats(bn[:, t, 0:6], src[:]))
                    own.settle()
                    own.did(V.bn_aggr(bn[:, t, 6:8], bn[:, t, 0:6]))
                    own.settle()
                    V.tensor_scalar(bn[:, t, 8:9], bn[:, t, 7:8], GN_EPS, None, ALU.add).then_inc(sem("ret_var"), 1)
                for t, src in enumerate((pt, po)):
                    dve.wait_ge(sem("ret_sqrt"), 2 * h + t + 1)
                    own.did(V.reciprocal(bn[:, t, 8:9], bn[:, t, 8:9]))
                    own.settle()
                    if h and t == 0:
                        dve.wait_ge(proj_ready, GROUP_AT[f"rt{h - 1}_1"] + 1)
                    V.tensor_scalar(ron[:, t, :], src[:], bn[:, t, 6:7], bn[:, t, 8:9], ALU.subtract, ALU.mult) \
                        .then_inc(sem("ret_normed"), 1)
                dve.wait_ge(sem("ret_normed"), 2 * h + 2)
                if h == 0:
                    mod_out("modC", ADA - ADA_DVE + ADA_FIRST, ADA)
                    own.did(V.scalar_tensor_tensor(gain2[:], mod[:, 32:40], 1.0, col("norm2_g_2", 0, 8), ALU.add, ALU.mult))
                    own.settle()
                    for g in range(AG):
                        b = ready(f"dl{g}")
                        V.tensor_tensor(line[:, g, :], b[0:AH, 0:LINE], linemask[:, g, :], ALU.add).then_inc(free_of(f"dl{g}"), 1)
                    for g in range(AG):
                        dve.wait_ge(*evacuated(f"dl{g}"))
                    V.tensor_copy(bn[0:AH, 1, 9:10], line[:, 0, 0:1]).then_inc(sem("line_ready"), 1)
            dve.wait_ge(sem("dil_in"), 16)
            attention(PART["a"], FILL_A)
            for name in BRANCHES:
                i = int(name[2])
                if name == BRANCHES[-1]:
                    parts_low(mT, range(3))
                b = ready(name)
                gate, dst = (gaT, mT) if name[1] == "r" else (gbT, gbT)
                dve.wait_ge(*evacuated(f"g{'a' if name[1] == 'r' else 'b'}{i}"))
                V.tensor_tensor(two(dst, i), b[:], two(gate, i), ALU.mult).then_inc(free_of(name), 1)
                if name != "wr0" and (name[1] == "r" or i == 0):
                    dve.wait_ge(*evacuated(f"wa{i}"))
                    dve.wait_ge(*evacuated(f"wr{i}"))
                    V.tensor_tensor(two(mT, i), two(mT, i), two(gbT, i), ALU.add).then_inc(sem("merged"), 1)
            parts_low(mT, range(3, 4))

            def gated_residual(names, per, gate):
                for i, name in enumerate(names):
                    b = ready(name)
                    for j in range(per):
                        k = per * i + j
                        ins = V.scalar_tensor_tensor(xT[:, k, :], b[:, S * j:S * j + S], mod[:, gate + k:gate + k + 1], xT[:, k, :],
                                                     ALU.mult, ALU.add)
                    ins.then_inc(free_of(name), 1)

            gated_residual([f"wo2_{i}" for i in range(4)], 2, 16)
            stream_norm("x3", gain2[:], shift=24)
            for i in range(16):
                r = tmp[:, i % 2]
                dve.wait_ge(sem("hid_high"), i + 1)
                own.did(V.tensor_tensor(r, r, r, ALU.mult))
                own.settle()
                V.tensor_tensor(two(hid_lo, i), r, two(hid_hi, i).bitcast(F32), ALU.subtract).then_inc(sem("hid_ready"), 1)
            gated_residual([f"f2_{i}" for i in range(8)], 1, 40)
            stream_norm("xf", col("norm_f_g_2", 0, 8), split=False)


def shape_constants():
    f = np.float32
    p = np.arange(P)
    slopes = np.power(2.0, -8.0 * np.arange(1, NH + 1) / NH).astype(f)
    dist = (P + p[:, None] - np.arange(S)[None, :]).astype(f)
    lin = -slopes[None, :, None] * dist[:, None, :]
    alibi = np.where(dist[:, None, :] >= 0, lin, -1e30).astype(f)
    swa = np.where((dist[:, None, :] >= 0) & (dist[:, None, :] < 128), lin, -1e30).astype(f)
    t = (np.arange(2)[None, :] * P + p[:, None])[:, :, None, None]
    dc = (t - (16 * np.arange(NCMP) + 31)).astype(f)
    cmp_bias = np.where(dc >= 0, -slopes[None, None, :, None] * dc, -1e30).astype(f)
    log_g = np.log1p(-(f(2.0) ** (-5.0 - np.arange(RH, dtype=f)))).astype(f)
    i = np.arange(LINE)
    j = np.where(i < S, 0, P)[None, :] + p[:, None]
    rel = (np.where(i < S, i, i - P)[None, :] - j).astype(f)
    decay = np.where(rel[:, None, :] >= 0, np.exp(log_g[None, :, None] * np.maximum(rel, 0)[:, None, :]), 0) / 16
    inv = f(10000.0) ** (-np.arange(P, dtype=f) / f(P))
    ang = np.arange(S, dtype=f)[None, :] * inv.astype(f)[:, None]
    d = 255 - np.arange(LINE)
    onehot = np.zeros((32, AG, LINE), f)
    mask = np.full((AH, AG, LINE), -1e30, f)
    for g, (win, dil) in enumerate(((128, 1), (512, 4), (2048, 16))):
        ok = (d >= 0) & (d <= win) & (d % dil == 0)
        dd = np.maximum(d, 1).astype(f)
        large = 16 + (np.log(dd / f(16)) / f(np.log(2048 / 16)) * f(16)).astype(np.int32)
        bucket = np.where(d < 16, d, np.minimum(large, 31))
        for u in np.nonzero(ok)[0]:
            onehot[bucket[u], g, u] = 1
            mask[:, g, u] = 0
    return dict(alibi=alibi, swa=swa, cmp_bias=cmp_bias,
                decay=decay.astype(f), cos=np.cos(ang).astype(f), sin=np.sin(ang).astype(f), onehot=onehot, linemask=mask)


def lay_out(inputs):
    v = {n: np.asarray(inputs[n]) for n in inputs}
    tiles = lambda w: w.reshape(-1, P, w.shape[-1]).transpose(1, 0, 2).reshape(P, -1)

    def unit(u):
        kt, w = unit_shape(u)
        i = 0 if u in OD_ONE else int(u.rstrip("ab")[-1])
        if u in OD_ONE:
            return tiles(np.concatenate([v["o_w_in"][0][:, c:c + n] for c, n in OD_ONE[u]], axis=1))
        if u in PAIRED:
            heads = [2 * i + j // 2 + 4 * (j % 2) for j in range(4)]
            return tiles(np.concatenate([v["o_w_in"][0][:, OD[u[:2]] + HD * h:OD[u[:2]] + HD * h + HD] for h in heads], axis=1))
        if u[:2] in ("ck", "cv"):
            return tiles(v[f"c_{u[1]}_w1"][0][D * i:D * i + D])
        if u[:2] == "wr":
            c = 256 * i + P * (u[-1] == "b")
            return tiles(v["w_ret_out_2"][0][:, c:c + P])
        if u[:2] == "f2":
            k = 2048 * (u[-1] == "b")
            return tiles(v["w_ff2_2"][0][k:k + 2048, P * i:P * i + P])
        if u[:2] == "wa":
            return tiles(v["w_att_out_2"][0][:, 512 * i:512 * i + 512])
        if u[:3] == "wo1":
            c = 256 * int(u[-1])
            return tiles(v["w_out"][1][:, c:c + 256].reshape(2, 2, 4, HD, 256).transpose(0, 2, 1, 3, 4).reshape(D, 256))
        if u[:2] == "wo":
            src, c = (v["w_out"][0] if u[2] == "0" else v["w_o_2"][0]), 0
        elif u[:2] == "f1":
            src, c, i = v["w_ff1_2"][0], 0, int(u[3:])
        elif u[:2] in EV:
            src, c = v["e_w_in"][0], EV[u[:2]]
        elif u[:2] in IN2:
            src, c = v["w_in_2"][0], IN2[u[:2]]
        else:
            src, c = v["w_in_2"][0], IN2_ATT + 1536 * int(u[2]) + 512 * "qkv".index(u[1])
        return tiles(src[:, c + 256 * i:c + 256 * i + 256])

    weights = np.zeros((len(WEIGHTS), P, UNIT), np.float32)
    for n, u in enumerate(WEIGHTS):
        part = unit(u)
        weights[n, :, 0:part.shape[1]] = part
    columns = [v[n].reshape(c, P).T for n, c in FULL] + [np.tile(v[n].reshape(HD), 2)[:, None] for n in HALF]
    columns.append(v["a_conv_w"][0].T.reshape(4, P, TAPS).transpose(1, 0, 2).reshape(P, 4 * TAPS))
    columns += [np.ones((P, P), np.float32), np.eye(P, dtype=np.float32), np.broadcast_to(v["d_sinks"], (P, NH))]
    p = np.arange(P)
    rel = np.zeros((P, AG * AH), np.float32)
    rel[0:32] = v["rel_bias_2"]
    kw2 = np.tile(v["c_k_w2"][0].reshape(2, P, 1, HD), (1, 1, 2, 1)).transpose(1, 0, 2, 3).reshape(P, 4 * HD)
    small = [(p[:, None] // HD == p[None, :] // HD).astype(np.float32), kw2, tiles(v["c_v_w2"][0]),
             np.broadcast_to(np.tile(v["c_v_b2"].reshape(HD), 2), (P, 2 * HD)), rel]
    out = dict(small=np.concatenate(small, axis=1), x=tiles(v["x"][0].T), weights=weights, vectors=np.concatenate(columns, axis=1),
               w_ada=v["w_ada_2"][0].reshape(KD, P, ADA, P).transpose(2, 1, 0, 3).reshape(ADA, P, KD * P))
    return out


def kernel(**inputs):
    import concourse.bacc as bacc
    from concourse.bass_utils import run_bass_kernel_spmd as run

    nc = bacc.Bacc("TRN2", target_bir_lowering=False, num_devices=1)
    arrays = lay_out(inputs)
    arrays.update(shape_constants())
    arrays = {f"in_{n}": np.ascontiguousarray(v) for n, v in arrays.items()}
    aps = {n[3:]: nc.dram_tensor(n, v.shape, mybir.dt.from_np(v.dtype), kind="ExternalInput").ap() for n, v in arrays.items()}
    out = nc.dram_tensor("y", (P, KD * S), F32, kind="ExternalOutput").ap()
    mixer_kernel(nc, aps, out)
    y = run(nc, [arrays], core_ids=[0]).results[0]["y"]
    return y.reshape(P, KD, S).transpose(2, 1, 0).reshape(1, S, D)
```
